# Optimizing a Trainium2 kernel written in Bass

```python
import jax, jax.numpy as jnp
from jax import lax
import numpy as np
import math

D_MODEL = 1024
BATCH = 1
SEQ = 256
DEPTH = 1

N_MEM = 256
EPS = 1e-6

HEAD_DIM = 64
DIL_PATTERNS = ((128, 1), (512, 4), (2048, 16))
N_GROUPS = len(DIL_PATTERNS)
ATTN_SLOTS = 4
ATTN_HEADS = N_GROUPS * ATTN_SLOTS
ATTN_WIDTH = ATTN_HEADS * HEAD_DIM
ATTN_OUT = ATTN_SLOTS * HEAD_DIM
ROT_DIM = HEAD_DIM // 4
ROPE_THETA = 500000.0

CONV_WIDTH = 768
CONV_K = 3

MEM_HEADS = 4
MEM_HEAD_DIM = 128
MEM_WIDTH = MEM_HEADS * MEM_HEAD_DIM

N_BRANCH = 3
IN_SIZES = (ATTN_WIDTH, ATTN_WIDTH, ATTN_WIDTH, CONV_WIDTH, CONV_WIDTH, CONV_WIDTH,
            MEM_WIDTH, N_BRANCH * D_MODEL)
IN_COLS = sum(IN_SIZES)
IN_SPLITS = tuple(int(c) for c in np.cumsum(IN_SIZES)[:-1])

N_EXPERT_GROUPS = 4
EXPERTS_PER_GROUP = 8
N_EXPERTS = N_EXPERT_GROUPS * EXPERTS_PER_GROUP
TOP_K = 2
EXPERT_FF = 512
MOE_BLOCK = 256


def _rmsnorm(x, g):
    xf = x.astype(jnp.float32)
    y = xf * lax.rsqrt(jnp.mean(xf * xf, axis=-1, keepdims=True) + EPS)
    return (y * g.astype(jnp.float32)).astype(x.dtype)

def _rope_tables(positions):
    inv = ROPE_THETA ** (-jnp.arange(0, ROT_DIM, 2, dtype=jnp.float32) / ROT_DIM)
    ang = positions.astype(jnp.float32)[..., None] * inv
    return jnp.cos(ang)[:, :, None, :], jnp.sin(ang)[:, :, None, :]

def _partial_rope(t, cos, sin):
    tr = t[..., :ROT_DIM].astype(jnp.float32)
    t1, t2 = tr[..., :ROT_DIM // 2], tr[..., ROT_DIM // 2:]
    rot = jnp.concatenate([t1 * cos - t2 * sin, t2 * cos + t1 * sin], axis=-1)
    return jnp.concatenate([rot.astype(t.dtype), t[..., ROT_DIM:]], axis=-1)

def _banded_attention(q, k, v, half):
    b, g, L, h, dh = q.shape
    blk = half
    nb = -(-L // blk)
    lp = nb * blk
    qb = jnp.pad(q, ((0, 0), (0, 0), (0, lp - L), (0, 0), (0, 0))).reshape(b, g, nb, blk, h, dh)
    pad_k = ((0, 0), (0, 0), (blk, lp - L + blk), (0, 0), (0, 0))

    def windows(t):
        tb = jnp.pad(t, pad_k).reshape(b, g, nb + 2, blk, h, dh)
        return jnp.concatenate([tb[:, :, :-2], tb[:, :, 1:-1], tb[:, :, 2:]], axis=3)

    kw, vw = windows(k), windows(v)
    qpos = np.arange(nb)[:, None] * blk + np.arange(blk)[None, :]
    kpos = np.arange(nb)[:, None] * blk - blk + np.arange(3 * blk)[None, :]
    valid = ((np.abs(qpos[:, :, None] - kpos[:, None, :]) <= half)
             & (kpos[:, None, :] >= 0) & (kpos[:, None, :] < L))
    s = jnp.einsum('bgnqhd,bgnkhd->bgnhqk', qb, kw).astype(jnp.float32) * (dh ** -0.5)
    s = jnp.where(jnp.asarray(valid)[:, None], s, jnp.finfo(jnp.float32).min)
    m = jnp.max(s, axis=-1, keepdims=True)
    p = jnp.exp(s - m)
    den = jnp.sum(p, axis=-1)
    o = jnp.einsum('bgnhqk,bgnkhd->bgnqhd', p.astype(v.dtype), vw)
    o = o / jnp.transpose(den, (0, 1, 2, 4, 3))[..., None].astype(o.dtype)
    lse = jnp.transpose(m[..., 0] + jnp.log(den), (0, 1, 2, 4, 3))
    o = o.reshape(b, g, lp, h, dh)[:, :, :L]
    lse = lse.reshape(b, g, lp, h)[:, :, :L]
    return o, lse

def _dilated_attention(q, k, v, window, dilation):
    b, s, h, dh = q.shape
    L = s // dilation
    half = window // (2 * dilation)

    def to_sub(t):
        return jnp.transpose(t.reshape(b, L, dilation, h, dh), (0, 2, 1, 3, 4))

    o, lse = _banded_attention(to_sub(q), to_sub(k), to_sub(v), half)
    o = jnp.transpose(o, (0, 2, 1, 3, 4)).reshape(b, s, h, dh)
    lse = jnp.transpose(lse, (0, 2, 1, 3)).reshape(b, s, h)
    return o, lse

def _hierarchical_moe(h, w_rg, b_rg, w_re, b_re, w_gate, w_up, w_down):
    b, s, d = h.shape
    n = b * s
    hf = h.reshape(n, d)
    hr = hf.astype(jnp.float32)
    pg = jax.nn.softmax(hr @ w_rg.astype(jnp.float32) + b_rg.astype(jnp.float32), axis=-1)
    pg_top, g_idx = lax.top_k(pg, 1)
    el = (hr @ w_re.astype(jnp.float32) + b_re.astype(jnp.float32)).reshape(n, N_EXPERT_GROUPS, EXPERTS_PER_GROUP)
    sel = jnp.einsum('ng,nge->ne', jax.nn.one_hot(g_idx[:, 0], N_EXPERT_GROUPS, dtype=jnp.float32), el)
    pe_top, e_idx = lax.top_k(jax.nn.softmax(sel, axis=-1), TOP_K)
    weights = pg_top * pe_top / jnp.sum(pe_top, axis=-1, keepdims=True)
    ids = g_idx * EXPERTS_PER_GROUP + e_idx

    nk = n * TOP_K
    e = ids.reshape(nk).astype(jnp.int32)
    w = weights.reshape(nk)
    t = jnp.repeat(jnp.arange(n, dtype=jnp.int32), TOP_K)
    order = jnp.argsort(e, stable=True)
    e_s, t_s, w_s = e[order], t[order], w[order]
    counts = jnp.bincount(e, length=N_EXPERTS)
    padded = ((counts + MOE_BLOCK - 1) // MOE_BLOCK) * MOE_BLOCK
    start = jnp.cumsum(counts) - counts
    pend = jnp.cumsum(padded)
    pstart = pend - padded
    dest = pstart[e_s] + (jnp.arange(nk, dtype=jnp.int32) - start[e_s])
    n_rows = (-(-nk // MOE_BLOCK) + N_EXPERTS) * MOE_BLOCK
    n_blk = n_rows // MOE_BLOCK
    row_tok = jnp.zeros((n_rows,), jnp.int32).at[dest].set(t_s)
    row_w = jnp.zeros((n_rows,), jnp.float32).at[dest].set(w_s)
    blk_exp = jnp.minimum(jnp.searchsorted(pend, jnp.arange(n_blk) * MOE_BLOCK, side='right'),
                          N_EXPERTS - 1).astype(jnp.int32)

    def expert_block(args):
        tok, wt, ex = args
        xb = hf[tok]
        a = xb @ w_gate[ex]
        u = xb @ w_up[ex]
        y = (jax.nn.silu(a) * u) @ w_down[ex]
        return y * wt[:, None].astype(y.dtype)

    ys = lax.map(expert_block, (row_tok.reshape(n_blk, MOE_BLOCK),
                                row_w.reshape(n_blk, MOE_BLOCK), blk_exp))
    out = jnp.zeros((n, d), h.dtype).at[row_tok].add(ys.reshape(n_rows, d).astype(h.dtype))
    return out.reshape(b, s, d)

def first_inputs(seed: int = 0) -> dict:
    key = jax.random.key(seed)
    ks = jax.random.split(key, 24)
    f32 = jnp.float32

    def nrm(k, shape, scale):
        return jax.random.normal(k, shape, f32) * scale

    def gain(k, dim):
        return 1.0 + 0.05 * jax.random.normal(k, (DEPTH, dim), f32)

    x = jax.random.normal(ks[0], (BATCH, SEQ, D_MODEL), f32)
    mem = jax.random.normal(ks[1], (BATCH, N_MEM, D_MODEL), f32)
    positions = (jnp.arange(SEQ, dtype=jnp.int32)[None, :]
                 + jax.random.randint(ks[2], (BATCH, 1), 0, 4096, dtype=jnp.int32))
    return {
        'x': x,
        'mem': mem,
        'positions': positions,
        'g_mix': gain(ks[3], D_MODEL),
        'g_mem': gain(ks[4], D_MODEL),
        'w_in': nrm(ks[5], (DEPTH, D_MODEL, IN_COLS), D_MODEL ** -0.5),
        'g_qn_attn': gain(ks[6], HEAD_DIM),
        'g_kn_attn': gain(ks[7], HEAD_DIM),
        'w_conv': nrm(ks[8], (DEPTH, CONV_K, CONV_WIDTH), CONV_K ** -0.5),
        'w_mem_kv': nrm(ks[9], (DEPTH, D_MODEL, 2 * MEM_WIDTH), D_MODEL ** -0.5),
        'g_qn_mem': gain(ks[10], MEM_HEAD_DIM),
        'g_kn_mem': gain(ks[11], MEM_HEAD_DIM),
        'w_proj_attn': nrm(ks[12], (DEPTH, ATTN_OUT, D_MODEL), ATTN_OUT ** -0.5),
        'w_proj_conv': nrm(ks[13], (DEPTH, CONV_WIDTH, D_MODEL), CONV_WIDTH ** -0.5),
        'w_proj_mem': nrm(ks[14], (DEPTH, MEM_WIDTH, D_MODEL), MEM_WIDTH ** -0.5),
        'w_out': nrm(ks[15], (DEPTH, D_MODEL, D_MODEL), D_MODEL ** -0.5),
        'g_ffn': gain(ks[16], D_MODEL),
        'w_router_group': nrm(ks[17], (DEPTH, D_MODEL, N_EXPERT_GROUPS), D_MODEL ** -0.5),
        'b_router_group': nrm(ks[18], (DEPTH, N_EXPERT_GROUPS), 0.01),
        'w_router_expert': nrm(ks[19], (DEPTH, D_MODEL, N_EXPERTS), D_MODEL ** -0.5),
        'b_router_expert': nrm(ks[20], (DEPTH, N_EXPERTS), 0.01),
        'w_gate': nrm(ks[21], (DEPTH, N_EXPERTS, D_MODEL, EXPERT_FF), D_MODEL ** -0.5),
        'w_up': nrm(ks[22], (DEPTH, N_EXPERTS, D_MODEL, EXPERT_FF), D_MODEL ** -0.5),
        'w_down': nrm(ks[23], (DEPTH, N_EXPERTS, EXPERT_FF, D_MODEL), EXPERT_FF ** -0.5),
    }

def first_block(x, mem, positions, g_mix, g_mem, w_in, g_qn_attn, g_kn_attn, w_conv,
              w_mem_kv, g_qn_mem, g_kn_mem, w_proj_attn, w_proj_conv, w_proj_mem, w_out,
              g_ffn, w_router_group, b_router_group, w_router_expert, b_router_expert,
              w_gate, w_up, w_down):
    b, s, d = x.shape
    cos, sin = _rope_tables(positions)
    cos, sin = cos.astype(x.dtype), sin.astype(x.dtype)
    for l in range(DEPTH):
        h = _rmsnorm(x, g_mix[l])
        proj = h @ w_in[l]
        q_a, k_a, v_a, cx, cb, cc, q_m, gate_logits = jnp.split(proj, IN_SPLITS, axis=-1)

        q_a = _partial_rope(_rmsnorm(q_a.reshape(b, s, ATTN_HEADS, HEAD_DIM), g_qn_attn[l]), cos, sin)
        k_a = _partial_rope(_rmsnorm(k_a.reshape(b, s, ATTN_HEADS, HEAD_DIM), g_kn_attn[l]), cos, sin)
        v_a = v_a.reshape(b, s, ATTN_HEADS, HEAD_DIM)
        q_a = q_a.reshape(b, s, N_GROUPS, ATTN_SLOTS, HEAD_DIM)
        k_a = k_a.reshape(b, s, N_GROUPS, ATTN_SLOTS, HEAD_DIM)
        v_a = v_a.reshape(b, s, N_GROUPS, ATTN_SLOTS, HEAD_DIM)
        outs, lses = [], []
        for gi, (window, dilation) in enumerate(DIL_PATTERNS):
            o_g, lse_g = _dilated_attention(q_a[:, :, gi], k_a[:, :, gi], v_a[:, :, gi], window, dilation)
            outs.append(o_g)
            lses.append(lse_g)
        alpha = jax.nn.softmax(jnp.stack(lses, axis=2), axis=2)
        o_attn = jnp.einsum('bsgh,bsghd->bshd', alpha.astype(x.dtype),
                            jnp.stack(outs, axis=2)).reshape(b, s, ATTN_OUT)

        u = cc * cx
        up = jnp.pad(u, ((0, 0), (1, 1), (0, 0)))
        wc = w_conv[l]
        y_conv = wc[0] * up[:, :-2] + wc[1] * up[:, 1:-1] + wc[2] * up[:, 2:]
        z_conv = cb * y_conv

        mkv = _rmsnorm(mem, g_mem[l]) @ w_mem_kv[l]
        k_m, v_m = jnp.split(mkv, 2, axis=-1)
        k_m = _rmsnorm(k_m.reshape(b, N_MEM, MEM_HEADS, MEM_HEAD_DIM), g_kn_mem[l])
        v_m = v_m.reshape(b, N_MEM, MEM_HEADS, MEM_HEAD_DIM)
        q_m = _rmsnorm(q_m.reshape(b, s, MEM_HEADS, MEM_HEAD_DIM), g_qn_mem[l])
        sm = jnp.einsum('bshd,bmhd->bhsm', q_m, k_m).astype(jnp.float32) * (MEM_HEAD_DIM ** -0.5)
        pm = jax.nn.softmax(sm, axis=-1).astype(v_m.dtype)
        o_mem = jnp.einsum('bhsm,bmhd->bshd', pm, v_m).reshape(b, s, MEM_WIDTH)

        gates = jax.nn.sigmoid(gate_logits).reshape(b, s, N_BRANCH, d)
        merged = (gates[:, :, 0] * (o_attn @ w_proj_attn[l])
                  + gates[:, :, 1] * (z_conv @ w_proj_conv[l])
                  + gates[:, :, 2] * (o_mem @ w_proj_mem[l]))
        x = x + merged @ w_out[l]

        h2 = _rmsnorm(x, g_ffn[l])
        x = x + _hierarchical_moe(h2, w_router_group[l], b_router_group[l], w_router_expert[l],
                                  b_router_expert[l], w_gate[l], w_up[l], w_down[l])
    return x


GRID_W = 64
CTX_LEN = 256
D_MIX = 2 * D_MODEL
SSD_WIDTH = D_MIX // 2
SSD_HEAD_DIM = 64
SSD_HEADS = SSD_WIDTH // SSD_HEAD_DIM
SSD_GROUPS = 2
SSD_HPG = SSD_HEADS // SSD_GROUPS
SSD_STATE = 128
SSD_CONV_CH = SSD_WIDTH + 2 * SSD_GROUPS * SSD_STATE
GDN_WIDTH = D_MIX - SSD_WIDTH
GDN_HEAD_DIM = 128
GDN_HEADS = GDN_WIDTH // GDN_HEAD_DIM
GDN_CONV_CH = 3 * GDN_WIDTH
N_DIR = 2
CONV_K_2 = 5
CHUNK = 64
D_IN_PROJ = SSD_WIDTH + SSD_CONV_CH + N_DIR * SSD_HEADS + GDN_CONV_CH + GDN_WIDTH + 2 * N_DIR * GDN_HEADS
D_FF = ((8 * D_MODEL // 3 + 255) // 256) * 256
DEEPNORM_ALPHA = (2.0 * DEPTH) ** 0.25
DEEPNORM_BETA = (8.0 * DEPTH) ** -0.25
DT_MIN = 1e-3
DT_MAX = 1e-1
LN_EPS = 1e-5
RMS_EPS = 1e-6


f32 = jnp.float32

def layer_norm(x, g, b):
    xf = x.astype(f32)
    mu = jnp.mean(xf, -1, keepdims=True)
    var = jnp.mean(jnp.square(xf - mu), -1, keepdims=True)
    return ((xf - mu) * lax.rsqrt(var + LN_EPS) * g + b).astype(x.dtype)

def rms_norm(x):
    return x * lax.rsqrt(jnp.mean(x * x, -1, keepdims=True) + RMS_EPS)

def l2_norm(x):
    return x * lax.rsqrt(jnp.sum(x * x, -1, keepdims=True) + RMS_EPS)

def masked_exp(diff, mask):
    return jnp.exp(jnp.where(mask, diff, -jnp.inf))

def dwconv(u, w):
    return lax.conv_general_dilated(
        u, w[:, None, :].astype(u.dtype), (1,), [(CONV_K_2 // 2, CONV_K_2 // 2)],
        dimension_numbers=("NWC", "WIO", "NWC"), feature_group_count=u.shape[-1])

def conv_grid(u, w, rows):
    b, t, ch = u.shape
    return dwconv(u.reshape(b * rows, GRID_W, ch), w).reshape(b, t, ch)

def ssd_chunk_scan(xdt, la, bm, cm, s0):
    b, t = la.shape[:2]
    nc = t // CHUNK
    xdt, la, bm, cm = (a.reshape(b, nc, CHUNK, *a.shape[2:]) for a in (xdt, la, bm, cm))
    acs = jnp.cumsum(la, axis=2)
    tril = jnp.tril(jnp.ones((CHUNK, CHUNK), bool))[:, :, None, None]
    decay = masked_exp(acs[:, :, :, None] - acs[:, :, None, :], tril)
    att = jnp.einsum("bclgn,bcsgn->bclsg", cm, bm)[..., None] * decay
    y = jnp.einsum("bclsgj,bcsgjp->bclgjp", att, xdt)
    states = jnp.einsum("bclgn,bclgjp->bcgjpn", bm,
                        xdt * jnp.exp(acs[:, :, -1:] - acs)[..., None])

    def step(s, inp):
        dec, st = inp
        return s * dec[..., None, None] + st, s

    s_fin, s_in = lax.scan(step, s0, (jnp.exp(acs[:, :, -1]).swapaxes(0, 1), states.swapaxes(0, 1)))
    y = y + jnp.einsum("bclgn,cbgjpn->bclgjp", cm, s_in) * jnp.exp(acs)[..., None]
    return y.reshape(b, t, *y.shape[3:]), s_fin

def gdn_chunk_scan(q, k, v, log_a, beta, s0):
    b, t, h, dv = v.shape
    nc = t // CHUNK
    q, k, v, log_a, beta = (a.reshape(b, nc, CHUNK, *a.shape[2:]) for a in (q, k, v, log_a, beta))
    g = jnp.cumsum(log_a, axis=2)
    diff = g[:, :, :, None] - g[:, :, None, :]
    idx = jnp.arange(CHUNK)
    strict = (idx[:, None] > idx[None, :])[:, :, None]
    incl = (idx[:, None] >= idx[None, :])[:, :, None]
    a_mat = jnp.einsum("bclhd,bcshd->bclsh", k, k) * beta[:, :, :, None] * masked_exp(diff, strict)
    lhs = jnp.moveaxis(a_mat, -1, 2) + jnp.eye(CHUNK, dtype=a_mat.dtype)
    rhs = jnp.concatenate([v * beta[..., None], k * (beta * jnp.exp(g))[..., None]], -1)
    sol = lax.linalg.triangular_solve(lhs, jnp.moveaxis(rhs, 3, 2), left_side=True,
                                      lower=True, unit_diagonal=True)
    u, w = sol[..., :dv], sol[..., dv:]
    qk = jnp.einsum("bclhd,bcshd->bchls", q, k) * jnp.moveaxis(masked_exp(diff, incl), -1, 2)
    qg = jnp.moveaxis(q * jnp.exp(g)[..., None], 3, 2)
    kd = jnp.moveaxis(k * jnp.exp(g[:, :, -1:] - g)[..., None], 3, 2)
    dec = jnp.exp(g[:, :, -1])

    def step(s, inp):
        u_c, w_c, qk_c, qg_c, kd_c, dec_c = inp
        v_new = u_c - jnp.einsum("bhlk,bhkv->bhlv", w_c, s)
        o = jnp.einsum("bhlk,bhkv->bhlv", qg_c, s) + jnp.einsum("bhls,bhsv->bhlv", qk_c, v_new)
        s = s * dec_c[..., None, None] + jnp.einsum("bhlk,bhlv->bhkv", kd_c, v_new)
        return s, o

    s_fin, o = lax.scan(step, s0, tuple(jnp.moveaxis(a, 1, 0) for a in (u, w, qk, qg, kd, dec)))
    return jnp.transpose(o, (1, 0, 3, 2, 4)).reshape(b, t, h, dv), s_fin

def prefix_scan(scan_fn, ctx_in, lat_in, s0, reverse):
    flip = (lambda a: jnp.flip(a, axis=1)) if reverse else (lambda a: a)
    y_c, s_c = scan_fn(*map(flip, ctx_in), s0)
    y_l, _ = scan_fn(*map(flip, lat_in), s_c)
    return flip(y_c), flip(y_l)

def token_mixers(h_ctx, h_lat, rows, w_in, conv_w_ssd, conv_b_ssd, dt_bias_ssd, a_log_ssd,
                 d_skip_ssd, norm_w_ssd, conv_w_gdn, dt_bias_gdn, a_log_gdn, norm_w_gdn):
    splits = [int(s) for s in np.cumsum([SSD_WIDTH, SSD_CONV_CH, N_DIR * SSD_HEADS,
                                          GDN_CONV_CH, GDN_WIDTH, N_DIR * GDN_HEADS])]

    def project(h, conv):
        bsz, t = h.shape[:2]
        z, xbc, dt_raw, qkv, gate, b_raw, a_raw = jnp.split(h @ w_in, splits, axis=-1)
        xbc = jax.nn.silu(conv(xbc, conv_w_ssd) + conv_b_ssd).astype(f32)
        qkv = jax.nn.silu(conv(qkv, conv_w_gdn)).astype(f32)
        xs, bm, cm = jnp.split(xbc, [SSD_WIDTH, SSD_WIDTH + SSD_GROUPS * SSD_STATE], -1)
        dt = jax.nn.softplus(dt_raw.astype(f32).reshape(bsz, t, N_DIR, SSD_HEADS) + dt_bias_ssd)
        q, k, v = (a.reshape(bsz, t, GDN_HEADS, GDN_HEAD_DIM) for a in jnp.split(qkv, 3, -1))
        return {
            "z": z.astype(f32).reshape(bsz, t, SSD_GROUPS, SSD_WIDTH // SSD_GROUPS),
            "xs": xs.reshape(bsz, t, SSD_GROUPS, SSD_HPG, SSD_HEAD_DIM),
            "bm": bm.reshape(bsz, t, SSD_GROUPS, SSD_STATE),
            "cm": cm.reshape(bsz, t, SSD_GROUPS, SSD_STATE),
            "dt": dt.reshape(bsz, t, N_DIR, SSD_GROUPS, SSD_HPG),
            "q": l2_norm(q) * GDN_HEAD_DIM ** -0.5,
            "k": l2_norm(k),
            "v": v,
            "gate": gate.astype(f32).reshape(bsz, t, GDN_HEADS, GDN_HEAD_DIM),
            "beta": jax.nn.sigmoid(b_raw.astype(f32).reshape(bsz, t, N_DIR, GDN_HEADS)),
            "log_a": -jnp.exp(a_log_gdn.astype(f32)) * jax.nn.softplus(
                a_raw.astype(f32).reshape(bsz, t, N_DIR, GDN_HEADS) + dt_bias_gdn),
        }

    pc = project(h_ctx, dwconv)
    pl = project(h_lat, lambda u, w: conv_grid(u, w, rows))
    a_ssd = -jnp.exp(a_log_ssd.astype(f32)).reshape(N_DIR, SSD_GROUPS, SSD_HPG)

    def ssd_in(p, d):
        dt_d = p["dt"][:, :, d]
        return (p["xs"] * dt_d[..., None], dt_d * a_ssd[d], p["bm"], p["cm"])

    def gdn_in(p, d):
        return (p["q"], p["k"], p["v"], p["log_a"][:, :, d], p["beta"][:, :, d])

    bsz = h_lat.shape[0]
    s0_ssd = jnp.zeros((bsz, SSD_GROUPS, SSD_HPG, SSD_HEAD_DIM, SSD_STATE), f32)
    s0_gdn = jnp.zeros((bsz, GDN_HEADS, GDN_HEAD_DIM, GDN_HEAD_DIM), f32)
    d_skip = d_skip_ssd.astype(f32).reshape(SSD_GROUPS, SSD_HPG, 1)
    y_ssd_c, y_ssd_l = d_skip * pc["xs"], d_skip * pl["xs"]
    o_gdn_c, o_gdn_l = 0.0, 0.0
    for d, rev in enumerate((False, True)):
        yc, yl = prefix_scan(ssd_chunk_scan, ssd_in(pc, d), ssd_in(pl, d), s0_ssd, rev)
        y_ssd_c, y_ssd_l = y_ssd_c + yc, y_ssd_l + yl
        oc, ol = prefix_scan(gdn_chunk_scan, gdn_in(pc, d), gdn_in(pl, d), s0_gdn, rev)
        o_gdn_c, o_gdn_l = o_gdn_c + oc, o_gdn_l + ol

    def finish(p, y_ssd, o_gdn, dtype):
        bsz, t = y_ssd.shape[:2]
        y = rms_norm(y_ssd.reshape(p["z"].shape) * jax.nn.silu(p["z"])).reshape(bsz, t, SSD_WIDTH) * norm_w_ssd
        o = (rms_norm(o_gdn) * norm_w_gdn * jax.nn.silu(p["gate"])).reshape(bsz, t, GDN_WIDTH)
        return jnp.concatenate([y, o], -1).astype(dtype)

    return (finish(pc, y_ssd_c, o_gdn_c, h_ctx.dtype), finish(pl, y_ssd_l, o_gdn_l, h_lat.dtype))

def swiglu(h, w_gate, w_up, w_down):
    return (jax.nn.silu(h @ w_gate) * (h @ w_up)) @ w_down

def second_inputs(seed: int = 0) -> dict:
    key = jax.random.key(seed)
    ks = iter(jax.random.split(key, 32))

    def nrm(shape, scale):
        return jax.random.normal(next(ks), shape, f32) * scale

    def dt_bias(shape):
        u = jax.random.uniform(next(ks), shape, f32)
        dt = jnp.exp(u * (math.log(DT_MAX) - math.log(DT_MIN)) + math.log(DT_MIN))
        return dt + jnp.log(-jnp.expm1(-dt))

    def a_log(shape):
        return jnp.log(jax.random.uniform(next(ks), shape, f32, 1.0, 16.0))

    L = DEPTH
    return {
        "x": nrm((BATCH, SEQ, D_MODEL), 1.0),
        "c": nrm((BATCH, D_MODEL), 1.0),
        "ctx": nrm((BATCH, CTX_LEN, D_MODEL), 1.0),
        "c_ctx": nrm((D_MODEL,), 1.0),
        "w_ada": nrm((L, D_MODEL, 6 * D_MODEL), D_MODEL ** -0.5),
        "b_ada": nrm((L, 6 * D_MODEL), 0.02),
        "w_in": nrm((L, D_MODEL, D_IN_PROJ), D_MODEL ** -0.5),
        "conv_w_ssd": nrm((L, CONV_K_2, SSD_CONV_CH), CONV_K_2 ** -0.5),
        "conv_b_ssd": nrm((L, SSD_CONV_CH), 0.02),
        "dt_bias_ssd": dt_bias((L, N_DIR, SSD_HEADS)),
        "a_log_ssd": a_log((L, N_DIR, SSD_HEADS)),
        "d_skip_ssd": 1.0 + nrm((L, SSD_HEADS), 0.1),
        "norm_w_ssd": 1.0 + nrm((L, SSD_WIDTH), 0.1),
        "conv_w_gdn": nrm((L, CONV_K_2, GDN_CONV_CH), CONV_K_2 ** -0.5),
        "dt_bias_gdn": dt_bias((L, N_DIR, GDN_HEADS)),
        "a_log_gdn": a_log((L, N_DIR, GDN_HEADS)),
        "norm_w_gdn": 1.0 + nrm((L, GDN_HEAD_DIM), 0.1),
        "w_out": nrm((L, D_MIX, D_MODEL), D_MIX ** -0.5 * DEEPNORM_BETA),
        "ln1_g": 1.0 + nrm((L, D_MODEL), 0.1),
        "ln1_b": nrm((L, D_MODEL), 0.02),
        "w_ffn_gate": nrm((L, D_MODEL, D_FF), D_MODEL ** -0.5),
        "w_ffn_up": nrm((L, D_MODEL, D_FF), D_MODEL ** -0.5),
        "w_ffn_down": nrm((L, D_FF, D_MODEL), D_FF ** -0.5 * DEEPNORM_BETA),
        "ln2_g": 1.0 + nrm((L, D_MODEL), 0.1),
        "ln2_b": nrm((L, D_MODEL), 0.02),
    }

def second_block(x, c, ctx, c_ctx, w_ada, b_ada, w_in, conv_w_ssd, conv_b_ssd, dt_bias_ssd, a_log_ssd,
              d_skip_ssd, norm_w_ssd, conv_w_gdn, dt_bias_gdn, a_log_gdn, norm_w_gdn, w_out,
              ln1_g, ln1_b, w_ffn_gate, w_ffn_up, w_ffn_down, ln2_g, ln2_b):
    rows = x.shape[1] // GRID_W
    bsz = x.shape[0]
    for l in range(DEPTH):
        mod_l = (jax.nn.silu(c) @ w_ada[l] + b_ada[l]).reshape(bsz, 6, 1, D_MODEL)
        mod_c = (jax.nn.silu(c_ctx) @ w_ada[l] + b_ada[l]).reshape(6, D_MODEL)
        sh1, sc1, g1, sh2, sc2, g2 = (mod_l[:, i] for i in range(6))
        csh1, csc1, cg1, csh2, csc2, cg2 = (mod_c[i] for i in range(6))
        y_c, y_l = token_mixers(
            ctx * (1.0 + csc1) + csh1, x * (1.0 + sc1) + sh1, rows, w_in[l],
            conv_w_ssd[l], conv_b_ssd[l], dt_bias_ssd[l], a_log_ssd[l], d_skip_ssd[l], norm_w_ssd[l],
            conv_w_gdn[l], dt_bias_gdn[l], a_log_gdn[l], norm_w_gdn[l])
        x = layer_norm(DEEPNORM_ALPHA * x + g1 * (y_l @ w_out[l]), ln1_g[l], ln1_b[l])
        x = layer_norm(DEEPNORM_ALPHA * x + g2 * swiglu(x * (1.0 + sc2) + sh2, w_ffn_gate[l],
                                                        w_ffn_up[l], w_ffn_down[l]), ln2_g[l], ln2_b[l])
        if l + 1 < DEPTH:
            ctx = layer_norm(DEEPNORM_ALPHA * ctx + cg1 * (y_c @ w_out[l]), ln1_g[l], ln1_b[l])
            ctx = layer_norm(DEEPNORM_ALPHA * ctx + cg2 * swiglu(ctx * (1.0 + csc2) + csh2, w_ffn_gate[l],
                                                                w_ffn_up[l], w_ffn_down[l]), ln2_g[l], ln2_b[l])
    return x


def setup_inputs(seed=0):
    out = dict(first_inputs(seed))
    for name, value in second_inputs(seed + 1).items():
        if name != "x":
            out[name + "_2"] = value
    return out


def reference(
    x, mem, positions, g_mix, g_mem, w_in, g_qn_attn, g_kn_attn, w_conv, w_mem_kv, g_qn_mem,
    g_kn_mem, w_proj_attn, w_proj_conv, w_proj_mem, w_out, g_ffn, w_router_group,
    b_router_group, w_router_expert, b_router_expert, w_gate, w_up, w_down, c_2, ctx_2, c_ctx_2,
    w_ada_2, b_ada_2, w_in_2, conv_w_ssd_2, conv_b_ssd_2, dt_bias_ssd_2, a_log_ssd_2,
    d_skip_ssd_2, norm_w_ssd_2, conv_w_gdn_2, dt_bias_gdn_2, a_log_gdn_2, norm_w_gdn_2, w_out_2,
    ln1_g_2, ln1_b_2, w_ffn_gate_2, w_ffn_up_2, w_ffn_down_2, ln2_g_2, ln2_b_2,
):
    x = first_block(
        x, mem, positions, g_mix, g_mem, w_in, g_qn_attn, g_kn_attn, w_conv, w_mem_kv, g_qn_mem,
        g_kn_mem, w_proj_attn, w_proj_conv, w_proj_mem, w_out, g_ffn, w_router_group,
        b_router_group, w_router_expert, b_router_expert, w_gate, w_up, w_down,
    )
    return second_block(
        x, c_2, ctx_2, c_ctx_2, w_ada_2, b_ada_2, w_in_2, conv_w_ssd_2, conv_b_ssd_2,
        dt_bias_ssd_2, a_log_ssd_2, d_skip_ssd_2, norm_w_ssd_2, conv_w_gdn_2, dt_bias_gdn_2,
        a_log_gdn_2, norm_w_gdn_2, w_out_2, ln1_g_2, ln1_b_2, w_ffn_gate_2, w_ffn_up_2,
        w_ffn_down_2, ln2_g_2, ln2_b_2,
    )


_drawn_inputs = setup_inputs


def setup_inputs(seed=0):
    import zlib

    import numpy as np

    out = dict(_drawn_inputs(seed))
    spreads = {}
    factors = {'g_mem': 8.0,
     'g_qn_attn': 6.019,
     'g_kn_attn': 4.198,
     'g_qn_mem': 8.0,
     'g_kn_mem': 4.044,
     'b_router_group': 23.408,
     'b_router_expert': 27.01,
     'ctx_2': 3.821,
     'c_ctx_2': 3.101,
     'b_ada_2': 3.05,
     'conv_b_ssd_2': 64.0,
     'd_skip_ssd_2': 64.0,
     'norm_w_ssd_2': 12.024,
     'norm_w_gdn_2': 2.727,
     'ln2_b_2': 2.856,
     'g_ffn': 3.724}
    for name, (base, spread) in spreads.items():
        noise = np.random.default_rng([zlib.crc32(name.encode()), seed]).standard_normal(out[name].shape)
        drawn = base * np.exp(spread * noise) if base else spread * noise
        out[name] = __import__('jax').numpy.asarray(drawn.astype(out[name].dtype))
    for name, factor in factors.items():
        out[name] = (out[name] * factor).astype(out[name].dtype)
    return out
```

```python
from contextlib import ExitStack

import concourse.bass as bass
import numpy as np
from concourse import mybir

F32 = mybir.dt.float32
I32 = mybir.dt.int32
ALU = mybir.AluOpType
ACT = mybir.ActivationFunctionType
AX = mybir.AxisListType

P = 128
D = 1024
KD = D // P
SEQ = 256
NT = SEQ // P
BANKS = 6
SLOTS = 3
SLOT = 4096
WIDE = 512
EPS = 1e-6
LN_EPS = 1e-5
FAR = -1e30

HEADS, DH = 12, 64
DILATIONS = (1, 4, 16)
BAND = 64
ROT = DH // 8
CONV_TILES = 768 // P
MEM_HEADS, MEM_DH = 4, 128
GROUPS, PER_GROUP, FF = 4, 8, 512
EXPERTS = GROUPS * PER_GROUP
FF_TILES = FF // P
THETA = 500000.0

ROUND = 1.5 * 2.0 ** 23
TURN = (6.28125, 0.001934051513671875, 2 * np.pi - 6.28125 - 0.001934051513671875)

GRID = 64
ROWS = SEQ // GRID
CHUNKS = 4
SSD_HEADS, SSD_P, SSD_G, SSD_N = 16, 64, 2, 128
GDN_HEADS, GDN_DH = 8, 128
TAPS = 5
FFN = 2816
FFN_TILES = FFN // P
ALPHA = 2.0 ** 0.25
CTX_PAD = SEQ + TAPS - 1
ROW_PAD = GRID + TAPS - 1
LAT_PAD = ROWS * ROW_PAD

COLS_A = {"g_mix": (0, 8), "g_mem": (8, 8), "g_ffn": (16, 8), "w_conv": (24, 18),
          "conv_b_ssd_2": (42, 12), "conv_w_ssd_2": (54, 60), "c_ctx_2": (114, 8)}
ROWS_A = 122
COLS_B = {"conv_w_gdn_2": (0, 120), "c_2": (120, 8)}
ROWS_B = 128


class TileOrder:

    def __init__(self):
        self.count = 0
        self.at = {}

    def number(self, key):
        assert key not in self.at, key
        self.at[key] = self.count
        self.count += 1
        return self.at[key]


def weight_stream():
    before = ["in0", "in1", "in2", "in3", "in4", "in9", "mk0", "mk1"]
    before += [f"in{i}" for i in (5, 6, 7, 8, 10, 11, 12, 13, 14, 15)]
    before += ["pa", "pc0", "pc1", "pm", "wo0", "wo1", "ad0", "ad1", "ad2", "ad3"]
    after = ["dta", "xb0", "xb1", "xb2", "k0", "k1", "v0", "v1", "q0", "q1", "z0", "z1", "gt0", "gt1"]
    after += ["ad4", "ad5", "w20", "w21", "w22", "w23", "ad6", "ad7", "ad8", "ad9"]
    after += [f"{w}{i}" for i in range(6) for w in ("fg", "fu")]
    after += [f"fd{i}" for i in range(6)] + ["ad10", "ad11"]
    return before, after


def two_block_kernel(nc, a, out):
    before_experts, after_experts = weight_stream()
    ctx = ExitStack()
    with ctx:
        def sb(name, shape, dt=F32):
            return ctx.enter_context(nc.sbuf_tensor(name, shape, dt))

        def sem(name):
            return ctx.enter_context(nc.semaphore(name))

        ring = sb("ring", [P, SLOTS, SLOT])
        x = sb("x", [P, NT, D])
        const = sb("const", [P, 11, P])
        ident, ones, upto, since, below, above, blk16, lev32, lev64, lev128, slot_row = (const[:, i, :] for i in range(11))
        rows_a = sb("rows_a", [P, 2, P])
        cols = sb("cols", [P, 2 * P])
        head_gain = sb("head_gain", [P, 2, DH])
        mem_gain = sb("mem_gain", [P, 2, MEM_DH])
        router_b = sb("router_b", [P, GROUPS + EXPERTS])
        router_w = sb("router_w", [P, KD, GROUPS + EXPERTS])
        gate_bias = sb("gate_bias", [P, 48])
        decay_rate = sb("decay_rate", [P, 48])
        d_skip = sb("d_skip", [P, SSD_HEADS])
        gdn_gain = sb("gdn_gain", [P, GDN_DH])
        stats = sb("stats", [P, 64])
        pos_i = sb("pos_i", [P, NT], I32)
        rope = sb("rope", [P, 8, 2, NT, ROT])
        inv_freq = sb("inv_freq", [P, ROT])
        overflow = sb("overflow", [P, 1], I32)
        AREA = 35400
        area = sb("area", [P, AREA])

        def at(offset, *shape):
            size = int(np.prod(shape))
            assert offset + size <= AREA, (offset, shape)
            flat = area[:, offset:offset + size]
            names = "abcd"[:len(shape)]
            if len(shape) == 1:
                return flat
            return flat.rearrange(f"p ({' '.join(names)}) -> p {' '.join(names)}", **dict(zip(names, shape)))

        xn = at(0, NT, D)
        cb = at(0, CONV_TILES, SEQ)
        hT = at(2048, KD, SEQ)
        mergedT = at(2048, KD, SEQ)
        mem = at(4096, NT, D)
        o_mem = at(4096, NT, MEM_HEADS * MEM_DH)
        mT = at(6144, KD, SEQ)
        o_dil = at(6144, NT, 3, 256)
        qk = at(8192, NT, 24, DH)
        oT = at(8192, 6, SEQ)
        v_dil = at(11264, NT, 12 * DH)
        qk_mem = at(12800, NT, 8, MEM_DH)
        PT = at(12800, 3, 4, P)
        v_mem = at(14848, NT, 512)
        qkT = at(15872, 12, SEQ)
        merged = at(15872, NT, D)
        qk_memT = at(18944, 8, SEQ)
        gates = at(20992, NT, 3 * D)
        u_conv = at(27136, CONV_TILES, SEQ + 2)
        S = at(28684, 3, 2, SEQ)
        squares = at(28684, 24, DH)
        mask = at(30220, 4, SEQ)
        tap = at(31244, 2, SEQ)
        mix = at(31756, 768)
        neg_max = at(32524, NT, 4, 4)
        den = at(32556, NT, 4, 4)
        combine = at(32588, 4, 3, 4)

        mod_a = at(0, 2, D)
        mod_c = at(2048, 2, D)
        h2 = at(4096, NT, D)
        h2T = at(6144, KD, SEQ)
        ffn_gain = at(31000, D)
        place = at(8192, NT, GROUPS, P)
        placeT = at(9216, GROUPS, SEQ)
        place_now = at(10240, SEQ)
        hcT = at(10496, KD, P)
        silu_g = at(11520, 2, FF)
        act = at(12544, 2, FF)
        actT = at(13568, 2, FF_TILES, P)
        y_group = at(14592, D)
        r_log = at(15616, NT, 36)
        r_tmp = at(15688, 8, NT, 8)
        r_big = at(15816, NT, GROUPS, 8)
        r_hot = at(15880, NT, GROUPS)
        r_we = at(15888, NT, 8)
        r_rank = at(15904, 12)
        r_prio = sb("r_prio", [P, 8])
        w_slot = at(15924, GROUPS, 8)
        r_col = at(15956, 16, NT)
        c_wide = at(34300, KD, P)
        c_ctx_wide = at(17024, KD, P)
        ctx_in = at(18048, NT, D)
        h_lat = at(20096, NT, D)

        head_stats = squares_root = sb("head_stats", [P, NT, 24])
        distance, mask_i = tap[:, 0, :].bitcast(I32), tap[:, 1, :].bitcast(I32)

        def flat(ap):
            return ap.rearrange({1: "n -> n", 2: "a n -> (a n)", 3: "a b n -> (a b n)"}[len(ap.shape)])

        small_loads = [(pos_i[:, t:t + 1], a["positions"][0, t * P:(t + 1) * P].rearrange("(p o) -> p o", o=1)) for t in range(NT)]
        small_loads += [(router_w[:, :, 0:4], a["w_router_group"][0].rearrange("(k p) n -> p k n", p=P)),
                        (router_w[:, :, 4:36], a["w_router_expert"][0].rearrange("(k p) n -> p k n", p=P))]
        for dst, name in ((head_gain[:, 0, :], "g_qn_attn"), (head_gain[:, 1, :], "g_kn_attn"),
                          (mem_gain[:, 0, :], "g_qn_mem"), (mem_gain[:, 1, :], "g_kn_mem"),
                          (router_b[:, 0:4], "b_router_group"), (router_b[:, 4:36], "b_router_expert"),
                          (gate_bias[:, 0:32], "dt_bias_ssd_2"), (gate_bias[:, 32:48], "dt_bias_gdn_2"),
                          (decay_rate[:, 0:32], "a_log_ssd_2"), (decay_rate[:, 32:48], "a_log_gdn_2"),
                          (d_skip[:, :], "d_skip_ssd_2"), (gdn_gain[:, :], "norm_w_gdn_2")):
            small_loads.append((dst, flat(a[name]).partition_broadcast(P)))
        N_SMALL = len(small_loads)

        hB = at(4096, KD, 2 * SEQ)
        v_gdn = at(0, CHUNKS, D)
        xs = at(8192, CHUNKS, D)
        bm = at(12288, CHUNKS, 256)
        bmT = at(13312, SSD_G, 2 * SEQ)
        cmT = at(14336, SSD_G, SEQ)
        k_gdn = at(14848, CHUNKS, D)
        qT = at(18944, GDN_HEADS, SEQ)
        y_ssd = at(20992, NT, D)
        o_gdn = at(23040, NT, D)
        SMALL = 25088
        raw = at(SMALL, CHUNKS, 48)
        soft = at(SMALL + 192, CHUNKS, 48)
        beta = at(SMALL + 384, CHUNKS, 16)
        log_a = at(SMALL + 448, CHUNKS, 2, 24)
        cum = at(SMALL + 640, 2, CHUNKS, 24)
        cum_exp = at(SMALL + 832, 2, CHUNKS, 24)
        total = at(SMALL + 1024, 2, CHUNKS, 24)
        rest = at(SMALL + 1216, 2, CHUNKS, 24)
        beta_cum = at(SMALL + 1408, 2, CHUNKS, 8)
        k_root = at(SMALL + 1472, CHUNKS, 8)
        q_root = at(SMALL + 1504, NT, 8)
        y_root = at(SMALL + 1520, NT, SSD_G)
        o_root = at(SMALL + 1524, NT, 8)
        TEMP = SMALL + 1600
        pad = at(TEMP, 3, CTX_PAD + LAT_PAD)
        conv = at(TEMP + 1596, 3, CTX_PAD + LAT_PAD)
        chan = at(TEMP + 3192, 3, 2 * SEQ)
        ssd_state = at(TEMP, SSD_G, 512)
        xdt = at(TEMP + 1024, D)
        x_rest = at(TEMP + 2048, D)
        att = at(TEMP + 3072, 4, 4, P)
        cb_mask = at(TEMP + 5120, SSD_G, P)
        y_tmp = at(TEMP + 5376, 512)
        q_square = at(TEMP, GDN_HEADS, SEQ)
        k_square = at(TEMP + 2048, D)
        gdn_state = at(TEMP, GDN_HEADS, P)
        o_tmp = [at(TEMP + 1024 + 512 * h, 4, P) for h in range(2)]
        places = [8192 + 512 * i for i in range(12)] + [TEMP + 2048 + 512 * i for i in range(4)]
        buf = [[at(places[8 * h + i], 4, P) for i in range(8)] for h in range(2)]
        z_silu = at(TEMP, NT, D)
        gate_silu = at(TEMP + 2048, NT, D)
        yoT = at(8192, 2 * KD, SEQ)
        mod_rows = at(0, 4, D)
        norm_rows = at(14848, 5, D)
        h_ffn = at(TEMP, NT, D)
        h_ffnT = at(TEMP + 2048, KD, SEQ)
        ffn_silu = at(TEMP + 4096, 2, 2, SEQ)
        ffn_act = at(4096, FFN_TILES, SEQ)
        ffn_tmp = at(TEMP + 5120, 2, 512)

        psum = ctx.enter_context(nc.psum_tensor("psum", [P, 8, WIDE], F32))
        order = TileOrder()
        filled = sem("filled")
        drained = [sem(f"drained{b}") for b in range(BANKS)]
        landed = [sem(f"landed{s}") for s in range(SLOTS)]

        def wait_filled(eng, key):
            n = order.at[key]
            eng.wait_ge(filled, n + 1)
            return psum[:, n % BANKS, :]

        def drain_of(key):
            return drained[order.at[key] % BANKS]

        def wait_drained(eng, key):
            n = order.at[key]
            eng.wait_ge(drained[n % BANKS], n // BANKS + 1)

        s = {name: sem(name) for name in (
            "consts_ready", "x_in", "mem_in", "rows_in", "small_in", "wide_in", "ctx_in",
            "pool_step", "dve_step", "act_step", "root_asked", "root_done", "xn_ready", "mn_ready",
            "angles_ready", "tables_ready", "qk_ready", "logits_ready", "probs_ready", "zeros_ready",
            "z_ready", "peaks_ready", "peaks_exp", "o_ready", "gates_ready", "merged_ready", "x_mixed",
            "h2_ready", "gate_logits", "gate_exp", "hot_ready", "place_ready", "flag_ready",
            "x_ready", "c_silu", "c_wide_ready", "h_ready",
            "out_done", "mod_in", "hctx_ready", "hlat_ready", "pads_ready", "conv_ready", "channels_ready", "abs_ready",
            "abs_exp", "one_ready", "one_ln", "beta_raw", "beta_ready", "rate_ready", "log_a_ready", "cum_ready", "cum_exp",
            "x_rest_ready", "ssd_clipped", "ssd_decay", "att_ready", "kn_ready", "q_square_ready", "y_ssd_ready",
            "gdn_clipped", "gdn_clippedT", "gdn_decay", "gdn_decayT", "gdn_masked", "gdn_maskedT", "n_ready",
            "one_plus_n", "level_ready", "kv_ready", "yo_ready", "rows2_in", "norm_in", "h_ffn_ready", "beta_cum_ready",
            "gdn_done")}
        unit_use = {}
        MOE_TILES = 2 + 3 * PER_GROUP + 4

        def unit_source(name):
            kind, i = name.rstrip("0123456789"), int(name[len(name.rstrip("0123456789")):] or 0)
            if name.startswith("w2"):
                kind, i = "w2", int(name[2:])
            if kind == "in":
                return [(a["w_in"][0, :, i * WIDE:(i + 1) * WIDE], 8)]
            if kind == "mk":
                return [(a["w_mem_kv"][0, :, i * WIDE:(i + 1) * WIDE], 8)]
            if kind == "pa":
                return [(a["w_proj_attn"][0], 2)]
            if kind == "pc":
                return [(a["w_proj_conv"][0, 512 * i:min(512 * i + 512, 768), :], 4 if i == 0 else 2)]
            if kind == "pm":
                return [(a["w_proj_mem"][0], 4)]
            if kind == "wo":
                return [(a["w_out"][0, :, i * WIDE:(i + 1) * WIDE], 8)]
            if kind == "ad":
                return [(a["w_ada_2"][0, :, i * WIDE:(i + 1) * WIDE], 8)]
            first = {"xb": 1024, "q": 2592, "k": 3616, "v": 4640, "z": 0, "gt": 5664}
            if kind in first:
                c = first[kind] + i * WIDE
                return [(a["w_in_2"][0, :, c:c + WIDE], 8)]
            if kind == "dta":
                return [(a["w_in_2"][0, :, 2560:2592], 8), (a["w_in_2"][0, :, 6688:6720], 8)]
            if kind == "w2":
                return [(a["w_out_2"][0, 512 * i:512 * i + 512, :], 4)]
            if kind in ("fg", "fu"):
                w = a["w_ffn_gate_2" if kind == "fg" else "w_ffn_up_2"]
                return [(w[0, :, i * WIDE:min((i + 1) * WIDE, FFN)], 8)]
            assert kind == "fd", name
            return [(a["w_ffn_down_2"][0, 512 * i:min(512 * i + 512, FFN), :], 4 if i < 5 else 2)]

        def unit_views(name, slot):
            views, offset = [], 0
            for src, tiles in unit_source(name):
                width = src.shape[1]
                views.append(ring[:, slot, offset:offset + tiles * width].rearrange("p (k n) -> p k n", k=tiles))
                offset += tiles * width
            return views

        expert_units = [("g", 0), ("u", 0)]
        for e in range(1, PER_GROUP):
            expert_units += [("g", e), ("u", e), ("d", e - 1)]
        expert_units += [("d", PER_GROUP - 1)]
        GROUP_UNITS = len(expert_units)
        TILE = {"g": 2, "u": 3, "t": 4}

        def released_by(q):
            kind, e = expert_units[q]
            if kind == "d":
                return TILE["t"] + 3 * (e + 1) if e < PER_GROUP - 1 else 2 + 3 * PER_GROUP
            return TILE[kind] + 3 * e

        unit_number, landed_by, arrivals = {}, {}, [0] * SLOTS
        for n, name in enumerate(before_experts):
            unit_number[name] = n
            arrivals[n % SLOTS] += 16 * len(unit_source(name))
            landed_by[name] = arrivals[n % SLOTS]
        FIRST_UNIT = len(before_experts)
        expert_arrivals = list(arrivals)
        for n, name in enumerate(after_experts, FIRST_UNIT + EXPERTS * 3):
            unit_number[name] = n
            arrivals[n % SLOTS] += 16 * len(unit_source(name))
            landed_by[name] = arrivals[n % SLOTS] + 16 * EXPERTS * 3 // SLOTS

        block = ctx.enter_context(nc.Block())

        CHANNELS = [("xs", i) for i in range(8)] + [("bm", i) for i in range(2)] + [("cm", i) for i in range(2)]
        CHANNELS += [(kind, i) for kind in "kvq" for i in range(8)]
        TURNED = ("xs", "bm", "k", "v")
        LAT_ONLY = ("cm", "q")
        SEQUENCE = ((0, 1, 2, 3), (1, 0, 3, 2))
        LEVELS = (lev32, lev64, lev128)

        def channel_out(n):
            kind, i = CHANNELS[n]
            return {"bm": lambda: bmT[:, i, :], "cm": lambda: cmT[:, i, :], "q": lambda: qT[:, i, :]}.get(
                kind, lambda: chan[:, n % 3, :])()

        def second_block_pe(pe, open_tile, unit, used, transposes, product, tokens_by_weights, modulation):
            for src, h, ready in ((0, ctx_in, "hctx_ready"), (1, h_lat, "hlat_ready")):
                for t in range(NT):
                    pe.wait_ge(s[ready], t + 1)
                    for half in range(2):
                        transposes(("hB", src, t, half), [h[:, t, (4 * half + j) * P:(4 * half + j + 1) * P] for j in range(4)])
            for src in range(2):
                for t in range(NT):
                    for half in range(2):
                        wait_drained(pe, ("hB", src, t, half))
            w_dt, w_ba = unit("dta")
            dst = open_tile("dta")
            for c in range(CHUNKS):
                for i, w in enumerate((w_dt, w_ba)):
                    last = product(dst[:, 64 * c + 32 * i:64 * c + 32 * i + 32], lambda k: hB[:, k, c * P:(c + 1) * P],
                                   lambda k: w[:, k, :], KD)
            last.then_inc(filled, 1)
            used("dta")

            def turn_channels(n):
                if n >= 0 and CHANNELS[n][0] in TURNED:
                    pe.wait_ge(s["channels_ready"], n + 1)
                    transposes(("turned", n), [channel_out(n)[:, c * P:(c + 1) * P] for c in range(CHUNKS)])

            names = ["xb0", "xb1", "xb2", "k0", "k1", "v0", "v1", "q0", "q1"]
            for n in range(len(CHANNELS)):
                if n % 4 == 0:
                    w, = unit(names[n // 4])
                tokens = slice(SEQ if CHANNELS[n][0] in LAT_ONLY else 0, 2 * SEQ)
                dst = open_tile(("channel", n))
                product(dst[:, 0:tokens.stop - tokens.start], lambda k: w[:, k, n % 4 * P:(n % 4 + 1) * P],
                        lambda k: hB[:, k, tokens], KD).then_inc(filled, 1)
                if n % 4 == 3:
                    used(names[n // 4])
                turn_channels(n - 2)
                if n == 2:
                    pe.wait_ge(s["log_a_ready"], 1)
                    dst = open_tile("cum")
                    for d, order_of in enumerate((upto, since)):
                        nc.tensor.matmul(dst[:, 96 * d:96 * d + 96], order_of, log_a[:, :, d, :], start=True, stop=True)
                    nc.tensor.matmul(dst[:, 192:384], ones, log_a.rearrange("p c d h -> p (c d h)"),
                                     start=True, stop=True).then_inc(filled, 1)
            for n in (len(CHANNELS) - 2, len(CHANNELS) - 1):
                turn_channels(n)

            step = 0
            pe.wait_ge(s["cum_exp"], 3)
            for n in range(12):
                if CHANNELS[n][0] in TURNED:
                    wait_drained(pe, ("turned", n))
            for d in range(2):
                for ci, c in enumerate(SEQUENCE[d]):
                    if c >= 2:
                        tok, lat = slice(c * P, (c + 1) * P), slice((c - 2) * P, (c - 1) * P)
                        dst = open_tile(("cb", d, c))
                        for g in range(SSD_G):
                            last = nc.tensor.matmul(dst[:, g * P:(g + 1) * P], bmT[:, g, tok], cmT[:, g, lat], start=True, stop=True)
                        last.then_inc(filled, 1)
                        for q in range(4):
                            dst = open_tile(("ssd_rows", d, c, q))
                            for i in range(4):
                                last = nc.tensor.matmul(dst[:, i * P:(i + 1) * P],
                                                        log_a[:, c, d, 4 * q + i:4 * q + i + 1].to_broadcast([P, P]),
                                                        (upto, since)[d], start=True, stop=True)
                            last.then_inc(filled, 1)
                        for g in range(SSD_G):
                            if g == 0:
                                wait_drained(pe, ("state", d, SEQUENCE[d][ci - 1], 0))
                                wait_drained(pe, ("state", d, SEQUENCE[d][ci - 1], 1))
                            dst = open_tile(("y_state", d, c, g))
                            nc.tensor.matmul(dst, cmT[:, g, lat], ssd_state[:, g, :], start=True, stop=True).then_inc(filled, 1)
                    pe.wait_ge(s["x_rest_ready"], 4 * d + ci + 1)
                    if c >= 2:
                        for g in range(SSD_G):
                            pe.wait_ge(s["att_ready"], 4 * step + 2 * g + 2)
                            dst = open_tile(("y_inner", d, c, g))
                            for j in range(8):
                                h = 8 * g + j
                                last = nc.tensor.matmul(dst[:, j * SSD_P:(j + 1) * SSD_P], att[:, h // 4, h % 4, :],
                                                        xdt[:, h * SSD_P:(h + 1) * SSD_P], start=True, stop=True)
                            last.then_inc(filled, 1)
                        step += 1
                    if ci < 3:
                        for g in range(SSD_G):
                            dst = open_tile(("state", d, c, g))
                            nc.tensor.matmul(dst, bm[:, c, g * P:(g + 1) * P], x_rest[:, g * 512:(g + 1) * 512],
                                             start=True, stop=True).then_inc(filled, 1)

            pe.wait_ge(s["q_square_ready"], 1)
            dst = open_tile("q_sums")
            for t in range(NT):
                for h in range(GDN_HEADS):
                    last = nc.tensor.matmul(dst[:, 8 * t + h:8 * t + h + 1], q_square[:, h, t * P:(t + 1) * P], ones[:, 0:1],
                                            start=True, stop=True)
            last.then_inc(filled, 1)
            pe.wait_ge(s["kn_ready"], CHUNKS)

            def four(key, lhs, rhs):
                dst = open_tile(key)
                for i in range(4):
                    last = nc.tensor.matmul(dst[:, i * P:(i + 1) * P], lhs(i), rhs(i), start=True, stop=True)
                last.then_inc(filled, 1)

            m = lm = 0
            for d in range(2):
                for ci, c in enumerate(SEQUENCE[d]):
                    lat = slice((c - 2) * P, (c - 1) * P)
                    for h in range(2):
                        transposes(("gkT", d, c, h), [k_gdn[:, c, (4 * h + i) * P:(4 * h + i + 1) * P] for i in range(4)])
                    for h in range(2):
                        four(("gR", d, c, h), lambda i: log_a[:, c, d, 16 + 4 * h + i:17 + 4 * h + i].to_broadcast([P, P]),
                             lambda i: (upto, since)[d])
                    for h in range(2):
                        kT = buf[h][6]
                        wait_drained(pe, ("gkT", d, c, h))
                        four(("gKK", d, c, h), lambda i: kT[:, i, :], lambda i: kT[:, i, :])
                        if c >= 2:
                            four(("gQK", d, c, h), lambda i: kT[:, i, :], lambda i: qT[:, 4 * h + i, lat])
                    for h in range(2):
                        wait_drained(pe, ("gKK", d, c, h))
                        transposes(("gAT", d, c, h), [buf[h][1][:, i, :] for i in range(4)])
                    for h in range(2):
                        b = buf[h]
                        pe.wait_ge(s["n_ready"], 2 * (m + h) + 2)
                        four(("gP2", d, c, h), lambda i: b[5][:, i, :], lambda i: b[4][:, i, :])
                        four(("gP2T", d, c, h), lambda i: b[4][:, i, :], lambda i: b[5][:, i, :])
                    for h in range(2):
                        b = buf[h]
                        pe.wait_ge(s["one_plus_n"], m + h + 1)
                        wait_drained(pe, ("gP2", d, c, h))
                        wait_drained(pe, ("gP2T", d, c, h))
                        four(("gX2", d, c, h), lambda i: b[6][:, i, :], lambda i: b[7][:, i, :])
                        four(("gP4", d, c, h), lambda i: b[6][:, i, :], lambda i: b[0][:, i, :])
                        four(("gP4T", d, c, h), lambda i: b[0][:, i, :], lambda i: b[6][:, i, :])
                    for h in range(2):
                        b = buf[h]
                        for key in ("gX2", "gP4", "gP4T"):
                            wait_drained(pe, (key, d, c, h))
                        four(("gX4", d, c, h), lambda i: b[5][:, i, :], lambda i: b[7][:, i, :])
                        four(("gP8T", d, c, h), lambda i: b[4][:, i, :], lambda i: b[5][:, i, :])
                    for h in range(2):
                        b = buf[h]
                        for key in ("gX4", "gP8T"):
                            wait_drained(pe, (key, d, c, h))
                        four(("gX8", d, c, h), lambda i: b[6][:, i, :], lambda i: b[7][:, i, :])
                    for h in range(2):
                        wait_drained(pe, ("gX8", d, c, h))
                        transposes(("gXT", d, c, h, 0), [buf[h][7][:, i, :] for i in range(4)])
                    for lev in range(3):
                        for h in range(2):
                            b = buf[h]
                            pe.wait_ge(s["level_ready"], 3 * m + 2 * lev + h + 1)
                            four(("gT", d, c, h, lev), lambda i: b[6][:, i, :], lambda i: b[7][:, i, :])
                        for h in range(2):
                            b = buf[h]
                            wait_drained(pe, ("gXT", d, c, h, lev))
                            wait_drained(pe, ("gT", d, c, h, lev))
                            four(("gY", d, c, h, lev), lambda i: b[4][:, i, :], lambda i: b[0][:, i, :])
                        for h in range(2):
                            wait_drained(pe, ("gY", d, c, h, lev))
                            transposes(("gXT", d, c, h, lev + 1), [buf[h][7][:, i, :] for i in range(4)])
                    for h in range(2):
                        b = buf[h]
                        pe.wait_ge(s["kv_ready"], m + h + 1)
                        wait_drained(pe, ("gXT", d, c, h, 3))
                        if ci:
                            four(("gw", d, c, h), lambda i: b[0][:, i, :], lambda i: b[4][:, i, :])
                    for h in range(2):
                        b = buf[h]
                        if ci:
                            wait_drained(pe, ("gw", d, c, h))
                            wait_drained(pe, ("gS", d, SEQUENCE[d][ci - 1], h))
                        dst = open_tile(("gv", d, c, h))
                        for i in range(4):
                            part = dst[:, i * P:(i + 1) * P]
                            last = nc.tensor.matmul(part, b[4][:, i, :], b[1][:, i, :], start=True, stop=not ci)
                            if ci:
                                last = nc.tensor.matmul(part, b[3][:, i, :], gdn_state[:, 4 * h + i, :], start=False, stop=True)
                        last.then_inc(filled, 1)
                        if c >= 2:
                            four(("go1", d, c, h), lambda i: qT[:, 4 * h + i, lat], lambda i: gdn_state[:, 4 * h + i, :])
                    for h in range(2):
                        b = buf[h]
                        wait_drained(pe, ("gv", d, c, h))
                        if c >= 2:
                            wait_drained(pe, ("gQK", d, c, h))
                            four(("go2", d, c, h), lambda i: b[2][:, i, :], lambda i: b[5][:, i, :])
                        if ci < 3:
                            four(("gS", d, c, h), lambda i: b[6][:, i, :], lambda i: b[5][:, i, :])
                    m += 2

            lat = hB[:, :, SEQ:2 * SEQ]
            for kind in ("z", "gt"):
                for i in range(2):
                    w, = unit(f"{kind}{i}")
                    for t in range(NT):
                        tokens_by_weights((kind, i, t), lat, t, w)
                    used(f"{kind}{i}")
            modulation(4, False)
            modulation(5, False)
            for t in range(NT):
                for src in range(2):
                    pe.wait_ge(s["yo_ready"], 2 * src + t + 1)
            for src, rows in enumerate((y_ssd, o_gdn)):
                for t in range(NT):
                    for half in range(2):
                        transposes(("yoT", src, t, half), [rows[:, t, (4 * half + j) * P:(4 * half + j + 1) * P] for j in range(4)])
            for src in range(2):
                for t in range(NT):
                    for half in range(2):
                        wait_drained(pe, ("yoT", src, t, half))

            def long_product(key, names, lhs):
                banks = [open_tile((key, t, half)) for t in range(NT) for half in range(2)]
                k0 = 0
                for n, name in enumerate(names):
                    w, = unit(name)
                    tiles = w.shape[1]
                    for j, dst in enumerate(banks):
                        t, half = j // 2, j % 2
                        last = product(dst, lambda k: lhs[:, k0 + k, t * P:(t + 1) * P],
                                       lambda k: w[:, k, half * WIDE:(half + 1) * WIDE], tiles,
                                       first=n == 0, final=n == len(names) - 1)
                        if n == len(names) - 1:
                            last.then_inc(filled, 1)
                        elif j == len(banks) - 1:
                            last.then_inc(passed, 1)
                            unit_passed.append(name)
                    k0 += tiles
                used(names[-1])

            long_product("w2", [f"w2{i}" for i in range(4)], yoT)
            for i in range(6, 10):
                modulation(i, False)
            for t in range(NT):
                pe.wait_ge(s["h_ffn_ready"], t + 1)
                for half in range(2):
                    transposes(("h_ffnT", t, half), [h_ffn[:, t, (4 * half + j) * P:(4 * half + j + 1) * P] for j in range(4)])
            for t in range(NT):
                for half in range(2):
                    wait_drained(pe, ("h_ffnT", t, half))
            for i in range(6):
                views = [unit(f"{kind}{i}")[0] for kind in ("fg", "fu")]
                for j in range(views[0].shape[2] // 256):
                    for kind, w in zip(("fg", "fu"), views):
                        dst = open_tile((kind, 2 * i + j))
                        for c in range(2):
                            ch = slice(256 * j + c * P, 256 * j + (c + 1) * P)
                            last = product(dst[:, c * SEQ:(c + 1) * SEQ], lambda k: w[:, k, ch], lambda k: h_ffnT[:, k, :], KD)
                        last.then_inc(filled, 1)
                used(f"fg{i}")
                used(f"fu{i}")
            for j in range(FFN_TILES // 2):
                wait_drained(pe, ("fu", j))
            long_product("fd", [f"fd{i}" for i in range(6)], ffn_act)
            modulation(10, False)
            modulation(11, False)

        passed = sem("passed")
        unit_passed = []

        def second_block_act(eng, root, copy_out):
            for src in range(2):
                for t in range(NT):
                    for half in range(2):
                        copy_out(("hB", src, t, half), hB[:, 4 * half:4 * half + 4, src * SEQ + t * P:src * SEQ + (t + 1) * P])
            eng.wait_ge(s["beta_raw"], 1)
            nc.scalar.activation(beta, beta, ACT.Sigmoid).then_inc(s["beta_ready"], 1)
            nc.scalar.activation(decay_rate[:, :], decay_rate[:, :], ACT.Exp).then_inc(s["rate_ready"], 1)
            eng.wait_ge(s["abs_ready"], 1)
            nc.scalar.activation(soft, soft, ACT.Exp, scale=-1.0).then_inc(s["abs_exp"], 1)
            eng.wait_ge(s["one_ready"], 1)
            nc.scalar.activation(soft, soft, ACT.Ln).then_inc(s["one_ln"], 1)
            eng.wait_ge(s["pads_ready"], 1)

            def pad_in(n):
                key = ("channel", n)
                if n >= 3:
                    eng.wait_ge(s["conv_ready"], n - 2)
                src = wait_filled(eng, key)
                dst, lat = pad[:, n % 3, :], 0
                if CHANNELS[n][0] not in LAT_ONLY:
                    nc.scalar.copy(dst[:, 2:2 + SEQ], src[:, 0:SEQ])
                    lat = SEQ
                rows = dst[:, CTX_PAD:].rearrange("p (r c) -> p r c", r=ROWS)[:, :, 2:2 + GRID]
                nc.scalar.copy(rows, src[:, lat:lat + SEQ].rearrange("p (r c) -> p r c", r=ROWS)).then_inc(drain_of(key), 1)

            def activate(n):
                kind, _ = CHANNELS[n]
                eng.wait_ge(s["conv_ready"], n + 1)
                if n >= 3 and CHANNELS[n - 3][0] in TURNED:
                    wait_filled(eng, ("turned", n - 3))
                src, dst, lat = conv[:, n % 3, :], channel_out(n), 0
                bias = {"bias": cols[:, 42 + n:43 + n]} if n < 12 else {}
                if kind not in LAT_ONLY:
                    nc.scalar.activation(dst[:, 0:SEQ], src[:, 0:SEQ], ACT.Silu, **bias)
                    lat = SEQ
                rows = src[:, CTX_PAD:].rearrange("p (r c) -> p r c", r=ROWS)[:, :, 0:GRID]
                nc.scalar.activation(dst[:, lat:lat + SEQ].rearrange("p (r c) -> p r c", r=ROWS), rows, ACT.Silu,
                                     **bias).then_inc(s["channels_ready"], 1)

            for n in range(len(CHANNELS) + 1):
                if n < len(CHANNELS):
                    pad_in(n)
                if n >= 1:
                    activate(n - 1)
            eng.wait_ge(s["cum_ready"], 1)
            nc.scalar.activation(cum_exp, cum, ACT.Exp).then_inc(s["cum_exp"], 1)
            nc.scalar.activation(total, total, ACT.Exp).then_inc(s["cum_exp"], 1)
            nc.scalar.activation(rest, rest, ACT.Exp).then_inc(s["cum_exp"], 1)
            n = 0
            for d in range(2):
                for c in SEQUENCE[d][2:]:
                    for q in range(4):
                        n += 1
                        eng.wait_ge(s["ssd_clipped"], n)
                        nc.scalar.activation(att[:, q, :, :], att[:, q, :, :], ACT.Exp).then_inc(s["ssd_decay"], 1)
            root(k_root)
            root(q_root)

            def out4(key, dst, scale=1.0):
                src = wait_filled(eng, key).rearrange("p (h c) -> p h c", h=4)
                nc.scalar.activation(dst, src, ACT.Copy, scale=scale).then_inc(drain_of(key), 1)

            m = lm = 0
            for d in range(2):
                for ci, c in enumerate(SEQUENCE[d]):
                    for h in range(2):
                        out4(("gkT", d, c, h), buf[h][6])
                    for h in range(2):
                        eng.wait_ge(s["gdn_clipped"], m + h + 1)
                        nc.scalar.activation(buf[h][1], buf[h][1], ACT.Exp, scale=-1.0).then_inc(s["gdn_decay"], 1)
                        if c >= 2:
                            eng.wait_ge(s["gdn_clippedT"], lm + h + 1)
                            nc.scalar.activation(buf[h][2], buf[h][2], ACT.Exp).then_inc(s["gdn_decayT"], 1)
                    for h in range(2):
                        out4(("gAT", d, c, h), buf[h][3])
                    for h in range(2):
                        out4(("gP2", d, c, h), buf[h][0])
                        out4(("gP2T", d, c, h), buf[h][6])
                    for h in range(2):
                        out4(("gP4", d, c, h), buf[h][4])
                        out4(("gP4T", d, c, h), buf[h][5])
                    for h in range(2):
                        out4(("gP8T", d, c, h), buf[h][6])
                    for h in range(2):
                        out4(("gXT", d, c, h, 0), buf[h][4])
                    for lev in range(3):
                        for h in range(2):
                            out4(("gT", d, c, h, lev), buf[h][0])
                        for h in range(2):
                            out4(("gXT", d, c, h, lev + 1), buf[h][4])
                    if ci:
                        for h in range(2):
                            out4(("gw", d, c, h), buf[h][3], scale=-1.0)
                    for h in range(2):
                        out4(("gv", d, c, h), buf[h][5])
                    m += 2
                    lm += 2 * (c >= 2)
            for kind, dst in (("z", z_silu), ("gt", gate_silu)):
                for i in range(2):
                    for t in range(NT):
                        if kind == "z" and i == 0 and t == 0:
                            eng.wait_ge(s["gdn_done"], 1)
                        copy_out((kind, i, t), dst[:, t, i * WIDE:(i + 1) * WIDE], func=ACT.Silu)
            root(y_root)
            root(o_root)
            for src in range(2):
                for t in range(NT):
                    for half in range(2):
                        copy_out(("yoT", src, t, half), yoT[:, 8 * src + 4 * half:8 * src + 4 * half + 4, t * P:(t + 1) * P])
            root(stats[:, 6:8])
            for t in range(NT):
                for half in range(2):
                    copy_out(("h_ffnT", t, half), h_ffnT[:, 4 * half:4 * half + 4, t * P:(t + 1) * P])
            for j in range(FFN_TILES // 2):
                if j >= 2:
                    wait_drained(eng, ("fu", j - 2))
                copy_out(("fg", j), ffn_silu[:, j % 2, :, :], func=ACT.Silu)
            root(stats[:, 8:10])

        def second_block_dve(eng, step, link, root_mean, square_sums, spread, modulation):
            v = nc.vector
            for m in (26, 27, 28, 29):
                FIRST_PASS.wait_drained(eng, GROUPS - 1, m)
            for t in range(NT):
                link(v.tensor_tensor(h_lat[:, t, :], x[:, t, :], mod_a[:, 1, :], ALU.mult))
                v.tensor_tensor(h_lat[:, t, :], h_lat[:, t, :], mod_a[:, 0, :], ALU.add).then_inc(s["hlat_ready"], 1)
            src = wait_filled(eng, "dta")[:, 0:256].rearrange("p (c h) -> p c h", c=CHUNKS)
            v.tensor_copy(beta, src[:, :, 32:48]).then_inc(s["beta_raw"], 1)
            step(v.tensor_tensor(raw[:, :, 0:32], src[:, :, 0:32],
                                 gate_bias[:, 0:32].unsqueeze(1).to_broadcast([P, CHUNKS, 32]), ALU.add))
            v.tensor_tensor(raw[:, :, 32:48], src[:, :, 48:64],
                            gate_bias[:, 32:48].unsqueeze(1).to_broadcast([P, CHUNKS, 16]), ALU.add).then_inc(drain_of("dta"), 1)
            wait_drained(eng, "dta")
            v.scalar_tensor_tensor(soft, raw, -1.0, raw, ALU.mult, ALU.max).then_inc(s["abs_ready"], 1)
            eng.wait_ge(s["abs_exp"], 1)
            v.tensor_scalar(soft, soft, 1.0, None, ALU.add).then_inc(s["one_ready"], 1)
            eng.wait_ge(s["one_ln"], 1)
            link(v.scalar_tensor_tensor(soft, raw, 0.0, soft, ALU.max, ALU.add))
            eng.wait_ge(s["rate_ready"], 1)
            link(v.tensor_scalar(decay_rate[:, :], decay_rate[:, :], -1.0, None, ALU.mult))
            for first, n, place_at in ((0, 16, 0), (32, 8, 16)):
                for d in range(2):
                    part = slice(first + n * d, first + n * d + n)
                    step(v.tensor_tensor(log_a[:, :, d, place_at:place_at + n], soft[:, :, part],
                                         decay_rate[:, part].unsqueeze(1).to_broadcast([P, CHUNKS, n]), ALU.mult))
            link(v.tensor_copy(k_root, soft[:, :, 0:8]))
            v.tensor_copy(k_root, soft[:, :, 0:8]).then_inc(s["log_a_ready"], 1)

            def cumulate():
                src = wait_filled(eng, "cum")
                step(v.tensor_copy(cum.rearrange("p d c h -> p (d c h)"), src[:, 0:192]))
                v.tensor_copy(total, src[:, 192:384].rearrange("p (c d h) -> p d c h", c=CHUNKS, d=2)).then_inc(drain_of("cum"), 1)
                wait_drained(eng, "cum")
                v.tensor_tensor(rest, total, cum, ALU.subtract).then_inc(s["cum_ready"], 1)

            eng.wait_ge(s["pads_ready"], 1)

            def convolve(n):
                kind, i = CHANNELS[n]
                if n >= 3:
                    eng.wait_ge(s["channels_ready"], n - 2)
                wait_drained(eng, ("channel", n))
                first = CTX_PAD if kind in LAT_ONLY else 0
                width = CTX_PAD + LAT_PAD - first - TAPS + 1
                dst = conv[:, n % 3, first:first + width]
                for tap_i in range(TAPS):
                    if n < 12:
                        w = cols[:, 54 + 12 * tap_i + n:55 + 12 * tap_i + n]
                    else:
                        j = {"q": 0, "k": 8, "v": 16}[kind] + i
                        w = cols[:, P + 24 * tap_i + j:P + 24 * tap_i + j + 1]
                    src = pad[:, n % 3, first + tap_i:first + tap_i + width]
                    if tap_i == 0:
                        link(v.tensor_scalar(dst, src, w, None, ALU.mult))
                    elif tap_i < TAPS - 1:
                        link(v.scalar_tensor_tensor(dst, src, w, dst, ALU.mult, ALU.add))
                    else:
                        v.scalar_tensor_tensor(dst, src, w, dst, ALU.mult, ALU.add).then_inc(s["conv_ready"], 1)

            def turned(n):
                kind, i = CHANNELS[n]
                if kind in TURNED:
                    key = ("turned", n)
                    dst = {"xs": xs, "bm": bm, "k": k_gdn, "v": v_gdn}[kind][:, :, i * P:(i + 1) * P]
                    v.tensor_copy(dst, wait_filled(eng, key).rearrange("p (c d) -> p c d", c=CHUNKS)).then_inc(drain_of(key), 1)

            for n in range(len(CHANNELS) + 2):
                if n < len(CHANNELS):
                    convolve(n)
                if n == 2:
                    cumulate()
                if n >= 2:
                    turned(n - 2)

            eng.wait_ge(s["cum_exp"], 3)
            eng.wait_ge(s["channels_ready"], len(CHANNELS))
            for n in range(12):
                if CHANNELS[n][0] in TURNED:
                    wait_drained(eng, ("turned", n))
            heads = lambda ap: ap.rearrange("p (h d) -> p h d", d=SSD_P)
            for t in range(NT):
                step(v.tensor_tensor(heads(y_ssd[:, t, :]), heads(xs[:, 2 + t, :]), spread(d_skip[:, :], SSD_HEADS, SSD_P), ALU.mult))
            n = 0
            for d in range(2):
                for ci, c in enumerate(SEQUENCE[d]):
                    t = c - 2
                    before = ("state", d, SEQUENCE[d][ci - 1], 1) if ci else ("y_inner", 0, SEQUENCE[0][3], 1) if d else None
                    if before:
                        wait_filled(eng, before)
                    link(v.tensor_tensor(heads(xdt), heads(xs[:, c, :]),
                                         spread(soft[:, c, 16 * d:16 * d + 16], SSD_HEADS, SSD_P), ALU.mult))
                    v.tensor_tensor(heads(x_rest), heads(xdt), spread(rest[:, d, c, 0:16], SSD_HEADS, SSD_P), ALU.mult)\
                     .then_inc(s["x_rest_ready"], 1)
                    if c >= 2:
                        key = ("cb", d, c)
                        order_of = (upto, since)[d].unsqueeze(1).to_broadcast([P, SSD_G, P])
                        src = wait_filled(eng, key)[:, 0:2 * P].rearrange("p (g c) -> p g c", g=SSD_G)
                        v.tensor_tensor(cb_mask, src, order_of, ALU.mult).then_inc(drain_of(key), 1)
                        for q in range(4):
                            key = ("ssd_rows", d, c, q)
                            src = wait_filled(eng, key).rearrange("p (h c) -> p h c", h=4)
                            v.tensor_tensor(att[:, q, :, :], src, spread(cum[:, d, c, 4 * q:4 * q + 4], 4, P), ALU.subtract)\
                             .then_inc(drain_of(key), 1)
                        for g in range(SSD_G):
                            key = ("y_state", d, c, g)
                            src = heads(wait_filled(eng, key))
                            v.tensor_tensor(heads(y_tmp), src, spread(cum_exp[:, d, c, 8 * g:8 * g + 8], 8, SSD_P), ALU.mult)\
                             .then_inc(drain_of(key), 1)
                            wait_drained(eng, key)
                            part = y_ssd[:, t, g * 512:(g + 1) * 512]
                            link(v.tensor_tensor(part, part, y_tmp, ALU.add))
                        wait_drained(eng, ("cb", d, c))
                        for q in range(4):
                            n += 1
                            eng.wait_ge(s["ssd_decay"], n)
                            v.tensor_tensor(att[:, q, :, :], att[:, q, :, :],
                                            cb_mask[:, q // 2, :].unsqueeze(1).to_broadcast([P, 4, P]), ALU.mult)\
                             .then_inc(s["att_ready"], 1)
                        for g in range(SSD_G):
                            key = ("y_inner", d, c, g)
                            part = y_ssd[:, t, g * 512:(g + 1) * 512]
                            v.tensor_tensor(part, wait_filled(eng, key), part, ALU.add).then_inc(drain_of(key), 1)
                            wait_drained(eng, key)
                    if ci < 3:
                        for g in range(SSD_G):
                            key = ("state", d, c, g)
                            src = wait_filled(eng, key)
                            if ci == 0:
                                if d:
                                    wait_filled(eng, ("y_state", 0, SEQUENCE[0][3], g))
                                v.tensor_copy(ssd_state[:, g, :], src).then_inc(drain_of(key), 1)
                            else:
                                wait_drained(eng, ("state", d, SEQUENCE[d][ci - 1], g))
                                link(v.tensor_tensor(heads(ssd_state[:, g, :]), heads(ssd_state[:, g, :]),
                                                     spread(total[:, d, c, 8 * g:8 * g + 8], 8, SSD_P), ALU.mult))
                                v.tensor_tensor(ssd_state[:, g, :], src, ssd_state[:, g, :], ALU.add).then_inc(drain_of(key), 1)

            wait_filled(eng, ("y_inner", 1, SEQUENCE[1][3], 1))
            v.tensor_tensor(q_square, qT, qT, ALU.mult).then_inc(s["q_square_ready"], 1)
            for n in range(12, len(CHANNELS)):
                if CHANNELS[n][0] in TURNED:
                    wait_drained(eng, ("turned", n))
            of = lambda ap: ap.rearrange("p (h d) -> p h d", d=GDN_DH)
            for c in range(CHUNKS):
                link(v.tensor_tensor(k_square, k_gdn[:, c, :], k_gdn[:, c, :], ALU.mult))
                link(v.tensor_reduce(k_root[:, c, :], of(k_square), AX.X, ALU.add))
            root_mean(k_root, 1.0)
            for c in range(CHUNKS):
                v.tensor_tensor(of(k_gdn[:, c, :]), of(k_gdn[:, c, :]), spread(k_root[:, c, :], 8, GDN_DH), ALU.mult)\
                 .then_inc(s["kn_ready"], 1)
            src = wait_filled(eng, "q_sums")
            v.tensor_copy(q_root.rearrange("p t h -> p (t h)"), src[:, 0:16]).then_inc(drain_of("q_sums"), 1)
            wait_drained(eng, "q_sums")
            root_mean(q_root, 1.0)
            link(v.tensor_scalar(q_root, q_root, GDN_DH ** -0.5, None, ALU.mult))
            eng.wait_ge(s["beta_ready"], 1)
            for d in range(2):
                ins = v.tensor_tensor(beta_cum[:, d, :, :], beta[:, :, 8 * d:8 * d + 8], cum_exp[:, d, :, 16:24], ALU.mult)
                ins.then_inc(s["beta_cum_ready"], 1)

            negated = lambda out, a_in, m: v.scalar_tensor_tensor(out, a_in, -1.0, m.unsqueeze(1).to_broadcast([P, 4, P]),
                                                                  ALU.mult, ALU.mult)

            def four(key):
                return wait_filled(eng, key).rearrange("p (h c) -> p h c", h=4)

            m = lm = 0
            for d in range(2):
                for ci, c in enumerate(SEQUENCE[d]):
                    for h in range(2):
                        key = ("gR", d, c, h)
                        v.tensor_tensor(buf[h][0], four(key), spread(cum[:, d, c, 16 + 4 * h:20 + 4 * h], 4, P), ALU.subtract)\
                         .then_inc(drain_of(key), 1)
                    for h in range(2):
                        key = ("gKK", d, c, h)
                        eng.wait_ge(s["gdn_masked"], m + h + 1)
                        v.tensor_tensor(buf[h][1], four(key), buf[h][1], ALU.mult).then_inc(drain_of(key), 1)
                        if c >= 2:
                            key = ("gQK", d, c, h)
                            eng.wait_ge(s["gdn_maskedT"], lm + h + 1)
                            v.tensor_tensor(buf[h][2], four(key), buf[h][2], ALU.mult).then_inc(drain_of(key), 1)
                    for h in range(2):
                        wait_drained(eng, ("gKK", d, c, h))
                        negated(buf[h][4], buf[h][1], blk16).then_inc(s["n_ready"], 1)
                        wait_drained(eng, ("gAT", d, c, h))
                        negated(buf[h][5], buf[h][3], blk16).then_inc(s["n_ready"], 1)
                    for name in ("gX2", "gX4", "gX8"):
                        for h in range(2):
                            key = (name, d, c, h)
                            v.tensor_tensor(buf[h][7], four(key), buf[h][7], ALU.add).then_inc(drain_of(key), 1)
                    for lev in range(3):
                        for h in range(2):
                            key = ("gY", d, c, h, lev)
                            src = four(key)
                            v.tensor_tensor(buf[h][7], buf[h][7], src, ALU.subtract).then_inc(drain_of(key), 1)
                    if c >= 2:
                        for h in range(2):
                            key = ("go1", d, c, h)
                            v.tensor_tensor(o_tmp[h], four(key), spread(cum_exp[:, d, c, 16 + 4 * h:20 + 4 * h], 4, P), ALU.mult)\
                             .then_inc(drain_of(key), 1)
                    for h in range(2):
                        if c >= 2:
                            key = ("go2", d, c, h)
                            dst = of(o_gdn[:, c - 2, 512 * h:512 * h + 512])
                            wait_drained(eng, ("go1", d, c, h))
                            if d:
                                link(v.tensor_tensor(o_tmp[h], o_tmp[h], dst, ALU.add))
                            v.tensor_tensor(dst, four(key), o_tmp[h], ALU.add).then_inc(drain_of(key), 1)
                        if ci < 3:
                            key, state = ("gS", d, c, h), gdn_state[:, 4 * h:4 * h + 4, :]
                            src = four(key)
                            if ci == 0:
                                v.tensor_copy(state, src).then_inc(drain_of(key), 1)
                            else:
                                link(v.tensor_tensor(state, state, spread(total[:, d, c, 16 + 4 * h:20 + 4 * h], 4, P), ALU.mult))
                                v.tensor_tensor(state, src, state, ALU.add).then_inc(drain_of(key), 1)
                    m += 2
                    lm += 2 * (c >= 2)
            for d in range(2):
                for h in range(2):
                    for c in (2, 3):
                        wait_drained(eng, ("go2", d, c, h))
            link(v.tensor_copy(y_root[:, 0, :], stats[:, 0:2]))
            v.tensor_copy(y_root[:, 1, :], stats[:, 0:2]).then_inc(s["gdn_done"], 1)

            for t in range(NT):
                for i in range(2):
                    wait_drained(eng, ("z", i, t))
                link(v.tensor_tensor(y_ssd[:, t, :], y_ssd[:, t, :], z_silu[:, t, :], ALU.mult))
                for g in range(SSD_G):
                    square_sums(y_ssd[:, t, g * 512:(g + 1) * 512], z_silu[:, t, g * 512:(g + 1) * 512], y_root[:, t, g:g + 1])
            root_mean(y_root, 512)
            eng.wait_ge(s["norm_in"], 16 * 5)
            for t in range(NT):
                for g in range(SSD_G):
                    part = slice(g * 512, (g + 1) * 512)
                    step(v.scalar_tensor_tensor(y_ssd[:, t, part], y_ssd[:, t, part], y_root[:, t, g:g + 1],
                                                norm_rows[:, 0, part], ALU.mult, ALU.mult))
            link(v.tensor_copy(stats[:, 20:21], stats[:, 0:1]))
            for t in range(NT):
                v.tensor_copy(stats[:, 21 + t:22 + t], stats[:, 0:1]).then_inc(s["yo_ready"], 1)
            for t in range(NT):
                rows = of(o_gdn[:, t, :])
                junk = of(z_silu[:, t, :])
                link(v.tensor_tensor(rows, rows, spread(q_root[:, t, :], 8, GDN_DH), ALU.mult))
                link(v.tensor_tensor(junk, rows, rows, ALU.mult))
                link(v.tensor_reduce(o_root[:, t, :], junk, AX.X, ALU.add))
            root_mean(o_root, GDN_DH)
            for t in range(NT):
                rows = of(o_gdn[:, t, :])
                for i in range(2):
                    wait_drained(eng, ("gt", i, t))
                link(v.tensor_tensor(rows, rows, spread(o_root[:, t, :], 8, GDN_DH), ALU.mult))
                link(v.tensor_tensor(rows, rows, gdn_gain[:, :].unsqueeze(1).to_broadcast([P, 8, GDN_DH]), ALU.mult))
                v.tensor_tensor(o_gdn[:, t, :], o_gdn[:, t, :], gate_silu[:, t, :], ALU.mult).then_inc(s["yo_ready"], 1)

            eng.wait_ge(s["rows2_in"], 16)

            def modulate(i):
                modulation(i, 0, mod_rows[:, (i - 4) // 2, (i % 2) * WIDE:(i % 2 + 1) * WIDE], i in (8, 9))

            def residual(key, t, half, gate):
                part, tmp = slice(half * WIDE, (half + 1) * WIDE), ffn_tmp[:, half, :]
                v.tensor_tensor(tmp, wait_filled(eng, (key, t, half)), mod_rows[:, gate, part], ALU.mult)\
                 .then_inc(drain_of((key, t, half)), 1)
                wait_drained(eng, (key, t, half))
                link(v.scalar_tensor_tensor(x[:, t, part], x[:, t, part], ALPHA, tmp, ALU.mult, ALU.add))

            def layer_norm(ss, gain, last=None):
                mean = stats[:, 12:14]
                for t in range(NT):
                    link(v.tensor_reduce(mean[:, t:t + 1], x[:, t, :], AX.X, ALU.add))
                link(v.tensor_scalar(mean, mean, 1.0 / D, None, ALU.mult))
                for t in range(NT):
                    link(v.tensor_scalar(x[:, t, :], x[:, t, :], mean[:, t:t + 1], None, ALU.subtract))
                    square_sums(x[:, t, :], h_ffn[:, t, :], ss[:, t:t + 1])
                root_mean(ss, D, LN_EPS)
                for t in range(NT):
                    link(v.scalar_tensor_tensor(x[:, t, :], x[:, t, :], ss[:, t:t + 1], norm_rows[:, gain, :], ALU.mult, ALU.mult))
                    ins = v.tensor_tensor(x[:, t, :], x[:, t, :], norm_rows[:, gain + 1, :], ALU.add)
                    if last:
                        ins.then_inc(s[last], 1)
                    else:
                        link(ins)

            modulate(4)
            modulate(5)
            for i in (4, 5):
                wait_drained(eng, ("ad", i, 0))
            for t in range(NT):
                for half in range(2):
                    residual("w2", t, half, 0)
            layer_norm(stats[:, 6:8], 1)
            for i in range(6, 10):
                modulate(i)
            for i in range(6, 10):
                wait_drained(eng, ("ad", i, 0))
            for t in range(NT):
                link(v.tensor_tensor(h_ffn[:, t, :], x[:, t, :], mod_rows[:, 2, :], ALU.mult))
                v.tensor_tensor(h_ffn[:, t, :], h_ffn[:, t, :], mod_rows[:, 1, :], ALU.add).then_inc(s["h_ffn_ready"], 1)
            for j in range(FFN_TILES // 2):
                key = ("fu", j)
                wait_drained(eng, ("fg", j))
                v.tensor_tensor(ffn_act[:, 2 * j:2 * j + 2, :], wait_filled(eng, key).rearrange("p (c t) -> p c t", c=2),
                                ffn_silu[:, j % 2, :, :], ALU.mult).then_inc(drain_of(key), 1)
            modulate(10)
            modulate(11)
            for i in (10, 11):
                wait_drained(eng, ("ad", i, 0))
            for t in range(NT):
                for half in range(2):
                    residual("fd", t, half, 3)
            layer_norm(stats[:, 8:10], 3, last="x_ready")

        def second_block_pool(eng, g, link):
            eng.wait_ge(s["ctx_in"], 16)
            for i in range(4):
                wait_drained(eng, ("ad", i, 1))
            for t in range(NT):
                link(g.tensor_tensor(ctx_in[:, t, :], ctx_in[:, t, :], mod_c[:, 1, :], ALU.mult))
                g.tensor_tensor(ctx_in[:, t, :], ctx_in[:, t, :], mod_c[:, 0, :], ALU.add).then_inc(s["hctx_ready"], 1)
            g.memset(pad, 0.0).then_inc(s["pads_ready"], 1)
            n = 0
            for d in range(2):
                for c in SEQUENCE[d][2:]:
                    for q in range(4):
                        wait_drained(eng, ("ssd_rows", d, c, q))
                        g.tensor_scalar(att[:, q, :, :], att[:, q, :, :], 0.0, None, ALU.min).then_inc(s["ssd_clipped"], 1)
            m = lm = 0
            eng.wait_ge(s["beta_cum_ready"], 2)
            by_head = lambda ap: ap.unsqueeze(2).to_broadcast([P, 4, P])
            by_row = lambda ap: ap.unsqueeze(1).to_broadcast([P, 4, P])
            of = lambda ap: ap.rearrange("p (h d) -> p h d", d=GDN_DH)
            for d in range(2):
                for ci, c in enumerate(SEQUENCE[d]):
                    for h in range(2):
                        b = buf[h]
                        wait_drained(eng, ("gR", d, c, h))
                        g.tensor_scalar(b[1], b[0], 0.0, None, ALU.max).then_inc(s["gdn_clipped"], 1)
                        if c >= 2:
                            g.tensor_scalar(b[2], b[0], 0.0, None, ALU.min).then_inc(s["gdn_clippedT"], 1)
                    for h in range(2):
                        b = buf[h]
                        eng.wait_ge(s["gdn_decay"], m + h + 1)
                        link(g.tensor_tensor(b[1], b[1], by_row((below, above)[d]), ALU.mult))
                        g.tensor_tensor(b[1], b[1], by_head(beta[:, c, 8 * d + 4 * h:8 * d + 4 * h + 4]), ALU.mult)\
                         .then_inc(s["gdn_masked"], 1)
                        if c >= 2:
                            eng.wait_ge(s["gdn_decayT"], lm + h + 1)
                            g.tensor_tensor(b[2], b[2], by_row((upto, since)[d]), ALU.mult).then_inc(s["gdn_maskedT"], 1)
                    for h in range(2):
                        b = buf[h]
                        eng.wait_ge(s["n_ready"], 2 * (m + h) + 1)
                        g.tensor_tensor(b[7], b[4], by_row(ident), ALU.add).then_inc(s["one_plus_n"], 1)
                    for lev, mask_of in enumerate(LEVELS):
                        for h in range(2):
                            b = buf[h]
                            wait_filled(eng, ("gX8", d, c, h) if lev == 0 else ("gT", d, c, h, lev - 1))
                            g.tensor_tensor(b[6], b[3], by_row(mask_of), ALU.mult).then_inc(s["level_ready"], 1)
                    for h in range(2):
                        b = buf[h]
                        wait_filled(eng, ("gY", d, c, h, 2))
                        heads = slice(512 * h, 512 * h + 512)
                        link(g.tensor_tensor(b[0], of(k_gdn[:, c, heads]), by_head(beta_cum[:, d, c, 4 * h:4 * h + 4]), ALU.mult))
                        link(g.tensor_tensor(b[1], of(v_gdn[:, c, heads]),
                                             by_head(beta[:, c, 8 * d + 4 * h:8 * d + 4 * h + 4]), ALU.mult))
                        g.tensor_tensor(b[6], of(k_gdn[:, c, heads]), by_head(rest[:, d, c, 16 + 4 * h:20 + 4 * h]), ALU.mult)\
                         .then_inc(s["kv_ready"], 1)
                    m += 2
                    lm += 2 * (c >= 2)
            eng.wait_ge(s["gdn_done"], 1)
            eng.dma_start(mod_rows.rearrange("p i d -> p (i d)"), a["b_ada_2"][0, 2 * D:6 * D].partition_broadcast(P))\
               .then_inc(s["rows2_in"], 16)
            for i, name in enumerate(("norm_w_ssd_2", "ln1_g_2", "ln1_b_2", "ln2_g_2", "ln2_b_2")):
                eng.dma_start(norm_rows[:, i, :], a[name][0].partition_broadcast(P)).then_inc(s["norm_in"], 16)

        def second_block_sp(sp, load):
            for n, name in enumerate(after_experts):
                if n < SLOTS:
                    FIRST_PASS.wait_filled(sp, GROUPS - 1, released_by(GROUP_UNITS - SLOTS + n))
                elif after_experts[n - SLOTS] in unit_passed:
                    sp.wait_ge(passed, unit_passed.index(after_experts[n - SLOTS]) + 1)
                else:
                    sp.wait_ge(filled, unit_use[after_experts[n - SLOTS]])
                load(name)
            sp.wait_ge(s["x_ready"], NT)
            sp.dma_start(out[0].rearrange("(t p) d -> p t d", p=P), x[:, :, :]).then_inc(s["out_done"], 16)
            sp.wait_ge(s["out_done"], 16)

        class Pass:

            def __init__(self, name, filled, drained, landed, arrivals, base):
                self.base = base
                self.filled, self.drained, self.landed, self.arrivals = filled, drained, landed, arrivals
                self.y_full, self.y_ready, self.place_now = (sem(f"{w}_{name}") for w in ("y_full", "y_ready", "place_now"))

            def start(self, n0):
                self.n0 = n0

            def bank(self, m):
                return psum[:, (self.n0 + m) % BANKS, :]

            def wait_filled(self, eng, i, m):
                eng.wait_ge(self.filled, i * MOE_TILES + (self.n0 + m + 1 - self.base))

            def wait_drained(self, eng, i, m):
                n = self.n0 + m
                eng.wait_ge(self.drained[n % BANKS], i * (MOE_TILES // BANKS) + (n // BANKS + 1))

            def drain(self, m):
                return self.drained[(self.n0 + m) % BANKS]

            def wait_free(self, eng, i, m):
                n = self.n0 + m
                eng.wait_ge(self.drained[n % BANKS], i * (MOE_TILES // BANKS) + n // BANKS)

            def slot(self, q):
                return (FIRST_UNIT + q) % SLOTS

            def wait_landed(self, eng, i, q):
                before = sum(1 for r in range(q + 1) if self.slot(r) == self.slot(q))
                eng.wait_ge(self.landed[self.slot(q)],
                            i * (16 * GROUP_UNITS // SLOTS) + (self.arrivals[self.slot(q)] + 16 * before))

        FIRST_PASS = Pass("first", filled, drained, landed, expert_arrivals, 0)
        SECOND_PASS = Pass("second", sem("filled_second"), [sem(f"drained_second{b}") for b in range(BANKS)],
                           [sem(f"landed_second{n}") for n in range(SLOTS)], [0] * SLOTS, BANKS)
        PRELUDE = 3
        SECOND_PASS.start(BANKS + PRELUDE)
        LAST_TILES = range(MOE_TILES - BANKS, MOE_TILES)

        def where_overflow(eng, body):
            eng.wait_ge(s["flag_ready"], 1)
            with eng.If(eng.value_load(overflow[0:1, 0:1], min_val=0, max_val=1) > 0):
                body()
            eng.end_ifs()

        def second_pass_pe(pe):
            ps = SECOND_PASS
            for m in LAST_TILES:
                FIRST_PASS.wait_drained(pe, GROUPS - 1, m)
            for b in range(BANKS):
                pe.sem_inc(ps.drained[b], 1)
            pe.wait_ge(place_second, 1)
            for t in range(NT):
                ps.wait_free(pe, 0, t - PRELUDE)
                for g in range(GROUPS):
                    last = nc.tensor.transpose(ps.bank(t - PRELUDE)[:, g * P:(g + 1) * P], place[:, t, g, :], ident)
                last.then_inc(ps.filled, 1)
            ps.wait_free(pe, 0, -1)
            for g in range(GROUPS):
                for t in range(NT):
                    last = nc.tensor.matmul(ps.bank(-1)[:, 8 * g:8 * g + 8], place[:, t, g, :], r_we[:, t, :],
                                            start=t == 0, stop=t == NT - 1)
            last.then_inc(ps.filled, 1)
            experts_pe(pe, ps)
            for m in LAST_TILES:
                ps.wait_drained(pe, GROUPS - 1, m)

        def second_pass_act(eng):
            ps = SECOND_PASS
            for t in range(NT):
                ps.wait_filled(eng, 0, t - PRELUDE)
                nc.scalar.copy(placeT[:, :, t * P:(t + 1) * P],
                               ps.bank(t - PRELUDE).rearrange("p (g c) -> p g c", g=GROUPS)).then_inc(ps.drain(t - PRELUDE), 1)
            experts_act(eng, ps)

        def second_pass_dve(eng):
            ps, v = SECOND_PASS, nc.vector
            for m in LAST_TILES:
                FIRST_PASS.wait_drained(eng, GROUPS - 1, m)
            v.tensor_scalar(r_rank[:, 0:8], r_rank[:, 0:8], float(P), None, ALU.subtract).then_inc(rank_second, 1)
            eng.wait_ge(rank_second, 1)
            for t in range(NT):
                for g in range(GROUPS):
                    last = v.tensor_scalar(place[:, t, g, :], slot_row, r_rank[:, 4 * t + g:4 * t + g + 1],
                                           r_hot[:, t, g:g + 1], ALU.is_equal, ALU.mult)
            last.then_inc(place_second, 1)
            ps.wait_filled(eng, 0, -1)
            v.tensor_copy(w_slot.rearrange("p g e -> p (g e)"), ps.bank(-1)[:, 0:32]).then_inc(ps.drain(-1), 1)
            for m in (-PRELUDE, 1 - PRELUDE, -1):
                ps.wait_drained(eng, 0, m)
            experts_dve(eng, ps)
            for m in LAST_TILES:
                ps.wait_drained(eng, GROUPS - 1, m)

        def second_pass_sp(sp):
            for q in range(SLOTS):
                FIRST_PASS.wait_filled(sp, GROUPS - 1, released_by(GROUP_UNITS - SLOTS + q))
            first_loads(sp, SECOND_PASS)
            experts_sp(sp, SECOND_PASS)
            for q in range(SLOTS):
                SECOND_PASS.wait_filled(sp, GROUPS - 1, released_by(GROUP_UNITS - SLOTS + q))

        def first_loads(sp, ps, ready=lambda q: None):
            for q in range(SLOTS):
                kind, e = expert_units[q]
                ready(q)
                src = (a["w_gate"] if kind == "g" else a["w_up"])[0, e]
                sp.dma_start(expert_slot(ps, kind, e), src.rearrange("(k p) n -> p k n", p=P)).then_inc(ps.landed[ps.slot(q)], 16)

        rank_second, place_second = sem("rank_second"), sem("place_second")

        def expert_slot(ps, kind, e):
            return ring[:, ps.slot(expert_units.index((kind, e))), :].rearrange("p (k n) -> p k n", k=4 if kind == "d" else 8)

        def experts_pe(pe, ps):
            with pe.Fori(0, GROUPS) as i:
                for half in range(2):
                    ps.wait_free(pe, i, half)
                    dst = ps.bank(half)
                    for j in range(4):
                        k = 4 * half + j
                        for t in range(NT):
                            last = nc.tensor.matmul(dst[:, j * P:(j + 1) * P], h2[:, t, k * P:(k + 1) * P],
                                                    place[:, t, bass.ds(i, 1), :].rearrange("p a c -> p (a c)"),
                                                    start=t == 0, stop=t == NT - 1)
                    last.then_inc(ps.filled, 1)
                for half in range(2):
                    ps.wait_drained(pe, i, half)

                def wide(kind, e):
                    m = TILE[kind] + 3 * e
                    ps.wait_landed(pe, i, expert_units.index((kind, e)))
                    ps.wait_free(pe, i, m)
                    w, dst = expert_slot(ps, kind, e), ps.bank(m)
                    for k in range(KD):
                        last = nc.tensor.matmul(dst, hcT[:, k, :], w[:, k, :], start=k == 0, stop=k == KD - 1)
                    last.then_inc(ps.filled, 1)

                def down(e):
                    ps.wait_landed(pe, i, expert_units.index(("d", e)))
                    ps.wait_drained(pe, i, TILE["t"] + 3 * e)
                    w = expert_slot(ps, "d", e)
                    for half in range(2):
                        for k in range(FF_TILES):
                            last = nc.tensor.matmul(psum[:, BANKS + half, :], actT[:, e % 2, k, :],
                                                    w[:, k, half * WIDE:(half + 1) * WIDE],
                                                    start=e == 0 and k == 0, stop=e == PER_GROUP - 1 and k == FF_TILES - 1)
                    return last

                for e in range(PER_GROUP):
                    wide("g", e)
                    wide("u", e)
                    if e >= 1:
                        down(e - 1)
                    m = TILE["t"] + 3 * e
                    ps.wait_drained(pe, i, TILE["u"] + 3 * e)
                    ps.wait_free(pe, i, m)
                    for k in range(FF_TILES):
                        last = nc.tensor.transpose(ps.bank(m)[:, k * P:(k + 1) * P], act[:, e % 2, k * P:(k + 1) * P], ident)
                    last.then_inc(ps.filled, 1)
                down(PER_GROUP - 1).then_inc(ps.y_full, 1)
                pe.wait_ge(ps.place_now, i + 1)
                pe.wait_ge(ps.y_ready, i * 2 + 2)
                for t in range(NT):
                    for half in range(2):
                        m = 2 + 3 * PER_GROUP + 2 * t + half
                        ps.wait_free(pe, i, m)
                        nc.tensor.matmul(ps.bank(m), place_now[:, t * P:(t + 1) * P], y_group[:, half * WIDE:(half + 1) * WIDE],
                                         start=True, stop=True).then_inc(ps.filled, 1)

        def experts_act(eng, ps):
            with eng.Fori(0, GROUPS) as i:
                ps.wait_filled(eng, i, 0)
                nc.scalar.copy(hcT[:, 0:4, :].rearrange("p k n -> p (k n)"), ps.bank(0)).then_inc(ps.drain(0), 1)
                for e in range(PER_GROUP):
                    m = TILE["g"] + 3 * e
                    ps.wait_filled(eng, i, m)
                    nc.scalar.activation(silu_g[:, e % 2, :], ps.bank(m), ACT.Silu).then_inc(ps.drain(m), 1)
                    m = TILE["t"] + 3 * e
                    ps.wait_filled(eng, i, m)
                    nc.scalar.copy(actT[:, e % 2, :, :].rearrange("p k n -> p (k n)"), ps.bank(m)).then_inc(ps.drain(m), 1)
                eng.wait_ge(ps.y_full, i + 1)
                nc.scalar.copy(y_group[:, 0:WIDE], psum[:, BANKS, :]).then_inc(ps.y_ready, 1)

        def experts_dve(eng, ps):
            with eng.Fori(0, GROUPS) as i:
                ps.wait_filled(eng, i, 1)
                nc.vector.tensor_copy(hcT[:, 4:8, :].rearrange("p k n -> p (k n)"), ps.bank(1)).then_inc(ps.drain(1), 1)
                nc.vector.tensor_copy(place_now, placeT[:, bass.ds(i, 1), :].rearrange("p a c -> p (a c)"))\
                  .then_inc(ps.place_now, 1)
                for e in range(PER_GROUP):
                    m = TILE["u"] + 3 * e
                    ps.wait_drained(eng, i, TILE["g"] + 3 * e)
                    ps.wait_filled(eng, i, m)
                    nc.vector.scalar_tensor_tensor(
                        out=act[:, e % 2, :], in0=silu_g[:, e % 2, :],
                        scalar=w_slot[:, bass.ds(i, 1), e:e + 1].rearrange("p a c -> p (a c)"),
                        in1=ps.bank(m), op0=ALU.mult, op1=ALU.mult).then_inc(ps.drain(m), 1)
                eng.wait_ge(ps.y_full, i + 1)
                nc.vector.tensor_copy(y_group[:, WIDE:D], psum[:, BANKS + 1, :]).then_inc(ps.y_ready, 1)
                for t in range(NT):
                    for half in range(2):
                        m = 2 + 3 * PER_GROUP + 2 * t + half
                        ps.wait_filled(eng, i, m)
                        part = x[:, t, half * WIDE:(half + 1) * WIDE]
                        nc.vector.tensor_tensor(part, ps.bank(m), part, ALU.add).then_inc(ps.drain(m), 1)

        def experts_sp(sp, ps):
            tensors = {"g": a["w_gate"], "u": a["w_up"], "d": a["w_down"]}

            def load(group, q):
                kind, e = expert_units[q]
                src = tensors[kind][0, bass.ds(group * PER_GROUP + e, 1), :, :].rearrange("e (k p) n -> p (e k) n", p=P)
                sp.dma_start(expert_slot(ps, kind, e), src).then_inc(ps.landed[ps.slot(q)], 16)

            def load_rest(group):
                for q in range(SLOTS, GROUP_UNITS):
                    ps.wait_filled(sp, group, released_by(q - SLOTS))
                    load(group, q)

            with sp.Fori(0, GROUPS - 1) as i:
                load_rest(i)
                for q in range(SLOTS):
                    ps.wait_filled(sp, i, released_by(GROUP_UNITS - SLOTS + q))
                    load(i + 1, q)
            load_rest(GROUPS - 1)

        @block.tensor
        def _(pe):
            def open_tile(key):
                n = order.number(key)
                if n >= BANKS:
                    pe.wait_ge(drained[n % BANKS], n // BANKS)
                return psum[:, n % BANKS, :]

            def unit(name):
                n = unit_number[name]
                pe.wait_ge(landed[n % SLOTS], landed_by[name])
                return unit_views(name, n % SLOTS)

            def used(name):
                unit_use[name] = order.count

            def transposes(key, sources):
                t = open_tile(key)
                for j, src in enumerate(sources):
                    rows, width = src.shape
                    last = nc.tensor.transpose(t[0:width, j * P:j * P + rows], src, ident[0:rows, 0:rows])
                last.then_inc(filled, 1)

            def product(dst, lhs, rhs, count, first=True, final=True):
                for k in range(count):
                    last = nc.tensor.matmul(dst, lhs(k), rhs(k), start=first and k == 0, stop=final and k == count - 1)
                return last

            def tokens_by_weights(key, xT, t, w, width=WIDE):
                dst = open_tile(key)
                product(dst[:, 0:width], lambda k: xT[:, k, t * P:(t + 1) * P], lambda k: w[:, k, 0:width],
                        w.shape[1]).then_inc(filled, 1)

            pe.wait_ge(s["consts_ready"], 1)
            pe.wait_ge(s["rows_in"], 16 * 9)
            t = open_tile("cols")
            nc.tensor.transpose(t[:, 0:ROWS_A], rows_a[0:ROWS_A, 0, :], ident[0:ROWS_A, 0:ROWS_A])
            nc.tensor.transpose(t[:, P:2 * P], rows_a[:, 1, :], ident).then_inc(filled, 1)

            for t in range(NT):
                pe.wait_ge(s["xn_ready"], t + 1)
                for half in range(2):
                    transposes(("hT", t, half), [xn[:, t, (4 * half + j) * P:(4 * half + j + 1) * P] for j in range(4)])
            for t in range(NT):
                pe.wait_ge(s["mn_ready"], t + 1)
                for half in range(2):
                    transposes(("mT", t, half), [mem[:, t, (4 * half + j) * P:(4 * half + j + 1) * P] for j in range(4)])

            for t in range(NT):
                for half in range(2):
                    wait_drained(pe, ("hT", t, half))
            for i in (0, 1, 2, 3):
                w, = unit(f"in{i}")
                for t in range(NT):
                    tokens_by_weights(("in", i, t), hT, t, w)
                used(f"in{i}")

            def channels_by_tokens(key, w, first):
                dst = open_tile(key)
                for c in range(2):
                    last = product(dst[:, c * SEQ:(c + 1) * SEQ],
                                   lambda k: w[:, k, first + c * P:first + (c + 1) * P], lambda k: hT[:, k, :], KD)
                last.then_inc(filled, 1)

            w, = unit("in4")
            dst = open_tile("v_rest")
            for t in range(NT):
                last = product(dst[:, t * SEQ:(t + 1) * SEQ], lambda k: hT[:, k, t * P:(t + 1) * P],
                               lambda k: w[:, k, 0:256], KD)
            last.then_inc(filled, 1)
            channels_by_tokens(("cv", 0), w, 256)
            used("in4")
            w, = unit("in9")
            for t in range(NT):
                tokens_by_weights(("in", 9, t), hT, t, w)
            used("in9")
            for t in range(NT):
                for half in range(2):
                    wait_drained(pe, ("mT", t, half))
            for i in range(2):
                w, = unit(f"mk{i}")
                for t in range(NT):
                    tokens_by_weights(("mk", i, t), mT, t, w)
                used(f"mk{i}")

            def conv_piece(i):
                name = f"in{5 + (i - 1) // 2}"
                if (i - 1) % 2 == 0:
                    conv_piece.w, = unit(name)
                channels_by_tokens(("cv", i), conv_piece.w, ((i - 1) % 2) * 256)
                if (i - 1) % 2 == 1:
                    used(name)

            def gate_piece(i):
                name = f"in{10 + i // 2}"
                if i % 2 == 0:
                    gate_piece.w, = unit(name)
                tokens_by_weights(("gate", i // 2, i % 2), hT, i % 2, gate_piece.w)
                if i % 2 == 1:
                    used(name)

            conv_piece(1)
            conv_piece(2)
            conv_piece(3)
            conv_piece(4)

            for t in range(NT):
                pe.wait_ge(s["qk_ready"], t + 1)
                for j in range(3):
                    transposes(("qkT", t, j), [qk[:, t, 8 * j + 2 * i:8 * j + 2 * i + 2, :].rearrange("p h d -> p (h d)")
                                               for i in range(4)])
            for t in range(NT):
                pe.wait_ge(s["qk_ready"], NT + t + 1)
                for j in range(2):
                    transposes(("qk_memT", t, j), [qk_mem[:, t, 4 * j + i, :] for i in range(4)])

            def scores(j):
                kind, t, pair = j // 4, j // 2 % 2, j % 2
                if j == 0:
                    for tt in range(NT):
                        for jj in range(3):
                            wait_drained(pe, ("qkT", tt, jj))
                if j == 12:
                    for tt in range(NT):
                        for jj in range(2):
                            wait_drained(pe, ("qk_memT", tt, jj))
                dst = open_tile(("scores", j))
                for i in range(2):
                    if kind < 3:
                        head = 4 * kind + pair + 2 * i
                        part = slice(DH * (head % 2), DH * (head % 2) + DH)
                        q, k = qkT[part, head // 2, t * P:(t + 1) * P], qkT[part, 6 + head // 2, :]
                    else:
                        q, k = qk_memT[:, pair + 2 * i, t * P:(t + 1) * P], qk_memT[:, 4 + pair + 2 * i, :]
                    last = nc.tensor.matmul(dst[:, i * SEQ:(i + 1) * SEQ], q, k, start=True, stop=True)
                last.then_inc(filled, 1)

            def turn_probs(j):
                pe.wait_ge(s["probs_ready"], 2 * (j + 1))
                transposes(("PT", j), [S[:, j % 3, i, k * P:(k + 1) * P] for i in range(2) for k in range(NT)])

            def values(j):
                kind, pair = j // 4, j % 2
                wait_drained(pe, ("PT", j))
                if j == 0:
                    wait_drained(pe, ("in", 3, 0))
                    wait_drained(pe, ("in", 3, 1))
                    wait_drained(pe, "v_rest")
                if j == 12:
                    wait_drained(pe, ("mk", 1, 0))
                    wait_drained(pe, ("mk", 1, 1))
                dst = open_tile(("values", j))
                width = DH if kind < 3 else MEM_DH
                for i in range(2):
                    head = (4 * kind if kind < 3 else 0) + pair + 2 * i
                    v = v_dil if kind < 3 else v_mem
                    last = product(dst[:, i * width:(i + 1) * width], lambda k: PT[:, j % 3, 2 * i + k, :],
                                   lambda k: v[:, k, head * width:(head + 1) * width], NT)
                last.then_inc(filled, 1)

            pieces = {j: [(conv_piece, 5 + j)] for j in range(4)}
            pieces |= {j: [(gate_piece, j - 4)] for j in range(4, 16)}
            for j in range(18):
                if j < 16:
                    scores(j)
                    for piece, i in pieces[j]:
                        piece(i)
                if 1 <= j <= 16:
                    turn_probs(j - 1)
                if j >= 2:
                    values(j - 2)

            pe.wait_ge(s["o_ready"], NT)
            transposes("o_dilT", [o_dil[:, t, 0, k * P:(k + 1) * P] for t in range(NT) for k in range(2)])
            for t in range(NT):
                wait_drained(pe, ("values", 15))
                transposes(("o_memT", t), [o_mem[:, t, k * P:(k + 1) * P] for k in range(4)])

            def project(branch, names, lhs, count):
                views = [unit(n)[0] for n in names]
                weights = [(v, k) for v in views for k in range(v.shape[1])]
                for t in range(NT):
                    for half in range(2):
                        dst = open_tile(("proj", branch, t, half))
                        product(dst, lambda k: lhs[:, k, t * P:(t + 1) * P],
                                lambda k: weights[k][0][:, weights[k][1], half * WIDE:(half + 1) * WIDE],
                                count).then_inc(filled, 1)
                for n in names:
                    used(n)

            wait_drained(pe, "o_dilT")
            project(0, ["pa"], oT, 2)
            pe.wait_ge(s["z_ready"], CONV_TILES)
            project(1, ["pc0", "pc1"], cb, 6)
            for t in range(NT):
                wait_drained(pe, ("o_memT", t))
            project(2, ["pm"], oT[:, 2:6, :], 4)

            for t in range(NT):
                pe.wait_ge(s["merged_ready"], 2 * (t + 1))
                for half in range(2):
                    transposes(("mergedT", t, half),
                               [merged[:, t, (4 * half + j) * P:(4 * half + j + 1) * P] for j in range(4)])
            for t in range(NT):
                for half in range(2):
                    wait_drained(pe, ("mergedT", t, half))
            for i in range(2):
                w, = unit(f"wo{i}")
                for t in range(NT):
                    tokens_by_weights(("wo", i, t), mergedT, t, w)
                used(f"wo{i}")

            def modulation(i, context):
                w, = unit(f"ad{i}")
                for c in ((c_wide, c_ctx_wide) if context else (c_wide,)):
                    dst = open_tile(("ad", i, 0 if c is c_wide else 1))
                    product(dst, lambda k: c[:, k, :], lambda k: w[:, k, :], KD).then_inc(filled, 1)
                used(f"ad{i}")

            pe.wait_ge(s["c_wide_ready"], 2)
            for i in range(4):
                modulation(i, True)

            for t in range(NT):
                pe.wait_ge(s["h2_ready"], t + 1)
                for half in range(2):
                    transposes(("h2T", t, half), [h2[:, t, (4 * half + j) * P:(4 * half + j + 1) * P] for j in range(4)])
            for t in range(NT):
                for half in range(2):
                    wait_drained(pe, ("h2T", t, half))
            pe.wait_ge(s["small_in"], 16 * N_SMALL)
            dst = open_tile("router")
            for t in range(NT):
                last = product(dst[:, t * 36:(t + 1) * 36], lambda k: h2T[:, k, t * P:(t + 1) * P],
                               lambda k: router_w[:, k, :], KD)
            last.then_inc(filled, 1)
            pe.wait_ge(s["hot_ready"], 1)
            dst = open_tile("rank")
            nc.tensor.matmul(dst[:, 0:4], above, r_hot[:, 0, :], start=True, stop=True)
            nc.tensor.matmul(dst[:, 4:8], ones, r_hot[:, 0, :], start=True, stop=False)
            nc.tensor.matmul(dst[:, 4:8], above, r_hot[:, 1, :], start=False, stop=True)
            nc.tensor.matmul(dst[:, 8:12], ones, r_hot[:, 0, :], start=True, stop=False)
            nc.tensor.matmul(dst[:, 8:12], ones, r_hot[:, 1, :], start=False, stop=True).then_inc(filled, 1)
            pe.wait_ge(s["place_ready"], 1)
            for t in range(NT):
                transposes(("placeT", t), [place[:, t, g, :] for g in range(GROUPS)])
            dst = open_tile("w_slot")
            for g in range(GROUPS):
                last = product(dst[:, 8 * g:8 * g + 8], lambda t: place[:, t, g, :], lambda t: r_we[:, t, :], NT)
            last.then_inc(filled, 1)
            for t in range(NT):
                wait_drained(pe, ("placeT", t))
            FIRST_PASS.start(order.count)
            experts_pe(pe, FIRST_PASS)
            where_overflow(pe, lambda: second_pass_pe(pe))
            order.count += GROUPS * MOE_TILES
            second_block_pe(pe, open_tile, unit, used, transposes, product, tokens_by_weights, modulation)

        @block.scalar
        def _(act_eng):
            eng = act_eng
            roots = [0]

            def root(ap):
                roots[0] += 1
                eng.wait_ge(s["root_asked"], roots[0])
                nc.scalar.activation(ap, ap, ACT.Sqrt).then_inc(s["root_done"], 1)

            def copy_out(key, dst, cols=WIDE, func=ACT.Copy):
                t = wait_filled(eng, key)
                src = t[:, 0:cols]
                if len(dst.shape) == 3:
                    src = src.rearrange("p (a b) -> p a b", a=dst.shape[1])
                nc.scalar.activation(dst, src, func).then_inc(drain_of(key), 1)

            eng.dma_start(x[:, :, :], a["x"][0].rearrange("(t p) d -> p t d", p=P)).then_inc(s["x_in"], 16)
            eng.dma_start(mem, a["mem"][0].rearrange("(t p) d -> p t d", p=P)).then_inc(s["mem_in"], 16)
            for table, which in ((COLS_A, 0), (COLS_B, 1)):
                for name, (first, count) in table.items():
                    src = a[name]
                    flat = {1: "(a p) -> a p", 2: "x (a p) -> (x a) p", 3: "x y (a p) -> (x y a) p"}[len(src.shape)]
                    eng.dma_start(rows_a[first:first + count, which, :], src.rearrange(flat, p=P)).then_inc(s["rows_in"], 16)
            for dst, src in small_loads:
                eng.dma_start(dst, src).then_inc(s["small_in"], 16)

            root(stats[:, 0:2])
            root(stats[:, 2:4])
            eng.wait_ge(s["angles_ready"], 1)
            nc.scalar.activation(rope[:, 7, :, :, :], rope[:, 6, :, :, :], ACT.Sin).then_inc(s["tables_ready"], 1)
            for i in range(3):
                for t in range(NT):
                    copy_out(("in", i, t), qk[:, t, 8 * i:8 * i + 8, :])
            for t in range(NT):
                copy_out(("in", 3, t), v_dil[:, t, 0:WIDE])
            copy_out("v_rest", v_dil[:, :, WIDE:768])
            eng.wait_ge(s["zeros_ready"], 1)
            copy_out(("cv", 0), u_conv[:, 0:2, 1:SEQ + 1])
            for t in range(NT):
                copy_out(("in", 9, t), qk_mem[:, t, 0:4, :])
            for t in range(NT):
                copy_out(("mk", 0, t), qk_mem[:, t, 4:8, :])
            for t in range(NT):
                copy_out(("mk", 1, t), v_mem[:, t, :])

            def conv_piece(i):
                if i < 3:
                    copy_out(("cv", i), u_conv[:, 2 * i:2 * i + 2, 1:SEQ + 1])
                elif i < 6:
                    copy_out(("cv", i), cb[:, 2 * i - 6:2 * i - 4, :])

            def gate_piece(i):
                copy_out(("gate", i // 2, i % 2), gates[:, i % 2, (i // 2) * WIDE:(i // 2 + 1) * WIDE], func=ACT.Sigmoid)

            for i in (1, 2, 3, 4):
                conv_piece(i)
            for i in range(2 * NT):
                root(squares_root[:, i % 2, 0:24] if i < NT else squares_root[:, i % 2, 0:8])
            for t in range(NT):
                for j in range(3):
                    copy_out(("qkT", t, j), qkT[:, 4 * j:4 * j + 4, t * P:(t + 1) * P])
            for t in range(NT):
                for j in range(2):
                    copy_out(("qk_memT", t, j), qk_memT[:, 4 * j:4 * j + 4, t * P:(t + 1) * P])

            def probabilities(j):
                kind, t, pair = j // 4, j // 2 % 2, j % 2
                eng.wait_ge(s["logits_ready"], j + 1)
                for i in range(2):
                    h = pair + 2 * i
                    nc.scalar.activation(S[:, j % 3, i, :], S[:, j % 3, i, :], ACT.Exp,
                                         bias=neg_max[:, t, kind, h:h + 1],
                                         accum_out=den[:, t, kind, h:h + 1]).then_inc(s["probs_ready"], 1)

            pieces = {j: [(conv_piece, 5 + j)] for j in range(4)}
            pieces |= {j: [(gate_piece, j - 4)] for j in range(4, 16)}
            for j in range(18):
                if j < 16:
                    for piece, i in pieces[j]:
                        piece(i)
                    probabilities(j)
                if 1 <= j <= 16:
                    copy_out(("PT", j - 1), PT[:, (j - 1) % 3, :, :])
            for t in range(NT):
                eng.wait_ge(s["peaks_ready"], t + 1)
                nc.scalar.activation(combine[:, t, :, :], combine[:, t, :, :], ACT.Exp).then_inc(s["peaks_exp"], 1)
            t = wait_filled(eng, "o_dilT")
            for tt in range(NT):
                last = nc.scalar.copy(oT[:, 0:2, tt * P:(tt + 1) * P],
                                      t[:, tt * 256:(tt + 1) * 256].rearrange("p (k c) -> p k c", k=2))
            last.then_inc(drain_of("o_dilT"), 1)
            for t in range(NT):
                copy_out(("o_memT", t), oT[:, 2:6, t * P:(t + 1) * P])
            for t in range(NT):
                for half in range(2):
                    copy_out(("mergedT", t, half), mergedT[:, 4 * half:4 * half + 4, t * P:(t + 1) * P])
            wait_drained(eng, "cols")
            nc.scalar.activation(r_col[:, 0:8, 0], cols[:, P + 120:P + 128], ACT.Silu).then_inc(s["c_silu"], 1)
            nc.scalar.activation(r_col[:, 0:8, 1], cols[:, 114:122], ACT.Silu).then_inc(s["c_silu"], 1)
            root(stats[:, 4:6])
            for t in range(NT):
                for half in range(2):
                    copy_out(("h2T", t, half), h2T[:, 4 * half:4 * half + 4, t * P:(t + 1) * P])
            eng.wait_ge(s["gate_logits"], 1)
            nc.scalar.activation(r_tmp[:, 0, :, 0:4], r_tmp[:, 0, :, 0:4], ACT.Exp).then_inc(s["gate_exp"], 1)
            eng.wait_ge(s["gate_logits"], 2)
            nc.scalar.activation(r_col[:, 6, :], r_col[:, 6, :], ACT.Exp).then_inc(s["gate_exp"], 1)
            for t in range(NT):
                copy_out(("placeT", t), placeT[:, :, t * P:(t + 1) * P])
            experts_act(eng, FIRST_PASS)
            where_overflow(eng, lambda: second_pass_act(eng))
            second_block_act(eng, root, copy_out)

        @block.vector
        def _(eng):
            steps, roots = [0], [0]
            v = nc.vector

            def step(ins):
                steps[0] += 1
                ins.then_inc(s["dve_step"], 1)

            def link(ins):
                step(ins)
                eng.wait_ge(s["dve_step"], steps[0])

            def root_mean(ss, n, eps=EPS):
                roots[0] += 1
                v.tensor_scalar(ss, ss, 1.0 / n, eps, ALU.mult, ALU.add).then_inc(s["root_asked"], 1)
                eng.wait_ge(s["root_done"], roots[0])
                link(v.reciprocal(ss, ss))

            def square_sums(src, junk, ss):
                link(v.tensor_tensor_reduce(junk, src, src, 1.0, 0.0, ALU.mult, ALU.add, ss))

            def spread(ap, *shape):
                return ap.unsqueeze(len(ap.shape)).to_broadcast([P, *shape])

            eng.wait_ge(s["x_in"], 16)
            for t in range(NT):
                square_sums(x[:, t, :], xn[:, t, :], stats[:, t:t + 1])
            root_mean(stats[:, 0:2], D)
            for t in range(NT):
                v.tensor_scalar(xn[:, t, :], x[:, t, :], stats[:, t:t + 1], None, ALU.mult).then_inc(s["xn_ready"], 1)
            t = wait_filled(eng, "cols")
            step(v.tensor_copy(cols[:, 0:ROWS_A], t[:, 0:ROWS_A]))
            v.tensor_copy(cols[:, P:2 * P], t[:, P:2 * P]).then_inc(drain_of("cols"), 1)
            wait_drained(eng, "cols")

            def columns_out(key, dst, gain):
                t = wait_filled(eng, key)
                v.tensor_tensor(dst, t.rearrange("p (k c) -> p k c", k=4), spread(gain, 4, P), ALU.mult)\
                 .then_inc(drain_of(key), 1)

            for t in range(NT):
                for half in range(2):
                    columns_out(("hT", t, half), hT[:, 4 * half:4 * half + 4, t * P:(t + 1) * P],
                                cols[:, 4 * half:4 * half + 4])
            eng.wait_ge(s["mem_in"], 16)
            for t in range(NT):
                square_sums(mem[:, t, :], merged[:, t, :], stats[:, 2 + t:3 + t])
            root_mean(stats[:, 2:4], D)
            for t in range(NT):
                v.tensor_scalar(mem[:, t, :], mem[:, t, :], stats[:, 2 + t:3 + t], None, ALU.mult).then_inc(s["mn_ready"], 1)
            for t in range(NT):
                for half in range(2):
                    columns_out(("mT", t, half), mT[:, 4 * half:4 * half + 4, t * P:(t + 1) * P],
                                cols[:, 8 + 4 * half:12 + 4 * half])

            eng.wait_ge(s["small_in"], 16 * N_SMALL)
            eng.wait_ge(s["consts_ready"], 1)
            angle, turns, reduced = rope[:, 0, :, :, :], rope[:, 1, :, :, :], rope[:, 2, :, :, :]
            link(v.tensor_copy(rope[:, 3, 0, :, 0], pos_i[:, :]))
            for i in range(2):
                step(v.tensor_tensor(angle[:, i, :, :], spread(rope[:, 3, 0, :, 0], NT, ROT),
                                     inv_freq[:, :].unsqueeze(1).to_broadcast([P, NT, ROT]), ALU.mult))
            eng.wait_ge(s["dve_step"], steps[0])
            step(v.tensor_scalar(turns[:, 0, :, :], angle[:, 0, :, :], 1.0 / (2 * np.pi), 0.25, ALU.mult, ALU.add))
            link(v.tensor_scalar(turns[:, 1, :, :], angle[:, 1, :, :], 1.0 / (2 * np.pi), None, ALU.mult))
            link(v.tensor_scalar(turns, turns, ROUND, None, ALU.add))
            link(v.tensor_scalar(turns, turns, ROUND, None, ALU.subtract))
            link(v.scalar_tensor_tensor(reduced, turns, -TURN[0], angle, ALU.mult, ALU.add))
            link(v.scalar_tensor_tensor(reduced, turns, -TURN[1], reduced, ALU.mult, ALU.add))
            link(v.scalar_tensor_tensor(reduced, turns, -TURN[2], reduced, ALU.mult, ALU.add))
            link(v.tensor_scalar(reduced[:, 0, :, :], reduced[:, 0, :, :], np.pi / 2, None, ALU.add))
            v.tensor_scalar(rope[:, 6, :, :, :], reduced, 3.1415925, -3.1415925, ALU.min, ALU.max).then_inc(s["angles_ready"], 1)
            cos, sin = rope[:, 7, 0, :, :], rope[:, 7, 1, :, :]
            for i, dil in ((2, 4), (3, 16)):
                link(v.tensor_scalar(mask_i, distance, dil - 1, None, ALU.bitwise_and))
                link(v.tensor_scalar(mask[:, i, :], mask_i, 0.0, FAR, ALU.not_equal, ALU.mult))

            eng.wait_ge(s["tables_ready"], 1)
            for t in range(NT):
                for i in range(3):
                    wait_drained(eng, ("in", i, t))
                if t:
                    eng.wait_ge(s["qk_ready"], t)
                heads, ss = qk[:, t, :, :], squares_root[:, t, 0:24]
                link(v.tensor_tensor(squares, heads, heads, ALU.mult))
                link(v.tensor_reduce(ss, squares, AX.X, ALU.add))
                root_mean(ss, DH)
                link(v.tensor_tensor(heads, heads, spread(ss, 24, DH), ALU.mult))
                for i in range(2):
                    step(v.tensor_tensor(heads[:, 12 * i:12 * i + 12, :], heads[:, 12 * i:12 * i + 12, :],
                                         head_gain[:, i, :].unsqueeze(1).to_broadcast([P, 12, DH]), ALU.mult))
                eng.wait_ge(s["dve_step"], steps[0])
                x1, x2 = heads[:, :, 0:ROT], heads[:, :, ROT:2 * ROT]
                tmp = squares[:, :, 0:4 * ROT].rearrange("p h (f r) -> p f h r", f=4)
                c = cos[:, t, :].unsqueeze(1).to_broadcast([P, 24, ROT])
                sn = sin[:, t, :].unsqueeze(1).to_broadcast([P, 24, ROT])
                for f, (one, two) in enumerate(((x1, c), (x2, sn), (x2, c), (x1, sn))):
                    step(v.tensor_tensor(tmp[:, f, :, :], one, two, ALU.mult))
                eng.wait_ge(s["dve_step"], steps[0])
                step(v.tensor_tensor(x1, tmp[:, 0, :, :], tmp[:, 1, :, :], ALU.subtract))
                eng.wait_ge(s["dve_step"], steps[0])
                v.tensor_tensor(x2, tmp[:, 2, :, :], tmp[:, 3, :, :], ALU.add).then_inc(s["qk_ready"], 1)
            for t in range(NT):
                wait_drained(eng, ("in", 9, t))
                wait_drained(eng, ("mk", 0, t))
                eng.wait_ge(s["qk_ready"], NT + t)
                heads, ss = qk_mem[:, t, :, :], squares_root[:, t, 0:8]
                sq = squares.rearrange("p h d -> p (h d)")[:, 0:1024].rearrange("p (h d) -> p h d", h=8)
                link(v.tensor_tensor(sq, heads, heads, ALU.mult))
                link(v.tensor_reduce(ss, sq, AX.X, ALU.add))
                root_mean(ss, MEM_DH)
                link(v.tensor_tensor(heads, heads, spread(ss, 8, MEM_DH), ALU.mult))
                step(v.tensor_tensor(heads[:, 0:4, :], heads[:, 0:4, :],
                                     mem_gain[:, 0, :].unsqueeze(1).to_broadcast([P, 4, MEM_DH]), ALU.mult))
                eng.wait_ge(s["dve_step"], steps[0])
                v.tensor_tensor(heads[:, 4:8, :], heads[:, 4:8, :],
                                mem_gain[:, 1, :].unsqueeze(1).to_broadcast([P, 4, MEM_DH]), ALU.mult).then_inc(s["qk_ready"], 1)

            def logits(j):
                kind, t, pair = j // 4, j // 2 % 2, j % 2
                buf, key = S[:, j % 3, :, :], ("scores", j)
                if j >= 3:
                    wait_filled(eng, ("PT", j - 3))
                src = wait_filled(eng, key).rearrange("p (h k) -> p h k", h=2)
                if kind < 3:
                    rows = mask[:, t if kind == 0 else kind + 1, :]
                    v.scalar_tensor_tensor(buf, src, DH ** -0.5, rows.unsqueeze(1).to_broadcast([P, 2, SEQ]),
                                           ALU.mult, ALU.add).then_inc(drain_of(key), 1)
                else:
                    v.tensor_scalar(buf, src, MEM_DH ** -0.5, None, ALU.mult).then_inc(drain_of(key), 1)
                wait_drained(eng, key)
                v.tensor_reduce(neg_max[:, t, kind, pair:pair + 3:2], buf, AX.X, ALU.max, negate=True)\
                 .then_inc(s["logits_ready"], 1)

            def outputs(j):
                kind, t, pair = j // 4, j // 2 % 2, j % 2
                key = ("values", j)
                if kind < 3:
                    src = wait_filled(eng, key)[:, 0:2 * DH].rearrange("p (h d) -> p h d", h=2)
                    dst = o_dil[:, t, kind, :].rearrange("p (h d) -> p h d", h=4)[:, pair:pair + 3:2, :]
                    v.tensor_copy(dst, src).then_inc(drain_of(key), 1)
                else:
                    eng.wait_ge(s["probs_ready"], 2 * (j + 1))
                    rden = combine[:, 2 + t, 0, 2 * pair:2 * pair + 2]
                    link(v.reciprocal(rden, den[:, t, 3, pair:pair + 3:2]))
                    src = wait_filled(eng, key)[:, 0:256].rearrange("p (h d) -> p h d", h=2)
                    v.tensor_tensor(o_mem[:, t, :].rearrange("p (h d) -> p h d", h=4)[:, pair:pair + 3:2, :], src,
                                    spread(rden, 2, MEM_DH), ALU.mult).then_inc(drain_of(key), 1)

            def convolve(i):
                key = ("cv", i)
                src = wait_filled(eng, key)
                c0 = 2 * (i - 6)
                for k in range(3):
                    wait_drained(eng, ("cv", k))
                    wait_drained(eng, ("cv", 3 + k))
                u = u_conv[:, c0:c0 + 2, 1:SEQ + 1]
                v.tensor_tensor(u, src.rearrange("p (c t) -> p c t", c=2), u, ALU.mult).then_inc(drain_of(key), 1)
                wait_drained(eng, key)
                for c in range(2):
                    ch, dst = c0 + c, tap[:, c, :]
                    w = [cols[:, 24 + 6 * k + ch:25 + 6 * k + ch] for k in range(3)]
                    link(v.tensor_scalar(dst, u_conv[:, ch, 0:SEQ], w[0], None, ALU.mult))
                    link(v.scalar_tensor_tensor(dst, u_conv[:, ch, 1:SEQ + 1], w[1], dst, ALU.mult, ALU.add))
                    link(v.scalar_tensor_tensor(dst, u_conv[:, ch, 2:SEQ + 2], w[2], dst, ALU.mult, ALU.add))
                    v.tensor_tensor(cb[:, ch, :], cb[:, ch, :], dst, ALU.mult).then_inc(s["z_ready"], 1)

            eng.wait_ge(s["zeros_ready"], 1)
            for j in range(18):
                if j < 16:
                    logits(j)
                if j in (1, 2, 3):
                    convolve(5 + j)
                if j >= 2:
                    outputs(j - 2)

            for t in range(NT):
                m, e = neg_max[:, t, 0:3, :], combine[:, t, :, :]
                low = combine[:, 2 + t, 1, :]
                link(v.tensor_reduce(low, m.rearrange("p g h -> p h g"), AX.X, ALU.min))
                eng.wait_ge(s["dve_step"], steps[0])
                v.tensor_tensor(e, low.unsqueeze(1).to_broadcast([P, 3, 4]), m, ALU.subtract).then_inc(s["peaks_ready"], 1)
                eng.wait_ge(s["peaks_exp"], t + 1)
                total = combine[:, 2 + t, 2, :]
                weighed = mix[:, 0:12].rearrange("p (g h) -> p g h", g=3)
                link(v.tensor_tensor(weighed, e, den[:, t, 0:3, :], ALU.mult))
                link(v.tensor_reduce(total, weighed.rearrange("p g h -> p h g"), AX.X, ALU.add))
                link(v.reciprocal(total, total))
                link(v.tensor_tensor(e, e, total.unsqueeze(1).to_broadcast([P, 3, 4]), ALU.mult))
                o = o_dil[:, t, :, :].rearrange("p g (h d) -> p g h d", h=4)
                for g in range(3):
                    step(v.tensor_tensor(o[:, g, :, :], o[:, g, :, :], spread(e[:, g, :], 4, DH), ALU.mult))
                eng.wait_ge(s["dve_step"], steps[0])
                link(v.tensor_tensor(o_dil[:, t, 0, :], o_dil[:, t, 0, :], o_dil[:, t, 1, :], ALU.add))
                v.tensor_tensor(o_dil[:, t, 0, :], o_dil[:, t, 0, :], o_dil[:, t, 2, :], ALU.add).then_inc(s["o_ready"], 1)
                eng.wait_ge(s["o_ready"], t + 1)

            for branch in range(3):
                for t in range(NT):
                    for half in range(2):
                        key = ("proj", branch, t, half)
                        c = branch * D + half * WIDE
                        wait_drained(eng, ("gate", c // WIDE, t))
                        src, gate = wait_filled(eng, key), gates[:, t, c:c + WIDE]
                        dst = merged[:, t, half * WIDE:(half + 1) * WIDE]
                        if branch == 0:
                            v.tensor_tensor(dst, src, gate, ALU.mult).then_inc(drain_of(key), 1)
                        else:
                            v.tensor_tensor(gate, src, gate, ALU.mult).then_inc(drain_of(key), 1)
                            wait_drained(eng, key)
                            wait_drained(eng, ("proj", branch - 1, t, half))
                            if branch == 2:
                                eng.wait_ge(s["dve_step"], steps[0])
                                v.tensor_tensor(dst, dst, gate, ALU.add).then_inc(s["merged_ready"], 1)
                            else:
                                step(v.tensor_tensor(dst, dst, gate, ALU.add))
            for i in range(2):
                for t in range(NT):
                    key = ("wo", i, t)
                    part = x[:, t, i * WIDE:(i + 1) * WIDE]
                    v.tensor_tensor(part, wait_filled(eng, key), part, ALU.add).then_inc(drain_of(key), 1)

            eng.wait_ge(s["c_silu"], 2)
            for i, c in enumerate((c_wide, c_ctx_wide)):
                v.tensor_copy(c, spread(r_col[:, 0:8, i], 8, P)).then_inc(s["c_wide_ready"], 1)

            def modulation(i, which, dst, plus_one):
                key = ("ad", i, which)
                src = wait_filled(eng, key)
                v.scalar_tensor_tensor(dst, src, 1.0 if plus_one else 0.0, dst, ALU.add, ALU.add).then_inc(drain_of(key), 1)

            for i in range(2):
                for t in range(NT):
                    wait_drained(eng, ("wo", i, t))
            for t in range(NT):
                square_sums(x[:, t, :], h2[:, t, :], stats[:, 4 + t:5 + t])
            root_mean(stats[:, 4:6], D)
            eng.wait_ge(s["wide_in"], 16)
            for t in range(NT):
                v.scalar_tensor_tensor(h2[:, t, :], x[:, t, :], stats[:, 4 + t:5 + t], ffn_gain, ALU.mult, ALU.mult)\
                 .then_inc(s["h2_ready"], 1)
            eng.wait_ge(s["mod_in"], 32)
            for i in range(4):
                for which, dst in enumerate((mod_a, mod_c)):
                    modulation(i, which, dst[:, i // 2, (i % 2) * WIDE:(i % 2 + 1) * WIDE], i >= 2)

            src = wait_filled(eng, "router")
            v.tensor_tensor(r_log, src[:, 0:72].rearrange("p (t c) -> p t c", t=NT),
                            router_b[:, :].unsqueeze(1).to_broadcast([P, NT, 36]), ALU.add).then_inc(drain_of("router"), 1)
            wait_drained(eng, "router")
            groups, peak = r_log[:, :, 0:4], r_col[:, 0, :]
            link(v.tensor_reduce(peak, groups, AX.X, ALU.max))
            v.tensor_tensor(r_tmp[:, 0, :, 0:4], groups, spread(peak, NT, 4), ALU.subtract).then_inc(s["gate_logits"], 1)

            def first_of(values, top, out, n):
                prio = r_prio[:, 8 - n:8].unsqueeze(1).to_broadcast([P, NT, n])
                link(v.tensor_tensor(out, values, spread(top, NT, n), ALU.is_equal))
                link(v.tensor_tensor(out, out, prio, ALU.mult))
                link(v.tensor_reduce(r_col[:, 1, :], out, AX.X, ALU.max))
                link(v.tensor_tensor(out, out, spread(r_col[:, 1, :], NT, n), ALU.is_equal))

            first_of(groups, peak, r_hot, 4)
            v.tensor_copy(r_tmp[:, 1, :, 0:4], r_hot).then_inc(s["hot_ready"], 1)
            eng.wait_ge(s["gate_exp"], 1)
            link(v.tensor_reduce(r_col[:, 2, :], r_tmp[:, 0, :, 0:4], AX.X, ALU.add))
            link(v.reciprocal(r_col[:, 2, :], r_col[:, 2, :]))
            for t in range(NT):
                step(v.tensor_tensor(r_big[:, t, :, :], r_log[:, t, 4:36].rearrange("p (g e) -> p g e", g=GROUPS),
                                     spread(r_hot[:, t, :], GROUPS, 8), ALU.mult))
            eng.wait_ge(s["dve_step"], steps[0])
            sel, hot1, hot2 = r_tmp[:, 2, :, :], r_tmp[:, 3, :, :], r_tmp[:, 4, :, :]
            link(v.tensor_reduce(sel, r_big.rearrange("p t g e -> p t e g"), AX.X, ALU.add))
            link(v.tensor_reduce(r_col[:, 3, :], sel, AX.X, ALU.max))
            first_of(sel, r_col[:, 3, :], hot1, 8)
            link(v.scalar_tensor_tensor(sel, hot1, FAR, sel, ALU.mult, ALU.add))
            link(v.tensor_reduce(r_col[:, 4, :], sel, AX.X, ALU.max))
            first_of(sel, r_col[:, 4, :], hot2, 8)
            v.tensor_tensor(r_col[:, 6, :], r_col[:, 4, :], r_col[:, 3, :], ALU.subtract).then_inc(s["gate_logits"], 1)
            eng.wait_ge(s["gate_exp"], 2)
            link(v.tensor_scalar(r_col[:, 7, :], r_col[:, 6, :], 1.0, None, ALU.add))
            link(v.reciprocal(r_col[:, 7, :], r_col[:, 7, :]))
            link(v.tensor_tensor(r_col[:, 7, :], r_col[:, 7, :], r_col[:, 2, :], ALU.mult))
            link(v.tensor_tensor(r_col[:, 6, :], r_col[:, 6, :], r_col[:, 7, :], ALU.mult))
            step(v.tensor_tensor(hot1, hot1, spread(r_col[:, 7, :], NT, 8), ALU.mult))
            link(v.tensor_tensor(hot2, hot2, spread(r_col[:, 6, :], NT, 8), ALU.mult))
            link(v.tensor_tensor(r_we, hot1, hot2, ALU.add))
            src = wait_filled(eng, "rank")
            v.tensor_copy(r_rank, src[:, 0:12]).then_inc(drain_of("rank"), 1)
            wait_drained(eng, "rank")
            link(v.tensor_reduce(r_col[:, 8, 0:1], r_rank[:, 8:12], AX.X, ALU.max))
            v.tensor_scalar(overflow[:, :], r_col[:, 8, 0:1], float(P), None, ALU.is_gt).then_inc(s["flag_ready"], 1)
            for t in range(NT):
                for g in range(GROUPS):
                    step(v.tensor_scalar(place[:, t, g, :], slot_row, r_rank[:, 4 * t + g:4 * t + g + 1],
                                         r_hot[:, t, g:g + 1], ALU.is_equal, ALU.mult))
            eng.wait_ge(s["dve_step"], steps[0])
            v.tensor_copy(r_tmp[:, 5, :, 0:4], r_hot).then_inc(s["place_ready"], 1)
            src = wait_filled(eng, "w_slot")
            v.tensor_copy(w_slot.rearrange("p g e -> p (g e)"), src[:, 0:32]).then_inc(drain_of("w_slot"), 1)
            wait_drained(eng, "w_slot")
            for t in range(NT):
                wait_drained(eng, ("placeT", t))
            experts_dve(eng, FIRST_PASS)
            where_overflow(eng, lambda: second_pass_dve(eng))
            for m in LAST_TILES:
                FIRST_PASS.wait_drained(eng, GROUPS - 1, m)
            second_block_dve(eng, step, link, root_mean, square_sums, spread, modulation)

        @block.gpsimd
        def _(eng):
            g, steps = nc.gpsimd, [0]

            def link(ins):
                steps[0] += 1
                ins.then_inc(s["pool_step"], 1)
                eng.wait_ge(s["pool_step"], steps[0])

            def keep_where(dst, pattern, base, channel, op, fill):
                link(g.affine_select(out=dst, in_=dst, pattern=pattern, compare_op=op, fill=fill, base=base,
                                     channel_multiplier=channel))

            link(g.memset(const[:, 0, :], 0.0))
            link(g.memset(const[:, 1:10, :], 1.0))
            keep_where(ident, [[-1, P]], 0, 1, ALU.not_equal, 1.0)
            keep_where(upto, [[1, P]], 0, -1, ALU.is_ge, 0.0)
            keep_where(since, [[-1, P]], 0, 1, ALU.is_ge, 0.0)
            keep_where(below, [[-1, P]], 0, 1, ALU.is_gt, 0.0)
            keep_where(above, [[1, P]], 0, -1, ALU.is_gt, 0.0)
            for m, n in ((blk16, 16), (lev32, 32), (lev64, 64)):
                wide = m.rearrange("p (b c) -> p b c", c=n)
                keep_where(wide, [[-n, P // n], [0, n]], 0, 1, ALU.is_ge, 0.0)
                keep_where(wide, [[n, P // n], [0, n]], n - 1, -1, ALU.is_ge, 0.0)
            link(g.tensor_tensor(lev128, lev128, lev64, ALU.subtract))
            link(g.tensor_tensor(lev64, lev64, lev32, ALU.subtract))
            link(g.tensor_tensor(lev32, lev32, blk16, ALU.subtract))
            link(g.iota(slot_row, [[1, P]], base=0, channel_multiplier=0, allow_small_or_imprecise_dtypes=True))
            link(g.iota(r_prio[:, :], [[-1, 8]], base=8, channel_multiplier=0, allow_small_or_imprecise_dtypes=True))
            link(g.iota(distance, [[-1, SEQ]], base=SEQ, channel_multiplier=1))
            for i in range(ROT):
                link(g.memset(inv_freq[:, i:i + 1], float(np.float32(THETA) ** np.float32(-i / ROT))))
            link(g.memset(mask[:, 0:2, :], 0.0))
            for t in range(NT):
                keep_where(mask[:, t, :], [[-1, SEQ]], t * P + BAND, 1, ALU.is_ge, FAR)
                keep_where(mask[:, t, :], [[1, SEQ]], BAND - t * P, -1, ALU.is_ge, FAR)
            g.memset(u_conv[:, :, 0:1], 0.0).then_inc(s["consts_ready"], 1)
            g.memset(u_conv[:, :, SEQ + 1:SEQ + 2], 0.0).then_inc(s["zeros_ready"], 1)
            eng.wait_ge(s["o_ready"], NT)
            eng.wait_ge(s["z_ready"], CONV_TILES)
            eng.dma_start(ffn_gain, a["g_ffn"][0].partition_broadcast(P)).then_inc(s["wide_in"], 16)
            wait_filled(eng, ("wo", 1, 1))
            bias = a["b_ada_2"][0]
            eng.dma_start(mod_a.rearrange("p i d -> p (i d)"), bias[0:2 * D].partition_broadcast(P)).then_inc(s["mod_in"], 16)
            eng.dma_start(mod_c.rearrange("p i d -> p (i d)"), bias[0:2 * D].partition_broadcast(P)).then_inc(s["mod_in"], 16)
            eng.dma_start(ctx_in, a["ctx_2"][0].rearrange("(t p) d -> p t d", p=P)).then_inc(s["ctx_in"], 16)
            second_block_pool(eng, g, link)

        @block.sync
        def _(sp):
            def load(name):
                n = unit_number[name]
                for dst, (src, tiles) in zip(unit_views(name, n % SLOTS), unit_source(name)):
                    sp.dma_start(dst, src.rearrange("(k p) n -> p k n", p=P)).then_inc(landed[n % SLOTS], 16)

            for n, name in enumerate(before_experts):
                if n >= SLOTS:
                    sp.wait_ge(filled, unit_use[before_experts[n - SLOTS]])
                load(name)
            first_loads(sp, FIRST_PASS, lambda q: sp.wait_ge(filled, unit_use[before_experts[FIRST_UNIT - SLOTS + q]]))
            experts_sp(sp, FIRST_PASS)
            where_overflow(sp, lambda: second_pass_sp(sp))
            second_block_sp(sp, load)


INPUTS = ("x mem positions g_mix g_mem w_in g_qn_attn g_kn_attn w_conv w_mem_kv g_qn_mem g_kn_mem w_proj_attn w_proj_conv "
          "w_proj_mem w_out g_ffn w_router_group b_router_group w_router_expert b_router_expert w_gate w_up w_down c_2 ctx_2 "
          "c_ctx_2 w_ada_2 b_ada_2 w_in_2 conv_w_ssd_2 conv_b_ssd_2 dt_bias_ssd_2 a_log_ssd_2 d_skip_ssd_2 norm_w_ssd_2 "
          "conv_w_gdn_2 dt_bias_gdn_2 a_log_gdn_2 norm_w_gdn_2 w_out_2 ln1_g_2 ln1_b_2 w_ffn_gate_2 w_ffn_up_2 w_ffn_down_2 "
          "ln2_g_2 ln2_b_2").split()


def kernel(**inputs):
    import numpy as _np
    import concourse.bacc as _bacc
    from concourse import mybir as _mybir
    from concourse.bass_utils import run_bass_kernel_spmd as _run

    nc = _bacc.Bacc("TRN2", target_bir_lowering=False, num_devices=1)
    arrays, args = {}, {}
    for name in INPUTS:
        value = _np.ascontiguousarray(inputs[name])
        arrays[f"in_{name}"] = value
        args[name] = nc.dram_tensor(f"in_{name}", value.shape, _mybir.dt.from_np(value.dtype), kind="ExternalInput").ap()
    out = nc.dram_tensor("out_0", (1, SEQ, D), F32, kind="ExternalOutput").ap()
    two_block_kernel(nc, args, out)
    r = _run(nc, [arrays], core_ids=[0])
    return r.results[0]["out_0"]
```

```python
from contextlib import ExitStack

import concourse.bass as bass
import numpy as np
from concourse import mybir

F32 = mybir.dt.float32
I32 = mybir.dt.int32
ALU = mybir.AluOpType
ACT = mybir.ActivationFunctionType
AX = mybir.AxisListType

P = 128
D = 1024
KD = D // P
SEQ = 256
NT = SEQ // P
BANKS = 6
SLOTS = 3
SLOT = 4096
WIDE = 512
EPS = 1e-6
LN_EPS = 1e-5
FAR = -1e30

HEADS, DH = 12, 64
DILATIONS = (1, 4, 16)
BAND = 64
ROT = DH // 8
CONV_TILES = 768 // P
MEM_HEADS, MEM_DH = 4, 128
GROUPS, PER_GROUP, FF = 4, 8, 512
EXPERTS = GROUPS * PER_GROUP
FF_TILES = FF // P
THETA = 500000.0

ROUND = 1.5 * 2.0 ** 23
TURN = (6.28125, 0.001934051513671875, 2 * np.pi - 6.28125 - 0.001934051513671875)

GRID = 64
ROWS = SEQ // GRID
CHUNKS = 4
SSD_HEADS, SSD_P, SSD_G, SSD_N = 16, 64, 2, 128
GDN_HEADS, GDN_DH = 8, 128
TAPS = 5
FFN = 2816
FFN_TILES = FFN // P
ALPHA = 2.0 ** 0.25
CTX_PAD = SEQ + TAPS - 1
ROW_PAD = GRID + TAPS - 1
LAT_PAD = ROWS * ROW_PAD

COLS_A = {"g_mix": (0, 8), "g_mem": (8, 8), "g_ffn": (16, 8), "w_conv": (24, 18),
          "conv_b_ssd_2": (42, 12), "conv_w_ssd_2": (54, 60), "c_ctx_2": (114, 8)}
ROWS_A = 122
COLS_B = {"conv_w_gdn_2": (0, 120), "c_2": (120, 8)}
ROWS_B = 128


class TileOrder:

    def __init__(self):
        self.count = 0
        self.at = {}

    def number(self, key):
        assert key not in self.at, key
        self.at[key] = self.count
        self.count += 1
        return self.at[key]


def weight_stream():
    before = ["in0", "in1", "in2", "in3", "in4", "in9", "mk0", "mk1"]
    before += [f"in{i}" for i in (5, 6, 7, 8, 10, 11, 12, 13, 14, 15)]
    before += ["pc0", "pc1", "pa", "pm", "wo0", "wo1", "ad0", "ad1", "ad2", "ad3"]
    after = ["xb0", "dta", "xb1", "xb2", "k0", "k1", "v0", "v1", "q0", "q1", "gt0", "gt1", "z0", "z1"]
    after += [f"ad{i}" for i in range(4, 10)] + [f"w2{i}" for i in range(4)] + ["ad10", "ad11"]
    after += [f"{w}{i}" for i in range(6) for w in ("fg", "fu")] + [f"fd{i}" for i in range(6)]
    return before, after


def two_block_kernel(nc, a, out):
    before_experts, after_experts = weight_stream()
    ctx = ExitStack()
    with ctx:
        def sb(name, shape, dt=F32):
            return ctx.enter_context(nc.sbuf_tensor(name, shape, dt))

        def sem(name):
            return ctx.enter_context(nc.semaphore(name))

        ring = sb("ring", [P, SLOTS, SLOT])
        x = sb("x", [P, NT, D])
        const = sb("const", [P, 11, P])
        ident, ones, upto, since, below, above, blk16, lev32, lev64, lev128, slot_row = (const[:, i, :] for i in range(11))
        cols = sb("cols", [P, 2 * P])
        head_gain = sb("head_gain", [P, 2, DH])
        mem_gain = sb("mem_gain", [P, 2, MEM_DH])
        router_b = sb("router_b", [P, GROUPS + EXPERTS])
        router_w = sb("router_w", [P, KD, GROUPS + EXPERTS])
        gate_bias = sb("gate_bias", [P, 48])
        decay_rate = sb("decay_rate", [P, 48])
        d_skip = sb("d_skip", [P, SSD_HEADS])
        gdn_gain = sb("gdn_gain", [P, GDN_DH])
        stats = sb("stats", [P, 64])
        pos_i = sb("pos_i", [P, NT], I32)
        rope = sb("rope", [P, 8, 2, NT, ROT])
        inv_freq = sb("inv_freq", [P, ROT])
        overflow = sb("overflow", [P, 1], I32)
        AREA = 35760
        area = sb("area", [P, AREA])

        def at(offset, *shape):
            size = int(np.prod(shape))
            assert offset + size <= AREA, (offset, shape)
            flat = area[:, offset:offset + size]
            names = "abcd"[:len(shape)]
            if len(shape) == 1:
                return flat
            return flat.rearrange(f"p ({' '.join(names)}) -> p {' '.join(names)}", **dict(zip(names, shape)))

        xn = at(0, NT, D)
        cb = at(0, CONV_TILES, SEQ)
        hT = at(2048, KD, SEQ)
        mergedT = at(2048, KD, SEQ)
        mem = at(4096, NT, D)
        o_mem = at(4096, NT, MEM_HEADS * MEM_DH)
        mT = at(6144, KD, SEQ)
        o_dil = at(6144, NT, 3, 256)
        qk = at(8192, NT, 24, DH)
        oT = at(8192, 6, SEQ)
        v_dil = at(11264, NT, 12 * DH)
        qk_mem = at(12800, NT, 8, MEM_DH)
        PT = at(12800, 3, 4, P)
        v_mem = at(14848, NT, 512)
        qkT = at(15872, 12, SEQ)
        merged = at(15872, NT, D)
        qk_memT = at(18944, 8, SEQ)
        gates = at(20992, NT, 3 * D)
        u_conv = at(27136, CONV_TILES, SEQ + 2)
        rows_a = at(28684, 2, P)
        S = at(28684, 3, 2, SEQ)
        squares = at(28684, 24, DH)
        mask = at(30220, 4, SEQ)
        tap = at(31244, 2, SEQ)
        mix = at(31756, 768)
        neg_max = at(32524, NT, 4, 4)
        den = at(32556, NT, 4, 4)
        combine = at(32588, 4, 3, 4)

        mod_a = at(0, 2, D)
        mod_c = at(2048, 2, D)
        h2 = at(4096, NT, D)
        h2T = at(6144, KD, SEQ)
        ffn_gain = at(31000, D)
        place = at(8192, NT, GROUPS, P)
        placeT = at(9216, GROUPS, SEQ)
        place_now = at(10240, SEQ)
        hcT = at(10496, KD, P)
        silu_g = at(11520, 2, FF)
        act = at(12544, 2, FF)
        actT = at(13568, 2, FF_TILES, P)
        y_group = at(14592, D)
        r_log = at(15616, NT, 36)
        r_tmp = at(15688, 8, NT, 8)
        r_big = at(15816, NT, GROUPS, 8)
        r_hot = at(15880, NT, GROUPS)
        r_we = at(15888, NT, 8)
        r_rank = at(15904, 12)
        r_prio = sb("r_prio", [P, 8])
        w_slot = at(15924, GROUPS, 8)
        r_col = at(15956, 16, NT)
        c_wide = at(34690, KD, P)
        c_ctx_wide = at(17024, KD, P)
        ctx_in = at(18048, NT, D)
        h_lat = at(20096, NT, D)

        head_root = sb("head_root", [P, NT, 24])
        distance, mask_i = tap[:, 0, :].bitcast(I32), tap[:, 1, :].bitcast(I32)

        def flat(ap):
            return ap.rearrange({1: "n -> n", 2: "a n -> (a n)", 3: "a b n -> (a b n)"}[len(ap.shape)])

        small_loads = [(pos_i[:, t:t + 1], a["positions"][0, t * P:(t + 1) * P].rearrange("(p o) -> p o", o=1)) for t in range(NT)]
        small_loads += [(router_w[:, :, 0:4], a["w_router_group"][0].rearrange("(k p) n -> p k n", p=P)),
                        (router_w[:, :, 4:36], a["w_router_expert"][0].rearrange("(k p) n -> p k n", p=P))]
        for dst, name in ((head_gain[:, 0, :], "g_qn_attn"), (head_gain[:, 1, :], "g_kn_attn"),
                          (mem_gain[:, 0, :], "g_qn_mem"), (mem_gain[:, 1, :], "g_kn_mem"),
                          (router_b[:, 0:4], "b_router_group"), (router_b[:, 4:36], "b_router_expert"),
                          (gate_bias[:, 0:32], "dt_bias_ssd_2"), (gate_bias[:, 32:48], "dt_bias_gdn_2"),
                          (decay_rate[:, 0:32], "a_log_ssd_2"), (decay_rate[:, 32:48], "a_log_gdn_2"),
                          (d_skip[:, :], "d_skip_ssd_2"), (gdn_gain[:, :], "norm_w_gdn_2")):
            small_loads.append((dst, flat(a[name]).partition_broadcast(P)))
        N_SMALL = len(small_loads)

        hB = at(4096, KD, 2 * SEQ)
        v_gdn = at(0, CHUNKS, D)
        xs = at(8192, CHUNKS, D)
        bm = at(12288, CHUNKS, 256)
        bmT = at(13312, SSD_G, 2 * SEQ)
        cmT = at(14336, SSD_G, SEQ)
        k_gdn = at(14848, CHUNKS, D)
        qT = at(18944, GDN_HEADS, SEQ)
        y_ssd = at(20992, NT, D)
        o_gdn = at(23040, NT, D)
        SMALL = 25088
        raw = at(SMALL, CHUNKS, 48)
        soft = at(SMALL + 192, CHUNKS, 48)
        beta = at(SMALL + 384, CHUNKS, 16)
        log_a = at(SMALL + 448, CHUNKS, 2, 24)
        cum = at(SMALL + 640, 2, CHUNKS, 24)
        cum_exp = at(SMALL + 832, 2, CHUNKS, 24)
        total = at(SMALL + 1024, 2, CHUNKS, 24)
        rest = at(SMALL + 1216, 2, CHUNKS, 24)
        beta_cum = at(SMALL + 1408, 2, CHUNKS, 8)
        k_root = at(SMALL + 1472, CHUNKS, 8)
        q_root = at(SMALL + 1504, NT, 8)
        y_root = at(SMALL + 1520, NT, SSD_G)
        o_root = at(SMALL + 1524, NT, 8)
        TEMP = SMALL + 1600
        pad = at(TEMP, 3, CTX_PAD + LAT_PAD)
        conv = at(TEMP + 1596, 3, CTX_PAD + LAT_PAD)
        chan = at(TEMP + 3192, 3, 2 * SEQ)
        ssd_state = at(TEMP, SSD_G, 512)
        xdt = at(TEMP + 1024, D)
        x_rest = at(TEMP + 2048, D)
        att = at(TEMP + 3072, 4, 4, P)
        cb_mask = at(TEMP + 5120, SSD_G, P)
        y_tmp = at(TEMP + 5376, 512)
        dta_rows = at(TEMP + 3192, 2 * SEQ)[0:64, :]
        gdn_state = at(TEMP, GDN_HEADS, P)
        o_tmp = [at(TEMP + 1024 + 512 * h, 4, P) for h in range(2)]
        places = [8192 + 512 * i for i in range(12)] + [TEMP + 2048 + 512 * i for i in range(4)]
        buf = [[at(places[8 * h + i], 4, P) for i in range(8)] for h in range(2)]
        z_silu = at(23040, NT, D)
        gate_silu = at(TEMP + 5888, NT, D)
        ssd_gain = at(TEMP + 4096, D)
        q_square = at(TEMP + 4096, GDN_HEADS, P)
        o_square = at(TEMP + 4096, D)
        yoT = at(8192, 2 * KD, SEQ)
        mod_rows = at(4096, 4, D)
        norm_rows = at(14848, 4, D)
        h_ffn = at(0, NT, D)
        h_ffnT = at(2048, KD, SEQ)
        ffn_silu = at(TEMP, 4, 2, SEQ)
        ffn_act = at(8192, FFN_TILES, SEQ)
        ffn_tmp = at(TEMP + 2048, 2, 512)

        psum = ctx.enter_context(nc.psum_tensor("psum", [P, 8, WIDE], F32))
        order = TileOrder()
        filled = sem("filled")
        drained = [sem(f"drained{b}") for b in range(BANKS)]
        landed = [sem(f"landed{s}") for s in range(SLOTS)]

        def wait_filled(eng, key):
            n = order.at[key]
            eng.wait_ge(filled, n + 1)
            return psum[:, n % BANKS, :]

        def drain_of(key):
            return drained[order.at[key] % BANKS]

        def wait_drained(eng, key):
            n = order.at[key]
            eng.wait_ge(drained[n % BANKS], n // BANKS + 1)

        s = {name: sem(name) for name in (
            "ident_ready", "consts_ready", "x_in", "mem_in", "rows_in", "small_in", "wide_in", "ctx_in",
            "pool_step", "dve_step", "root_asked", "root_done", "xn_ready", "mn_ready",
            "angles_ready", "tables_ready", "qk_ready", "logits_ready", "probs_ready", "zeros_ready",
            "z_ready", "peaks_ready", "peaks_exp", "o_ready", "merged_ready", 
            "h2_ready", "gate_logits", "gate_exp", "hot_ready", "place_ready", "flag_ready",
            "x_ready", "x_scaled", "c_silu", "c_wide_ready", 
            "out_done", "mod_in", "hctx_ready", "hlat_ready", "pads_ready", "conv_ready", "channels_ready", "abs_ready",
            "abs_exp", "one_ready", "one_ln", "beta_raw", "beta_ready", "rate_ready", "log_a_ready", "cum_ready", "cum_exp",
            "x_rest_ready", "ssd_decay", "att_ready", "kn_ready", "q_square_ready", 
            "gdn_clipped", "gdn_decay", "gdn_decayT", "gdn_masked", "gdn_maskedT", "n_ready",
            "one_plus_n", "level_ready", "kv_ready", "k_rest_ready", "k_sums", "gate_gain", "k_rooted", "y_ready", "o_normed", "mod_filled", "mod_drained", "rows2_in", "norm_in", "h_ffn_ready", "beta_cum_ready",
            "gain_in")}
        PIECES = {j: 2 + j for j in range(10)}
        unit_use = {}
        MOE_TILES = 2 + 3 * PER_GROUP + 4

        def unit_source(name):
            kind, i = name.rstrip("0123456789"), int(name[len(name.rstrip("0123456789")):] or 0)
            if name.startswith("w2"):
                kind, i = "w2", int(name[2:])
            if kind == "in":
                return [(a["w_in"][0, :, i * WIDE:(i + 1) * WIDE], 8)]
            if kind == "mk":
                return [(a["w_mem_kv"][0, :, i * WIDE:(i + 1) * WIDE], 8)]
            if kind == "pa":
                return [(a["w_proj_attn"][0], 2)]
            if kind == "pc":
                return [(a["w_proj_conv"][0, 512 * i:min(512 * i + 512, 768), :], 4 if i == 0 else 2)]
            if kind == "pm":
                return [(a["w_proj_mem"][0], 4)]
            if kind == "wo":
                return [(a["w_out"][0, :, i * WIDE:(i + 1) * WIDE], 8)]
            if kind == "ad":
                return [(a["w_ada_2"][0, :, i * WIDE:(i + 1) * WIDE], 8)]
            first = {"xb": 1024, "q": 2592, "k": 3616, "v": 4640, "z": 0, "gt": 5664}
            if kind in first:
                c = first[kind] + i * WIDE
                return [(a["w_in_2"][0, :, c:c + WIDE], 8)]
            if kind == "dta":
                return [(a["w_in_2"][0, :, 2560:2592], 8), (a["w_in_2"][0, :, 6688:6720], 8)]
            if kind == "w2":
                return [(a["w_out_2"][0, 512 * i:512 * i + 512, :], 4)]
            if kind in ("fg", "fu"):
                w = a["w_ffn_gate_2" if kind == "fg" else "w_ffn_up_2"]
                return [(w[0, :, i * WIDE:min((i + 1) * WIDE, FFN)], 8)]
            assert kind == "fd", name
            return [(a["w_ffn_down_2"][0, 512 * i:min(512 * i + 512, FFN), :], 4 if i < 5 else 2)]

        def gate_inputs(slot):
            return ring[:, slot, 0:KD * 64].rearrange("p (k n) -> p k n", k=KD)

        def unit_views(name, slot):
            if name == "dta":
                both = gate_inputs(slot)
                return [both[:, :, 0:32], both[:, :, 32:64]]
            views, offset = [], 0
            for src, tiles in unit_source(name):
                width = src.shape[1]
                views.append(ring[:, slot, offset:offset + tiles * width].rearrange("p (k n) -> p k n", k=tiles))
                offset += tiles * width
            return views

        expert_units = [("g", 0), ("u", 0)]
        for e in range(1, PER_GROUP):
            expert_units += [("g", e), ("u", e), ("d", e - 1)]
        expert_units += [("d", PER_GROUP - 1)]
        GROUP_UNITS = len(expert_units)
        TILE = {"g": 2, "u": 3, "t": 4}

        def released_by(q):
            kind, e = expert_units[q]
            if kind == "d":
                return TILE["t"] + 3 * (e + 1) if e < PER_GROUP - 1 else 2 + 3 * PER_GROUP
            return TILE[kind] + 3 * e

        unit_number, landed_by, arrivals = {}, {}, [0] * SLOTS
        for n, name in enumerate(before_experts):
            unit_number[name] = n
            arrivals[n % SLOTS] += 16 * len(unit_source(name))
            landed_by[name] = arrivals[n % SLOTS]
        FIRST_UNIT = len(before_experts)
        expert_arrivals = list(arrivals)
        for n, name in enumerate(after_experts, FIRST_UNIT + EXPERTS * 3):
            unit_number[name] = n
            arrivals[n % SLOTS] += 16 * len(unit_source(name))
            landed_by[name] = arrivals[n % SLOTS] + 16 * EXPERTS * 3 // SLOTS

        block = ctx.enter_context(nc.Block())

        CHANNELS = [("xs", i) for i in range(8)] + [("bm", i) for i in range(2)] + [("cm", i) for i in range(2)]
        CHANNELS += [(kind, i) for kind in "kvq" for i in range(8)]
        TURNED = ("xs", "bm", "k", "v")
        LAT_ONLY = ("cm", "q")
        SEQUENCE = ((0, 1, 2, 3), (1, 0, 3, 2))
        LEVELS = (lev32, lev64, lev128)
        EARLY = 3
        Q_SUMS = (6, 8)
        MOD_FIRST = 4
        gate_order = [(kind, i, t) for kind in ("gt", "z") for i in range(2) for t in range(NT)]
        GATE_TILES = [gate_order[0:2], gate_order[2:4], gate_order[4:5], gate_order[6:7], gate_order[7:8]]
        TURN_TILES = gate_order[5:6]

        def channel_out(n):
            kind, i = CHANNELS[n]
            return {"bm": lambda: bmT[:, i, :], "cm": lambda: cmT[:, i, :], "q": lambda: qT[:, i, :]}.get(
                kind, lambda: chan[:, n % 3, :])()

        def second_block_pe(pe, open_tile, unit, used, transposes, product, tokens_by_weights, modulation):
            def columns(src, h, ready):
                for t in range(NT):
                    pe.wait_ge(s[ready], t + 1)
                    for half in range(2):
                        transposes(("hB", src, t, half), [h[:, t, (4 * half + j) * P:(4 * half + j + 1) * P] for j in range(4)])
                for t in range(NT):
                    for half in range(2):
                        wait_drained(pe, ("hB", src, t, half))

            columns(0, ctx_in, "hctx_ready")
            w, = unit("xb0")
            for n in range(EARLY):
                product(open_tile(("channel_ctx", n))[:, 0:SEQ], lambda k: w[:, k, n * P:(n + 1) * P],
                        lambda k: hB[:, k, 0:SEQ], KD).then_inc(filled, 1)
            columns(1, h_lat, "hlat_ready")
            unit("dta")
            both = gate_inputs(unit_number["dta"] % SLOTS)
            product(open_tile("dtaT")[0:64, :], lambda k: both[:, k, :], lambda k: hB[:, k, :], KD).then_inc(filled, 1)
            used("dta")

            def turn_channels(n):
                if n >= 0 and CHANNELS[n][0] in TURNED:
                    pe.wait_ge(s["channels_ready"], n + 1)
                    transposes(("turned", n), [channel_out(n)[:, c * P:(c + 1) * P] for c in range(CHUNKS)])

            names = ["xb0", "xb1", "xb2", "k0", "k1", "v0", "v1", "q0", "q1"]
            for n in range(len(CHANNELS)):
                if n % 4 == 0:
                    w, = unit(names[n // 4])
                tokens = slice(SEQ if n < EARLY or CHANNELS[n][0] in LAT_ONLY else 0, 2 * SEQ)
                dst = open_tile(("channel", n))
                product(dst[:, 0:tokens.stop - tokens.start], lambda k: w[:, k, n % 4 * P:(n % 4 + 1) * P],
                        lambda k: hB[:, k, tokens], KD).then_inc(filled, 1)
                if n % 4 == 3:
                    used(names[n // 4])
                if n == 0:
                    wait_drained(pe, "dtaT")
                    transposes("dta", [dta_rows[:, c * P:(c + 1) * P] for c in range(CHUNKS)])
                turn_channels(n - 2)
                if n == 3:
                    pe.wait_ge(s["log_a_ready"], 4)
                    dst = open_tile("cum")
                    for d, order_of in enumerate((upto, since)):
                        nc.tensor.matmul(dst[:, 96 * d:96 * d + 96], order_of, log_a[:, :, d, :], start=True, stop=True)
                    nc.tensor.matmul(dst[:, 192:384], ones, log_a.rearrange("p c d h -> p (c d h)"),
                                     start=True, stop=True).then_inc(filled, 1)

            def gate_tiles(steps_of):
                for kind, i, t in steps_of:
                    if t == 0:
                        gate_tiles.w, = unit(f"{kind}{i}")
                    tokens_by_weights((kind, i, t), hB[:, :, SEQ:2 * SEQ], t, gate_tiles.w)
                    if t == NT - 1:
                        used(f"{kind}{i}")

            gate_tiles(GATE_TILES[0])
            step = 0
            pe.wait_ge(s["cum_exp"], 3)
            for n in range(12):
                if CHANNELS[n][0] in TURNED:
                    wait_drained(pe, ("turned", n))
            for d in range(2):
                if d:
                    gate_tiles(TURN_TILES)
                for ci, c in enumerate(SEQUENCE[d]):
                    if c >= 2:
                        tok, lat = slice(c * P, (c + 1) * P), slice((c - 2) * P, (c - 1) * P)
                        dst = open_tile(("cb", d, c))
                        for g in range(SSD_G):
                            last = nc.tensor.matmul(dst[:, g * P:(g + 1) * P], bmT[:, g, tok], cmT[:, g, lat], start=True, stop=True)
                        last.then_inc(filled, 1)
                        for q in range(4):
                            dst = open_tile(("ssd_rows", d, c, q))
                            for i in range(4):
                                last = nc.tensor.matmul(dst[:, i * P:(i + 1) * P],
                                                        log_a[:, c, d, 4 * q + i:4 * q + i + 1].to_broadcast([P, P]),
                                                        (upto, since)[d], start=True, stop=True)
                            last.then_inc(filled, 1)
                        for g in range(SSD_G):
                            if g == 0:
                                wait_drained(pe, ("state", d, SEQUENCE[d][ci - 1], 0))
                                wait_drained(pe, ("state", d, SEQUENCE[d][ci - 1], 1))
                            dst = open_tile(("y_state", d, c, g))
                            nc.tensor.matmul(dst, cmT[:, g, lat], ssd_state[:, g, :], start=True, stop=True).then_inc(filled, 1)
                        gate_tiles(GATE_TILES[1 + step])
                    pe.wait_ge(s["x_rest_ready"], 4 * d + ci + 1)
                    if c >= 2:
                        for g in range(SSD_G):
                            pe.wait_ge(s["att_ready"], 4 * step + 2 * g + 2)
                            dst = open_tile(("y_inner", d, c, g))
                            for j in range(8):
                                h = 8 * g + j
                                last = nc.tensor.matmul(dst[:, j * SSD_P:(j + 1) * SSD_P], att[:, h // 4, h % 4, :],
                                                        xdt[:, h * SSD_P:(h + 1) * SSD_P], start=True, stop=True)
                            last.then_inc(filled, 1)
                        step += 1
                    if ci < 3:
                        for g in range(SSD_G):
                            dst = open_tile(("state", d, c, g))
                            nc.tensor.matmul(dst, bm[:, c, g * P:(g + 1) * P], x_rest[:, g * 512:(g + 1) * 512],
                                             start=True, stop=True).then_inc(filled, 1)

            def four(key, lhs, rhs):
                dst = open_tile(key)
                for i in range(4):
                    last = nc.tensor.matmul(dst[:, i * P:(i + 1) * P], lhs(i), rhs(i), start=True, stop=True)
                last.then_inc(filled, 1)

            def mod_steps(first, last):
                for i in range(first, last):
                    tile, k = MOD_FIRST + i // KD, i % KD
                    if k == 0:
                        mod_steps.w, = unit(f"ad{tile}")
                        if tile >= MOD_FIRST + 2:
                            pe.wait_ge(s["mod_drained"], tile - MOD_FIRST - 1)
                    ins = nc.tensor.matmul(psum[:, BANKS + tile % 2, :], c_wide[:, k, :], mod_steps.w[:, k, :],
                                           start=k == 0, stop=k == KD - 1)
                    if k == KD - 1:
                        ins.then_inc(s["mod_filled"], 1)
                        unit_use[f"ad{tile}"] = order.count + 1

            m = mods = 0

            def fill_in(count):
                nonlocal mods
                mod_steps(mods, mods + count)
                mods += count

            for d in range(2):
                for ci, c in enumerate(SEQUENCE[d]):
                    lat = slice((c - 2) * P, (c - 1) * P)
                    if d == 0:
                        pe.wait_ge(s["kn_ready"], c + 1)
                    for h in range(2):
                        transposes(("gkT", d, c, h), [k_gdn[:, c, (4 * h + i) * P:(4 * h + i + 1) * P] for i in range(4)])
                    for h in range(2):
                        four(("gR", d, c, h), lambda i: log_a[:, c, d, 16 + 4 * h + i:17 + 4 * h + i].to_broadcast([P, P]),
                             lambda i: (upto, since)[d])
                    for h in range(2):
                        kT = buf[h][6]
                        wait_drained(pe, ("gkT", d, c, h))
                        four(("gKK", d, c, h), lambda i: kT[:, i, :], lambda i: kT[:, i, :])
                        if c >= 2:
                            four(("gQK", d, c, h), lambda i: kT[:, i, :], lambda i: qT[:, 4 * h + i, lat])
                    fill_in(4)
                    for h in range(2):
                        wait_drained(pe, ("gKK", d, c, h))
                        transposes(("gAT", d, c, h), [buf[h][1][:, i, :] for i in range(4)])
                    fill_in(1)
                    for h in range(2):
                        b = buf[h]
                        pe.wait_ge(s["n_ready"], 2 * m + h + 3)
                        four(("gP2", d, c, h), lambda i: b[5][:, i, :], lambda i: b[4][:, i, :])
                        four(("gP2T", d, c, h), lambda i: b[4][:, i, :], lambda i: b[5][:, i, :])
                    for h in range(2):
                        b = buf[h]
                        pe.wait_ge(s["one_plus_n"], m + h + 1)
                        wait_drained(pe, ("gP2", d, c, h))
                        wait_drained(pe, ("gP2T", d, c, h))
                        four(("gX2", d, c, h), lambda i: b[6][:, i, :], lambda i: b[7][:, i, :])
                        four(("gP4", d, c, h), lambda i: b[6][:, i, :], lambda i: b[0][:, i, :])
                        four(("gP4T", d, c, h), lambda i: b[0][:, i, :], lambda i: b[6][:, i, :])
                    for h in range(2):
                        b = buf[h]
                        for key in ("gX2", "gP4", "gP4T"):
                            wait_drained(pe, (key, d, c, h))
                        four(("gX4", d, c, h), lambda i: b[5][:, i, :], lambda i: b[7][:, i, :])
                        four(("gP8T", d, c, h), lambda i: b[4][:, i, :], lambda i: b[5][:, i, :])
                    for h in range(2):
                        b = buf[h]
                        for key in ("gX4", "gP8T"):
                            wait_drained(pe, (key, d, c, h))
                        four(("gX8", d, c, h), lambda i: b[6][:, i, :], lambda i: b[7][:, i, :])
                    for h in range(2):
                        wait_drained(pe, ("gX8", d, c, h))
                        transposes(("gXT", d, c, h, 0), [buf[h][7][:, i, :] for i in range(4)])
                    for lev in range(3):
                        for h in range(2):
                            b = buf[h]
                            pe.wait_ge(s["level_ready"], 3 * m + 2 * lev + h + 1)
                            four(("gT", d, c, h, lev), lambda i: b[6][:, i, :], lambda i: b[7][:, i, :])
                        for h in range(2):
                            b = buf[h]
                            wait_drained(pe, ("gXT", d, c, h, lev))
                            wait_drained(pe, ("gT", d, c, h, lev))
                            if lev < 2:
                                four(("gY", d, c, h, lev), lambda i: b[4][:, i, :], lambda i: b[0][:, i, :])
                            else:
                                four(("gY", d, c, h, lev), lambda i: b[0][:, i, :], lambda i: b[4][:, i, :])
                        for h in range(2 if lev < 2 else 0):
                            wait_drained(pe, ("gY", d, c, h, lev))
                            transposes(("gXT", d, c, h, lev + 1), [buf[h][7][:, i, :] for i in range(4)])
                    for h in range(2):
                        b = buf[h]
                        pe.wait_ge(s["kv_ready"], m + h + 1)
                        wait_drained(pe, ("gY", d, c, h, 2))
                        if ci:
                            four(("gw", d, c, h), lambda i: b[3][:, i, :], lambda i: b[4][:, i, :])
                    for h in range(2):
                        b = buf[h]
                        if ci:
                            wait_drained(pe, ("gw", d, c, h))
                            wait_drained(pe, ("gS", d, SEQUENCE[d][ci - 1], h))
                        dst = open_tile(("gv", d, c, h))
                        for i in range(4):
                            part = dst[:, i * P:(i + 1) * P]
                            last = nc.tensor.matmul(part, b[4][:, i, :], b[1][:, i, :], start=True, stop=not ci)
                            if ci:
                                last = nc.tensor.matmul(part, b[0][:, i, :], gdn_state[:, 4 * h + i, :], start=False, stop=True)
                        last.then_inc(filled, 1)
                        if c >= 2:
                            four(("go1", d, c, h), lambda i: qT[:, 4 * h + i, lat], lambda i: gdn_state[:, 4 * h + i, :])
                    for h in range(2):
                        b = buf[h]
                        wait_drained(pe, ("gv", d, c, h))
                        if c >= 2:
                            wait_drained(pe, ("gQK", d, c, h))
                            four(("go2", d, c, h), lambda i: b[2][:, i, :], lambda i: b[5][:, i, :])
                        if ci < 3:
                            pe.wait_ge(s["k_rest_ready"], 6 * d + 2 * ci + h + 1)
                            four(("gS", d, c, h), lambda i: b[6][:, i, :], lambda i: b[5][:, i, :])
                    if m in Q_SUMS:
                        t = Q_SUMS.index(m)
                        pe.wait_ge(s["q_square_ready"], t + 1)
                        dst = open_tile(("q_sums", t))
                        for h in range(GDN_HEADS):
                            last = nc.tensor.matmul(dst[:, h:h + 1], q_square[:, h, :], ones[:, 0:1], start=True, stop=True)
                        last.then_inc(filled, 1)
                    m += 2

            pe.wait_ge(s["y_ready"], NT * SSD_G)
            for src, rows in enumerate((y_ssd, o_gdn)):
                for t in ((0, 1), (1, 0))[src]:
                    if src:
                        pe.wait_ge(s["o_normed"], 2 - t)
                    for half in range(2):
                        transposes(("yoT", src, t, half), [rows[:, t, (4 * half + j) * P:(4 * half + j + 1) * P] for j in range(4)])
                if src == 0:
                    mod_steps(mods, mods + KD)
                    mods += KD
            for src in range(2):
                for t in range(NT):
                    for half in range(2):
                        wait_drained(pe, ("yoT", src, t, half))

            def long_product(key, names, lhs):
                banks = [open_tile((key, t, half)) for t in range(NT) for half in range(2)]
                k0 = 0
                for n, name in enumerate(names):
                    w, = unit(name)
                    tiles = w.shape[1]
                    for j, dst in enumerate(banks):
                        t, half = j // 2, j % 2
                        last = product(dst, lambda k: lhs[:, k0 + k, t * P:(t + 1) * P],
                                       lambda k: w[:, k, half * WIDE:(half + 1) * WIDE], tiles,
                                       first=n == 0, final=n == len(names) - 1)
                        if n == len(names) - 1:
                            last.then_inc(filled, 1)
                        elif j == len(banks) - 1:
                            last.then_inc(passed, 1)
                            unit_passed.append(name)
                    k0 += tiles
                used(names[-1])

            long_product("w2", [f"w2{i}" for i in range(4)], yoT)
            mod_steps(mods, KD * (12 - MOD_FIRST))
            for t in range(NT):
                pe.wait_ge(s["h_ffn_ready"], t + 1)
                for half in range(2):
                    transposes(("h_ffnT", t, half), [h_ffn[:, t, (4 * half + j) * P:(4 * half + j + 1) * P] for j in range(4)])
            for t in range(NT):
                for half in range(2):
                    wait_drained(pe, ("h_ffnT", t, half))
            for i in range(6):
                for kind in ("fg", "fu"):
                    w, = unit(f"{kind}{i}")
                    for j in range(w.shape[2] // 256):
                        dst = open_tile((kind, 2 * i + j))
                        for c in range(2):
                            ch = slice(256 * j + c * P, 256 * j + (c + 1) * P)
                            last = product(dst[:, c * SEQ:(c + 1) * SEQ], lambda k: w[:, k, ch], lambda k: h_ffnT[:, k, :], KD)
                        last.then_inc(filled, 1)
                    used(f"{kind}{i}")
            for j in range(FFN_TILES // 2):
                wait_drained(pe, ("fu", j))
            long_product("fd", [f"fd{i}" for i in range(6)], ffn_act)

        passed = sem("passed")
        unit_passed = []

        def second_block_act(eng, root, copy_out):
            def columns(src):
                for t in range(NT):
                    for half in range(2):
                        copy_out(("hB", src, t, half), hB[:, 4 * half:4 * half + 4, src * SEQ + t * P:src * SEQ + (t + 1) * P])

            columns(0)
            eng.wait_ge(s["pads_ready"], 1)
            for n in range(EARLY):
                copy_out(("channel_ctx", n), pad[:, n, 2:2 + SEQ], cols=SEQ)
            columns(1)
            nc.scalar.copy(dta_rows, wait_filled(eng, "dtaT")[0:64, :]).then_inc(drain_of("dtaT"), 1)
            eng.wait_ge(s["beta_raw"], 1)
            nc.scalar.activation(beta, beta, ACT.Sigmoid).then_inc(s["beta_ready"], 1)
            nc.scalar.activation(decay_rate[:, :], decay_rate[:, :], ACT.Exp).then_inc(s["rate_ready"], 1)
            eng.wait_ge(s["abs_ready"], 1)
            nc.scalar.activation(soft, soft, ACT.Exp, scale=-1.0).then_inc(s["abs_exp"], 1)
            eng.wait_ge(s["one_ready"], 1)
            nc.scalar.activation(soft, soft, ACT.Ln).then_inc(s["one_ln"], 1)

            def pad_in(n):
                key = ("channel", n)
                if n >= 3:
                    eng.wait_ge(s["conv_ready"], n - 2)
                src = wait_filled(eng, key)
                dst, lat = pad[:, n % 3, :], 0
                if n >= EARLY and CHANNELS[n][0] not in LAT_ONLY:
                    nc.scalar.copy(dst[:, 2:2 + SEQ], src[:, 0:SEQ])
                    lat = SEQ
                rows = dst[:, CTX_PAD:].rearrange("p (r c) -> p r c", r=ROWS)[:, :, 2:2 + GRID]
                nc.scalar.copy(rows, src[:, lat:lat + SEQ].rearrange("p (r c) -> p r c", r=ROWS)).then_inc(drain_of(key), 1)

            def activate(n):
                kind, _ = CHANNELS[n]
                eng.wait_ge(s["conv_ready"], n + 1)
                if n >= 3 and CHANNELS[n - 3][0] in TURNED:
                    wait_filled(eng, ("turned", n - 3))
                src, dst, lat = conv[:, n % 3, :], channel_out(n), 0
                bias = {"bias": cols[:, 42 + n:43 + n]} if n < 12 else {}
                if kind not in LAT_ONLY:
                    nc.scalar.activation(dst[:, 0:SEQ], src[:, 0:SEQ], ACT.Silu, **bias)
                    lat = SEQ
                rows = src[:, CTX_PAD:].rearrange("p (r c) -> p r c", r=ROWS)[:, :, 0:GRID]
                nc.scalar.activation(dst[:, lat:lat + SEQ].rearrange("p (r c) -> p r c", r=ROWS), rows, ACT.Silu,
                                     **bias).then_inc(s["channels_ready"], 1)

            for n in range(len(CHANNELS) + 1):
                if n < len(CHANNELS):
                    pad_in(n)
                if n >= 1:
                    activate(n - 1)
            eng.wait_ge(s["cum_ready"], 1)
            nc.scalar.activation(cum_exp, cum, ACT.Exp).then_inc(s["cum_exp"], 1)
            nc.scalar.activation(total, total, ACT.Exp).then_inc(s["cum_exp"], 1)
            nc.scalar.activation(rest, rest, ACT.Exp).then_inc(s["cum_exp"], 1)

            def gate_tiles(steps_of):
                for kind, i, t in steps_of:
                    dst = {"z": z_silu, "gt": gate_silu}[kind]
                    copy_out((kind, i, t), dst[:, t, i * WIDE:(i + 1) * WIDE], func=ACT.Silu)

            gate_tiles(GATE_TILES[0])
            for n in range(12, len(CHANNELS)):
                if CHANNELS[n][0] == "k":
                    wait_drained(eng, ("turned", n))
            for c in range(CHUNKS):
                if c:
                    eng.wait_ge(s["k_sums"], 8 * c)
                for h in range(GDN_HEADS):
                    nc.scalar.activation(psum[:, BANKS + h // 4, h % 4 * P:(h % 4 + 1) * P], k_gdn[:, c, h * P:(h + 1) * P],
                                         ACT.Square, accum_out=k_root[:, c, h:h + 1]).then_inc(s["k_sums"], 1)
            n = 0
            for d in range(2):
                for c in SEQUENCE[d][2:]:
                    for q in range(4):
                        n += 1
                        wait_drained(eng, ("ssd_rows", d, c, q))
                        nc.scalar.activation(att[:, q, :, :], att[:, q, :, :], ACT.Exp).then_inc(s["ssd_decay"], 1)
                    gate_tiles(GATE_TILES[n // 4])
                if d == 0:
                    gate_tiles(TURN_TILES)
                    root(k_root)

            def out4(key, dst, scale=1.0):
                src = wait_filled(eng, key).rearrange("p (h c) -> p h c", h=4)
                nc.scalar.activation(dst, src, ACT.Copy, scale=scale).then_inc(drain_of(key), 1)

            m = lm = 0
            for d in range(2):
                for ci, c in enumerate(SEQUENCE[d]):
                    for h in range(2):
                        out4(("gkT", d, c, h), buf[h][6])
                    for h in range(2):
                        if c >= 2:
                            eng.wait_ge(s["gdn_clipped"], lm + h + 1)
                        else:
                            wait_drained(eng, ("gR", d, c, h))
                        nc.scalar.activation(buf[h][1], buf[h][1], ACT.Exp, scale=-1.0).then_inc(s["gdn_decay"], 1)
                    for h in range(2 if c >= 2 else 0):
                        wait_drained(eng, ("gR", d, c, h))
                        nc.scalar.activation(buf[h][2], buf[h][2], ACT.Exp).then_inc(s["gdn_decayT"], 1)
                    for h in range(2):
                        out4(("gAT", d, c, h), buf[h][3])
                    for h in range(2):
                        out4(("gP2", d, c, h), buf[h][0])
                        out4(("gP2T", d, c, h), buf[h][6])
                    for h in range(2):
                        out4(("gP4", d, c, h), buf[h][4])
                        out4(("gP4T", d, c, h), buf[h][5])
                    for h in range(2):
                        out4(("gP8T", d, c, h), buf[h][6])
                    for h in range(2):
                        out4(("gXT", d, c, h, 0), buf[h][4])
                    for lev in range(3):
                        for h in range(2):
                            out4(("gT", d, c, h, lev), buf[h][0])
                        for h in range(2 if lev < 2 else 0):
                            out4(("gXT", d, c, h, lev + 1), buf[h][4])
                    if ci:
                        for h in range(2):
                            out4(("gw", d, c, h), buf[h][0], scale=-1.0)
                    for h in range(2):
                        out4(("gv", d, c, h), buf[h][5])
                    if m == 2:
                        root(y_root)
                    if m == Q_SUMS[1] + 2:
                        root(q_root)
                    if m == 14:
                        root(o_root[:, 1, :])
                    m += 2
                    lm += 2 * (c >= 2)
            root(o_root[:, 0, :])
            for src in range(2):
                for t in ((0, 1), (1, 0))[src]:
                    for half in range(2):
                        copy_out(("yoT", src, t, half), yoT[:, 8 * src + 4 * half:8 * src + 4 * half + 4, t * P:(t + 1) * P])
            root(stats[:, 6:8])
            for t in range(NT):
                for half in range(2):
                    copy_out(("h_ffnT", t, half), h_ffnT[:, 4 * half:4 * half + 4, t * P:(t + 1) * P])
            for j in range(FFN_TILES // 2):
                if j >= 4:
                    wait_drained(eng, ("fu", j - 4))
                copy_out(("fg", j), ffn_silu[:, j % 4, :, :], func=ACT.Silu)
            root(stats[:, 8:10])

        def second_block_dve(eng, step, link, root_mean, root_ask, root_take, square_sums, spread):
            v = nc.vector
            for m in (26, 27, 28, 29):
                FIRST_PASS.wait_drained(eng, GROUPS - 1, m)
            for t in range(NT):
                link(v.tensor_tensor(h_lat[:, t, :], x[:, t, :], mod_a[:, 1, :], ALU.mult))
                v.tensor_tensor(h_lat[:, t, :], h_lat[:, t, :], mod_a[:, 0, :], ALU.add).then_inc(s["hlat_ready"], 1)
            src = wait_filled(eng, "dta").rearrange("p (c h) -> p c h", c=CHUNKS)
            v.tensor_copy(beta, src[:, :, 32:48]).then_inc(s["beta_raw"], 1)
            step(v.tensor_tensor(raw[:, :, 0:32], src[:, :, 0:32],
                                 gate_bias[:, 0:32].unsqueeze(1).to_broadcast([P, CHUNKS, 32]), ALU.add))
            v.tensor_tensor(raw[:, :, 32:48], src[:, :, 48:64],
                            gate_bias[:, 32:48].unsqueeze(1).to_broadcast([P, CHUNKS, 16]), ALU.add).then_inc(drain_of("dta"), 1)
            wait_drained(eng, "dta")
            v.scalar_tensor_tensor(soft, raw, -1.0, raw, ALU.mult, ALU.max).then_inc(s["abs_ready"], 1)
            eng.wait_ge(s["abs_exp"], 1)
            v.tensor_scalar(soft, soft, 1.0, None, ALU.add).then_inc(s["one_ready"], 1)
            eng.wait_ge(s["one_ln"], 1)
            link(v.scalar_tensor_tensor(soft, raw, 0.0, soft, ALU.max, ALU.add))
            eng.wait_ge(s["rate_ready"], 1)
            link(v.tensor_scalar(decay_rate[:, :], decay_rate[:, :], -1.0, None, ALU.mult))
            for first, n, place_at in ((0, 16, 0), (32, 8, 16)):
                for d in range(2):
                    part = slice(first + n * d, first + n * d + n)
                    v.tensor_tensor(log_a[:, :, d, place_at:place_at + n], soft[:, :, part],
                                    decay_rate[:, part].unsqueeze(1).to_broadcast([P, CHUNKS, n]), ALU.mult)\
                     .then_inc(s["log_a_ready"], 1)

            def cumulate():
                src = wait_filled(eng, "cum")
                step(v.tensor_copy(cum.rearrange("p d c h -> p (d c h)"), src[:, 0:192]))
                v.tensor_copy(total, src[:, 192:384].rearrange("p (c d h) -> p d c h", c=CHUNKS, d=2)).then_inc(drain_of("cum"), 1)
                wait_drained(eng, "cum")
                v.tensor_tensor(rest, total, cum, ALU.subtract).then_inc(s["cum_ready"], 1)

            eng.wait_ge(s["pads_ready"], 1)

            def convolve(n):
                kind, i = CHANNELS[n]
                if n >= 3:
                    eng.wait_ge(s["channels_ready"], n - 2)
                if n < EARLY:
                    wait_drained(eng, ("channel_ctx", n))
                wait_drained(eng, ("channel", n))
                first = CTX_PAD if kind in LAT_ONLY else 0
                width = CTX_PAD + LAT_PAD - first - TAPS + 1
                dst = conv[:, n % 3, first:first + width]
                for tap_i in range(TAPS):
                    if n < 12:
                        w = cols[:, 54 + 12 * tap_i + n:55 + 12 * tap_i + n]
                    else:
                        j = {"q": 0, "k": 8, "v": 16}[kind] + i
                        w = cols[:, P + 24 * tap_i + j:P + 24 * tap_i + j + 1]
                    src = pad[:, n % 3, first + tap_i:first + tap_i + width]
                    if tap_i == 0:
                        link(v.tensor_scalar(dst, src, w, None, ALU.mult))
                    elif tap_i < TAPS - 1:
                        link(v.scalar_tensor_tensor(dst, src, w, dst, ALU.mult, ALU.add))
                    else:
                        v.scalar_tensor_tensor(dst, src, w, dst, ALU.mult, ALU.add).then_inc(s["conv_ready"], 1)

            def turned(n):
                kind, i = CHANNELS[n]
                if kind in TURNED:
                    key = ("turned", n)
                    dst = {"xs": xs, "bm": bm, "k": k_gdn, "v": v_gdn}[kind][:, :, i * P:(i + 1) * P]
                    v.tensor_copy(dst, wait_filled(eng, key).rearrange("p (c d) -> p c d", c=CHUNKS)).then_inc(drain_of(key), 1)

            for n in range(len(CHANNELS) + 2):
                if n < len(CHANNELS):
                    convolve(n)
                if n == 3:
                    cumulate()
                if n >= 2:
                    turned(n - 2)

            eng.wait_ge(s["cum_exp"], 3)
            eng.wait_ge(s["channels_ready"], len(CHANNELS))
            for n in range(12):
                if CHANNELS[n][0] in TURNED:
                    wait_drained(eng, ("turned", n))
            heads = lambda ap: ap.rearrange("p (h d) -> p h d", d=SSD_P)
            for t in range(NT):
                step(v.tensor_tensor(heads(y_ssd[:, t, :]), heads(xs[:, 2 + t, :]), spread(d_skip[:, :], SSD_HEADS, SSD_P), ALU.mult))
            eng.wait_ge(s["beta_ready"], 1)
            for d in range(2):
                v.tensor_tensor(beta_cum[:, d, :, :], beta[:, :, 8 * d:8 * d + 8], cum_exp[:, d, :, 16:24], ALU.mult)\
                 .then_inc(s["beta_cum_ready"], 1)
            n = 0
            for d in range(2):
                for ci, c in enumerate(SEQUENCE[d]):
                    if (d, ci) == (1, 0):
                        eng.wait_ge(s["k_sums"], CHUNKS * GDN_HEADS)
                        root_ask(k_root, 1.0)
                    if (d, ci) == (1, 1):
                        root_take(k_root, "k_rooted")
                    t = c - 2
                    before = ("state", d, SEQUENCE[d][ci - 1], 1) if ci else ("y_inner", 0, SEQUENCE[0][3], 1) if d else None
                    if before:
                        wait_filled(eng, before)
                    link(v.tensor_tensor(heads(xdt), heads(xs[:, c, :]),
                                         spread(soft[:, c, 16 * d:16 * d + 16], SSD_HEADS, SSD_P), ALU.mult))
                    v.tensor_tensor(heads(x_rest), heads(xdt), spread(rest[:, d, c, 0:16], SSD_HEADS, SSD_P), ALU.mult)\
                     .then_inc(s["x_rest_ready"], 1)
                    if c >= 2:
                        key = ("cb", d, c)
                        order_of = (upto, since)[d].unsqueeze(1).to_broadcast([P, SSD_G, P])
                        src = wait_filled(eng, key)[:, 0:2 * P].rearrange("p (g c) -> p g c", g=SSD_G)
                        v.tensor_tensor(cb_mask, src, order_of, ALU.mult).then_inc(drain_of(key), 1)
                        for q in range(4):
                            key = ("ssd_rows", d, c, q)
                            src = wait_filled(eng, key)
                            for i in range(4):
                                ins = v.tensor_scalar(att[:, q, i, :], src[:, i * P:(i + 1) * P],
                                                      cum[:, d, c, 4 * q + i:4 * q + i + 1], 0.0, ALU.subtract, ALU.min)
                            ins.then_inc(drain_of(key), 1)
                        for g in range(SSD_G):
                            key = ("y_state", d, c, g)
                            src = heads(wait_filled(eng, key))
                            v.tensor_tensor(heads(y_tmp), src, spread(cum_exp[:, d, c, 8 * g:8 * g + 8], 8, SSD_P), ALU.mult)\
                             .then_inc(drain_of(key), 1)
                            wait_drained(eng, key)
                            part = y_ssd[:, t, g * 512:(g + 1) * 512]
                            link(v.tensor_tensor(part, part, y_tmp, ALU.add))
                        wait_drained(eng, ("cb", d, c))
                        for q in range(4):
                            n += 1
                            eng.wait_ge(s["ssd_decay"], n)
                            v.tensor_tensor(att[:, q, :, :], att[:, q, :, :],
                                            cb_mask[:, q // 2, :].unsqueeze(1).to_broadcast([P, 4, P]), ALU.mult)\
                             .then_inc(s["att_ready"], 1)
                        for g in range(SSD_G):
                            key = ("y_inner", d, c, g)
                            part = y_ssd[:, t, g * 512:(g + 1) * 512]
                            v.tensor_tensor(part, wait_filled(eng, key), part, ALU.add).then_inc(drain_of(key), 1)
                            wait_drained(eng, key)
                    if ci < 3:
                        for g in range(SSD_G):
                            key = ("state", d, c, g)
                            src = wait_filled(eng, key)
                            if ci == 0:
                                if d:
                                    wait_filled(eng, ("y_state", 0, SEQUENCE[0][3], g))
                                v.tensor_copy(ssd_state[:, g, :], src).then_inc(drain_of(key), 1)
                            else:
                                wait_drained(eng, ("state", d, SEQUENCE[d][ci - 1], g))
                                link(v.tensor_tensor(heads(ssd_state[:, g, :]), heads(ssd_state[:, g, :]),
                                                     spread(total[:, d, c, 8 * g:8 * g + 8], 8, SSD_P), ALU.mult))
                                v.tensor_tensor(ssd_state[:, g, :], src, ssd_state[:, g, :], ALU.add).then_inc(drain_of(key), 1)

            of = lambda ap: ap.rearrange("p (h d) -> p h d", d=GDN_DH)
            negated = lambda out, a_in, m: v.scalar_tensor_tensor(out, a_in, -1.0, m.unsqueeze(1).to_broadcast([P, 4, P]),
                                                                  ALU.mult, ALU.mult)

            def four(key):
                return wait_filled(eng, key).rearrange("p (h c) -> p h c", h=4)

            def modulate(i):
                if i == MOD_FIRST:
                    eng.wait_ge(s["rows2_in"], 16)
                eng.wait_ge(s["mod_filled"], i - MOD_FIRST + 1)
                dst = mod_rows[:, (i - MOD_FIRST) // 2, (i % 2) * WIDE:(i % 2 + 1) * WIDE]
                v.scalar_tensor_tensor(dst, psum[:, BANKS + i % 2, :], 1.0 if i in (8, 9) else 0.0, dst, ALU.add, ALU.add)\
                 .then_inc(s["mod_drained"], 1)

            def gated_y():
                for t in range(NT):
                    for i in range(2):
                        wait_drained(eng, ("z", i, t))
                    link(v.tensor_tensor(y_ssd[:, t, :], y_ssd[:, t, :], z_silu[:, t, :], ALU.mult))
                    for g in range(SSD_G):
                        square_sums(y_ssd[:, t, g * 512:(g + 1) * 512], y_tmp, y_root[:, t, g:g + 1])
                root_ask(y_root, 512)

            def normed_y():
                root_take(y_root)
                eng.wait_ge(s["gain_in"], 16)
                for t in range(NT):
                    for g in range(SSD_G):
                        part = slice(g * 512, (g + 1) * 512)
                        v.scalar_tensor_tensor(y_ssd[:, t, part], y_ssd[:, t, part], y_root[:, t, g:g + 1],
                                               ssd_gain[:, part], ALU.mult, ALU.mult).then_inc(s["y_ready"], 1)

            def o_squares(t):
                for d in range(2):
                    for h in range(2):
                        wait_drained(eng, ("go2", d, 2 + t, h))
                rows, junk = of(o_gdn[:, t, :]), of(o_square)
                link(v.tensor_tensor(junk, rows, rows, ALU.mult))
                link(v.tensor_reduce(o_root[:, t, :], junk, AX.X, ALU.add))
                for _ in range(2):
                    link(v.tensor_tensor(o_root[:, t, :], o_root[:, t, :], q_root[:, t, :], ALU.mult))

            m = lm = done = 0
            for d in range(2):
                for ci, c in enumerate(SEQUENCE[d]):
                    for which, clip in ((1, ALU.max), (2, ALU.min))[:1 + (c >= 2)]:
                        for h in range(2):
                            src = four(("gR", d, c, h))
                            for i in range(4):
                                ins = v.tensor_scalar(buf[h][which][:, i, :], src[:, i, :],
                                                      cum[:, d, c, 16 + 4 * h + i:17 + 4 * h + i], 0.0, ALU.subtract, clip)
                            if which == 1 and c >= 2:
                                ins.then_inc(s["gdn_clipped"], 1)
                            else:
                                ins.then_inc(drain_of(("gR", d, c, h)), 1)
                    for h in range(2):
                        key = ("gKK", d, c, h)
                        eng.wait_ge(s["gdn_masked"], m + h + 1)
                        src = four(key)
                        for i in range(4):
                            rate = beta[:, c, 8 * d + 4 * h + i:8 * d + 4 * h + i + 1]
                            ins = v.scalar_tensor_tensor(buf[h][1][:, i, :], src[:, i, :], rate, buf[h][1][:, i, :],
                                                         ALU.mult, ALU.mult)
                        ins.then_inc(drain_of(key), 1)
                    for h in range(2):
                        wait_drained(eng, ("gKK", d, c, h))
                        negated(buf[h][4], buf[h][1], blk16).then_inc(s["n_ready"], 1)
                    for h in range(2):
                        if c >= 2:
                            key = ("gQK", d, c, h)
                            eng.wait_ge(s["gdn_maskedT"], lm + h + 1)
                            v.tensor_tensor(buf[h][2], four(key), buf[h][2], ALU.mult).then_inc(drain_of(key), 1)
                        wait_drained(eng, ("gAT", d, c, h))
                        negated(buf[h][5], buf[h][3], blk16).then_inc(s["n_ready"], 1)
                    for name in ("gX2", "gX4", "gX8"):
                        for h in range(2):
                            key = (name, d, c, h)
                            v.tensor_tensor(buf[h][7], four(key), buf[h][7], ALU.add).then_inc(drain_of(key), 1)
                    for lev in range(3):
                        for h in range(2):
                            key = ("gY", d, c, h, lev)
                            if lev == 2:
                                wait_drained(eng, ("gXT", d, c, h, lev))
                            dst = buf[h][7 if lev < 2 else 4]
                            v.tensor_tensor(dst, dst, four(key), ALU.subtract).then_inc(drain_of(key), 1)
                    if c >= 2:
                        for h in range(2):
                            key = ("go1", d, c, h)
                            v.tensor_tensor(o_tmp[h], four(key), spread(cum_exp[:, d, c, 16 + 4 * h:20 + 4 * h], 4, P), ALU.mult)\
                             .then_inc(drain_of(key), 1)
                    for h in range(2):
                        if c >= 2:
                            key = ("go2", d, c, h)
                            dst = of(o_gdn[:, c - 2, 512 * h:512 * h + 512])
                            wait_drained(eng, ("go1", d, c, h))
                            if d:
                                link(v.tensor_tensor(o_tmp[h], o_tmp[h], dst, ALU.add))
                            v.tensor_tensor(dst, four(key), o_tmp[h], ALU.add).then_inc(drain_of(key), 1)
                        if ci < 3:
                            key, state = ("gS", d, c, h), gdn_state[:, 4 * h:4 * h + 4, :]
                            src = four(key)
                            if ci == 0:
                                v.tensor_copy(state, src).then_inc(drain_of(key), 1)
                            else:
                                link(v.tensor_tensor(state, state, spread(total[:, d, c, 16 + 4 * h:20 + 4 * h], 4, P), ALU.mult))
                                v.tensor_tensor(state, src, state, ALU.add).then_inc(drain_of(key), 1)
                    if m == 0:
                        gated_y()
                    if m == 2:
                        normed_y()
                    if m in Q_SUMS:
                        t = Q_SUMS.index(m)
                        v.tensor_copy(q_root[:, t, :], wait_filled(eng, ("q_sums", t))[:, 0:8]).then_inc(drain_of(("q_sums", t)), 1)
                    if m + 2 in Q_SUMS:
                        t = Q_SUMS.index(m + 2)
                        eng.wait_ge(s["y_ready"], NT * SSD_G)
                        v.tensor_tensor(q_square, qT[:, :, t * P:(t + 1) * P], qT[:, :, t * P:(t + 1) * P], ALU.mult)\
                         .then_inc(s["q_square_ready"], 1)
                    if m == Q_SUMS[1]:
                        for t in range(NT):
                            wait_drained(eng, ("q_sums", t))
                        root_ask(q_root, 1.0)
                    if m == Q_SUMS[1] + 2:
                        root_take(q_root)
                        link(v.tensor_scalar(q_root, q_root, GDN_DH ** -0.5, None, ALU.mult))
                    if m == 12:
                        o_squares(1)
                        root_ask(o_root[:, 1, :], GDN_DH)
                    m += 2
                    lm += 2 * (c >= 2)
                    while done < 5 * m // 2 // KD:
                        modulate(MOD_FIRST + done)
                        done += 1
            eng.wait_ge(s["gate_gain"], NT)
            root_take(o_root[:, 1, :])
            o_squares(0)
            root_ask(o_root[:, 0, :], GDN_DH)
            for t in (1, 0):
                if t == 0:
                    root_take(o_root[:, 0, :])
                rows = of(o_gdn[:, t, :])
                link(v.tensor_tensor(o_root[:, t, :], o_root[:, t, :], q_root[:, t, :], ALU.mult))
                link(v.tensor_tensor(rows, rows, spread(o_root[:, t, :], 8, GDN_DH), ALU.mult))
                v.tensor_tensor(o_gdn[:, t, :], o_gdn[:, t, :], gate_silu[:, t, :], ALU.mult).then_inc(s["o_normed"], 1)

            def residual(key, t, half, gate):
                part, tmp = slice(half * WIDE, (half + 1) * WIDE), ffn_tmp[:, half, :]
                v.tensor_tensor(tmp, wait_filled(eng, (key, t, half)), mod_rows[:, gate, part], ALU.mult)\
                 .then_inc(drain_of((key, t, half)), 1)
                wait_drained(eng, (key, t, half))
                link(v.tensor_tensor_reduce(x[:, t, part], x[:, t, part], tmp, 1.0, 0.0, ALU.add, ALU.add,
                                            row_sums[:, half, t:t + 1]))

            row_sums = stats[:, 16:20].rearrange("p (h t) -> p h t", h=2)

            def layer_norm(ss, gain, then):
                mean = stats[:, 12:14]
                link(v.tensor_tensor(mean, row_sums[:, 0, :], row_sums[:, 1, :], ALU.add))
                link(v.tensor_scalar(mean, mean, 1.0 / D, None, ALU.mult))
                for t in range(NT):
                    link(v.tensor_scalar(x[:, t, :], x[:, t, :], mean[:, t:t + 1], None, ALU.subtract))
                    square_sums(x[:, t, :], h_ffn[:, t, :], ss[:, t:t + 1])
                root_mean(ss, D, LN_EPS)
                for t in range(NT):
                    if t == 0:
                        eng.wait_ge(s["norm_in"], 16 * 4)
                    link(v.scalar_tensor_tensor(x[:, t, :], x[:, t, :], ss[:, t:t + 1], norm_rows[:, gain, :], ALU.mult, ALU.mult))
                    then(t, v.tensor_tensor(x[:, t, :], x[:, t, :], norm_rows[:, gain + 1, :], ALU.add))

            def modulated(t, ins):
                link(ins)
                link(v.tensor_tensor(h_ffn[:, t, :], x[:, t, :], mod_rows[:, 2, :], ALU.mult))
                v.tensor_tensor(h_ffn[:, t, :], h_ffn[:, t, :], mod_rows[:, 1, :], ALU.add).then_inc(s["h_ffn_ready"], 1)

            modulate(9)
            eng.wait_ge(s["mod_drained"], 10 - MOD_FIRST)
            eng.wait_ge(s["x_scaled"], 1)
            for t in range(NT):
                for half in range(2):
                    residual("w2", t, half, 0)
            layer_norm(stats[:, 6:8], 0, modulated)
            modulate(10)
            modulate(11)
            for j in range(FFN_TILES // 2):
                key = ("fu", j)
                wait_drained(eng, ("fg", j))
                v.tensor_tensor(ffn_act[:, 2 * j:2 * j + 2, :], wait_filled(eng, key).rearrange("p (c t) -> p c t", c=2),
                                ffn_silu[:, j % 4, :, :], ALU.mult).then_inc(drain_of(key), 1)
            eng.wait_ge(s["mod_drained"], 12 - MOD_FIRST)
            eng.wait_ge(s["x_scaled"], 2)
            for t in range(NT):
                for half in range(2):
                    residual("fd", t, half, 3)
            layer_norm(stats[:, 8:10], 2, lambda t, ins: ins.then_inc(s["x_ready"], 1))

        def second_block_pool(eng, g, link):
            eng.wait_ge(s["ctx_in"], 16)
            for i in range(4):
                wait_drained(eng, ("ad", i, 1))
            for t in range(NT):
                link(g.tensor_tensor(ctx_in[:, t, :], ctx_in[:, t, :], mod_c[:, 1, :], ALU.mult))
                g.tensor_tensor(ctx_in[:, t, :], ctx_in[:, t, :], mod_c[:, 0, :], ALU.add).then_inc(s["hctx_ready"], 1)
            g.memset(pad, 0.0).then_inc(s["pads_ready"], 1)
            eng.wait_ge(s["hlat_ready"], NT)
            g.tensor_scalar(x[:, :, :], x[:, :, :], ALPHA, None, ALU.mult).then_inc(s["x_scaled"], 1)
            of = lambda ap: ap.rearrange("p (h d) -> p h d", d=GDN_DH)
            eng.wait_ge(s["k_rooted"], 1)
            for c in range(CHUNKS):
                g.tensor_tensor(of(k_gdn[:, c, :]), of(k_gdn[:, c, :]),
                                k_root[:, c, :].unsqueeze(2).to_broadcast([P, GDN_HEADS, GDN_DH]), ALU.mult)\
                 .then_inc(s["kn_ready"], 1)
            eng.wait_ge(s["kn_ready"], CHUNKS)
            for n in range(12, len(CHANNELS)):
                if CHANNELS[n][0] in TURNED:
                    wait_drained(eng, ("turned", n))
            wait_filled(eng, GATE_TILES[-1][-1])
            eng.dma_start(mod_rows.rearrange("p i d -> p (i d)"), a["b_ada_2"][0, 2 * D:6 * D].partition_broadcast(P))\
               .then_inc(s["rows2_in"], 16)
            wait_filled(eng, ("y_inner", 1, SEQUENCE[1][3], 1))
            eng.dma_start(ssd_gain, a["norm_w_ssd_2"][0].partition_broadcast(P)).then_inc(s["gain_in"], 16)
            m = lm = 0
            eng.wait_ge(s["beta_cum_ready"], 2)
            by_head = lambda ap: ap.unsqueeze(2).to_broadcast([P, 4, P])
            by_row = lambda ap: ap.unsqueeze(1).to_broadcast([P, 4, P])
            for d in range(2):
                for ci, c in enumerate(SEQUENCE[d]):
                    for h in range(2):
                        eng.wait_ge(s["gdn_decay"], m + h + 1)
                        g.tensor_tensor(buf[h][1], buf[h][1], by_row((below, above)[d]), ALU.mult).then_inc(s["gdn_masked"], 1)
                    for h in range(2 if c >= 2 else 0):
                        eng.wait_ge(s["gdn_decayT"], lm + h + 1)
                        g.tensor_tensor(buf[h][2], buf[h][2], by_row((upto, since)[d]), ALU.mult).then_inc(s["gdn_maskedT"], 1)
                    for h in range(2):
                        b = buf[h]
                        eng.wait_ge(s["n_ready"], 2 * m + h + 1)
                        g.tensor_tensor(b[7], b[4], by_row(ident), ALU.add).then_inc(s["one_plus_n"], 1)
                    for lev, mask_of in enumerate(LEVELS):
                        for h in range(2):
                            b = buf[h]
                            wait_filled(eng, ("gX8", d, c, h) if lev == 0 else ("gT", d, c, h, lev - 1))
                            g.tensor_tensor(b[6], b[3], by_row(mask_of), ALU.mult).then_inc(s["level_ready"], 1)
                    for h in range(2):
                        b = buf[h]
                        heads = slice(512 * h, 512 * h + 512)
                        eng.wait_ge(s["level_ready"], 3 * m + 5 + h)
                        if ci:
                            link(g.tensor_tensor(b[3], of(k_gdn[:, c, heads]), by_head(beta_cum[:, d, c, 4 * h:4 * h + 4]), ALU.mult))
                        g.tensor_tensor(b[1], of(v_gdn[:, c, heads]),
                                        by_head(beta[:, c, 8 * d + 4 * h:8 * d + 4 * h + 4]), ALU.mult).then_inc(s["kv_ready"], 1)
                    for h in range(2 if ci < 3 else 0):
                        b = buf[h]
                        wait_filled(eng, ("gT", d, c, h, 2))
                        g.tensor_tensor(b[6], of(k_gdn[:, c, 512 * h:512 * h + 512]),
                                        by_head(rest[:, d, c, 16 + 4 * h:20 + 4 * h]), ALU.mult).then_inc(s["k_rest_ready"], 1)
                    if m in (4, 6):
                        t = m // 2 - 2
                        for i in range(2):
                            wait_drained(eng, ("gt", i, t))
                        g.tensor_tensor(of(gate_silu[:, t, :]), of(gate_silu[:, t, :]),
                                        gdn_gain[:, :].unsqueeze(1).to_broadcast([P, GDN_HEADS, GDN_DH]), ALU.mult)\
                         .then_inc(s["gate_gain"], 1)
                    m += 2
                    lm += 2 * (c >= 2)
            for h in range(2):
                wait_filled(eng, ("go2", 1, SEQUENCE[1][3], h))
            eng.wait_ge(s["kv_ready"], m)
            for i, name in enumerate(("ln1_g_2", "ln1_b_2", "ln2_g_2", "ln2_b_2")):
                eng.dma_start(norm_rows[:, i, :], a[name][0].partition_broadcast(P)).then_inc(s["norm_in"], 16)
            eng.wait_ge(s["h_ffn_ready"], NT)
            g.tensor_scalar(x[:, :, :], x[:, :, :], ALPHA, None, ALU.mult).then_inc(s["x_scaled"], 1)

        def second_block_sp(sp, load):
            for n, name in enumerate(after_experts):
                if n < SLOTS:
                    FIRST_PASS.wait_filled(sp, GROUPS - 1, released_by(GROUP_UNITS - SLOTS + n))
                elif after_experts[n - SLOTS] in unit_passed:
                    sp.wait_ge(passed, unit_passed.index(after_experts[n - SLOTS]) + 1)
                else:
                    sp.wait_ge(filled, unit_use[after_experts[n - SLOTS]])
                load(name)
            for t in range(NT):
                sp.wait_ge(s["x_ready"], t + 1)
                sp.dma_start(out[0, t * P:(t + 1) * P, :], x[:, t, :]).then_inc(s["out_done"], 16)
            sp.wait_ge(s["out_done"], 16 * NT)

        class Pass:

            def __init__(self, name, filled, drained, landed, arrivals, base):
                self.base = base
                self.filled, self.drained, self.landed, self.arrivals = filled, drained, landed, arrivals
                self.y_full, self.place_now = sem(f"y_full_{name}"), sem(f"place_now_{name}")
                self.y_ready = [sem(f"y_left_ready_{name}"), sem(f"y_right_ready_{name}")]

            def start(self, n0):
                self.n0 = n0

            def bank(self, m):
                return psum[:, (self.n0 + m) % BANKS, :]

            def wait_filled(self, eng, i, m):
                eng.wait_ge(self.filled, i * MOE_TILES + (self.n0 + m + 1 - self.base))

            def wait_drained(self, eng, i, m):
                n = self.n0 + m
                eng.wait_ge(self.drained[n % BANKS], i * (MOE_TILES // BANKS) + (n // BANKS + 1))

            def drain(self, m):
                return self.drained[(self.n0 + m) % BANKS]

            def wait_free(self, eng, i, m):
                n = self.n0 + m
                eng.wait_ge(self.drained[n % BANKS], i * (MOE_TILES // BANKS) + n // BANKS)

            def slot(self, q):
                return (FIRST_UNIT + q) % SLOTS

            def wait_landed(self, eng, i, q):
                before = sum(1 for r in range(q + 1) if self.slot(r) == self.slot(q))
                eng.wait_ge(self.landed[self.slot(q)],
                            i * (16 * GROUP_UNITS // SLOTS) + (self.arrivals[self.slot(q)] + 16 * before))

        FIRST_PASS = Pass("first", filled, drained, landed, expert_arrivals, 0)
        SECOND_PASS = Pass("second", sem("filled_second"), [sem(f"drained_second{b}") for b in range(BANKS)],
                           [sem(f"landed_second{n}") for n in range(SLOTS)], [0] * SLOTS, BANKS)
        PRELUDE = 3
        SECOND_PASS.start(BANKS + PRELUDE)
        LAST_TILES = range(MOE_TILES - BANKS, MOE_TILES)

        def where_overflow(eng, body):
            eng.wait_ge(s["flag_ready"], 1)
            with eng.If(eng.value_load(overflow[0:1, 0:1], min_val=0, max_val=1) > 0):
                body()
            eng.end_ifs()

        def second_pass_pe(pe):
            ps = SECOND_PASS
            for m in LAST_TILES:
                FIRST_PASS.wait_drained(pe, GROUPS - 1, m)
            for b in range(BANKS):
                pe.sem_inc(ps.drained[b], 1)
            pe.wait_ge(place_second, 1)
            for t in range(NT):
                ps.wait_free(pe, 0, t - PRELUDE)
                for g in range(GROUPS):
                    last = nc.tensor.transpose(ps.bank(t - PRELUDE)[:, g * P:(g + 1) * P], place[:, t, g, :], ident)
                last.then_inc(ps.filled, 1)
            ps.wait_free(pe, 0, -1)
            for g in range(GROUPS):
                for t in range(NT):
                    last = nc.tensor.matmul(ps.bank(-1)[:, 8 * g:8 * g + 8], place[:, t, g, :], r_we[:, t, :],
                                            start=t == 0, stop=t == NT - 1)
            last.then_inc(ps.filled, 1)
            experts_pe(pe, ps)
            for m in LAST_TILES:
                ps.wait_drained(pe, GROUPS - 1, m)

        def second_pass_act(eng):
            ps = SECOND_PASS
            for t in range(NT):
                ps.wait_filled(eng, 0, t - PRELUDE)
                nc.scalar.copy(placeT[:, :, t * P:(t + 1) * P],
                               ps.bank(t - PRELUDE).rearrange("p (g c) -> p g c", g=GROUPS)).then_inc(ps.drain(t - PRELUDE), 1)
            experts_act(eng, ps)

        def second_pass_dve(eng):
            ps, v = SECOND_PASS, nc.vector
            for m in LAST_TILES:
                FIRST_PASS.wait_drained(eng, GROUPS - 1, m)
            v.tensor_scalar(r_rank[:, 0:8], r_rank[:, 0:8], float(P), None, ALU.subtract).then_inc(rank_second, 1)
            eng.wait_ge(rank_second, 1)
            for t in range(NT):
                for g in range(GROUPS):
                    last = v.tensor_scalar(place[:, t, g, :], slot_row, r_rank[:, 4 * t + g:4 * t + g + 1],
                                           r_hot[:, t, g:g + 1], ALU.is_equal, ALU.mult)
            last.then_inc(place_second, 1)
            ps.wait_filled(eng, 0, -1)
            v.tensor_copy(w_slot.rearrange("p g e -> p (g e)"), ps.bank(-1)[:, 0:32]).then_inc(ps.drain(-1), 1)
            for m in (-PRELUDE, 1 - PRELUDE, -1):
                ps.wait_drained(eng, 0, m)
            experts_dve(eng, ps)
            for m in LAST_TILES:
                ps.wait_drained(eng, GROUPS - 1, m)

        def second_pass_sp(sp):
            for q in range(SLOTS):
                FIRST_PASS.wait_filled(sp, GROUPS - 1, released_by(GROUP_UNITS - SLOTS + q))
            first_loads(sp, SECOND_PASS)
            experts_sp(sp, SECOND_PASS)
            for q in range(SLOTS):
                SECOND_PASS.wait_filled(sp, GROUPS - 1, released_by(GROUP_UNITS - SLOTS + q))

        def first_loads(sp, ps, ready=lambda q: None):
            for q in range(SLOTS):
                kind, e = expert_units[q]
                ready(q)
                src = (a["w_gate"] if kind == "g" else a["w_up"])[0, e]
                sp.dma_start(expert_slot(ps, kind, e), src.rearrange("(k p) n -> p k n", p=P)).then_inc(ps.landed[ps.slot(q)], 16)

        rank_second, place_second = sem("rank_second"), sem("place_second")

        def expert_slot(ps, kind, e):
            return ring[:, ps.slot(expert_units.index((kind, e))), :].rearrange("p (k n) -> p k n", k=4 if kind == "d" else 8)

        def experts_pe(pe, ps):
            with pe.Fori(0, GROUPS) as i:
                for half in range(2):
                    ps.wait_free(pe, i, half)
                    dst = ps.bank(half)
                    for j in range(4):
                        k = 4 * half + j
                        for t in range(NT):
                            last = nc.tensor.matmul(dst[:, j * P:(j + 1) * P], h2[:, t, k * P:(k + 1) * P],
                                                    place[:, t, bass.ds(i, 1), :].rearrange("p a c -> p (a c)"),
                                                    start=t == 0, stop=t == NT - 1)
                    last.then_inc(ps.filled, 1)
                ps.wait_drained(pe, i, 0)

                def wide(kind, e):
                    m = TILE[kind] + 3 * e
                    ps.wait_landed(pe, i, expert_units.index((kind, e)))
                    ps.wait_free(pe, i, m)
                    w, dst = expert_slot(ps, kind, e), ps.bank(m)
                    for k in range(KD):
                        if (kind, e, k) == ("g", 0, KD // 2):
                            ps.wait_drained(pe, i, 1)
                        last = nc.tensor.matmul(dst, hcT[:, k, :], w[:, k, :], start=k == 0, stop=k == KD - 1)
                    last.then_inc(ps.filled, 1)

                def down(e):
                    ps.wait_landed(pe, i, expert_units.index(("d", e)))
                    ps.wait_drained(pe, i, TILE["t"] + 3 * e)
                    w = expert_slot(ps, "d", e)
                    for half in range(2):
                        for k in range(FF_TILES):
                            last = nc.tensor.matmul(psum[:, BANKS + half, :], actT[:, e % 2, k, :],
                                                    w[:, k, half * WIDE:(half + 1) * WIDE],
                                                    start=e == 0 and k == 0, stop=e == PER_GROUP - 1 and k == FF_TILES - 1)
                        if e == PER_GROUP - 1:
                            last.then_inc(ps.y_full, 1)

                for e in range(PER_GROUP):
                    wide("g", e)
                    wide("u", e)
                    if e >= 1:
                        down(e - 1)
                    m = TILE["t"] + 3 * e
                    ps.wait_drained(pe, i, TILE["u"] + 3 * e)
                    ps.wait_free(pe, i, m)
                    for k in range(FF_TILES):
                        last = nc.tensor.transpose(ps.bank(m)[:, k * P:(k + 1) * P], act[:, e % 2, k * P:(k + 1) * P], ident)
                    last.then_inc(ps.filled, 1)
                down(PER_GROUP - 1)
                pe.wait_ge(ps.place_now, i + 1)
                for half in range(2):
                    pe.wait_ge(ps.y_ready[half], i + 1)
                    for t in range(NT):
                        m = 2 + 3 * PER_GROUP + 2 * half + t
                        ps.wait_free(pe, i, m)
                        nc.tensor.matmul(ps.bank(m), place_now[:, t * P:(t + 1) * P], y_group[:, half * WIDE:(half + 1) * WIDE],
                                         start=True, stop=True).then_inc(ps.filled, 1)

        def experts_act(eng, ps):
            with eng.Fori(0, GROUPS) as i:
                ps.wait_filled(eng, i, 0)
                nc.scalar.copy(hcT[:, 0:4, :].rearrange("p k n -> p (k n)"), ps.bank(0)).then_inc(ps.drain(0), 1)
                for e in range(PER_GROUP):
                    m = TILE["g"] + 3 * e
                    ps.wait_filled(eng, i, m)
                    nc.scalar.activation(silu_g[:, e % 2, :], ps.bank(m), ACT.Silu).then_inc(ps.drain(m), 1)
                    m = TILE["t"] + 3 * e
                    ps.wait_filled(eng, i, m)
                    nc.scalar.copy(actT[:, e % 2, :, :].rearrange("p k n -> p (k n)"), ps.bank(m)).then_inc(ps.drain(m), 1)
                eng.wait_ge(ps.y_full, i * 2 + 1)
                nc.scalar.copy(y_group[:, 0:WIDE], psum[:, BANKS, :]).then_inc(ps.y_ready[0], 1)

        def experts_dve(eng, ps):
            with eng.Fori(0, GROUPS) as i:
                ps.wait_filled(eng, i, 1)
                nc.vector.tensor_copy(hcT[:, 4:8, :].rearrange("p k n -> p (k n)"), ps.bank(1)).then_inc(ps.drain(1), 1)
                nc.vector.tensor_copy(place_now, placeT[:, bass.ds(i, 1), :].rearrange("p a c -> p (a c)"))\
                  .then_inc(ps.place_now, 1)
                for e in range(PER_GROUP):
                    m = TILE["u"] + 3 * e
                    ps.wait_drained(eng, i, TILE["g"] + 3 * e)
                    ps.wait_filled(eng, i, m)
                    nc.vector.scalar_tensor_tensor(
                        out=act[:, e % 2, :], in0=silu_g[:, e % 2, :],
                        scalar=w_slot[:, bass.ds(i, 1), e:e + 1].rearrange("p a c -> p (a c)"),
                        in1=ps.bank(m), op0=ALU.mult, op1=ALU.mult).then_inc(ps.drain(m), 1)
                eng.wait_ge(ps.y_full, i * 2 + 2)
                nc.vector.tensor_copy(y_group[:, WIDE:D], psum[:, BANKS + 1, :]).then_inc(ps.y_ready[1], 1)
                for half in range(2):
                    for t in range(NT):
                        m = 2 + 3 * PER_GROUP + 2 * half + t
                        ps.wait_filled(eng, i, m)
                        part = x[:, t, half * WIDE:(half + 1) * WIDE]
                        nc.vector.tensor_tensor(part, ps.bank(m), part, ALU.add).then_inc(ps.drain(m), 1)

        def experts_sp(sp, ps):
            tensors = {"g": a["w_gate"], "u": a["w_up"], "d": a["w_down"]}

            def load(group, q):
                kind, e = expert_units[q]
                src = tensors[kind][0, bass.ds(group * PER_GROUP + e, 1), :, :].rearrange("e (k p) n -> p (e k) n", p=P)
                sp.dma_start(expert_slot(ps, kind, e), src).then_inc(ps.landed[ps.slot(q)], 16)

            def load_rest(group):
                for q in range(SLOTS, GROUP_UNITS):
                    ps.wait_filled(sp, group, released_by(q - SLOTS))
                    load(group, q)

            with sp.Fori(0, GROUPS - 1) as i:
                load_rest(i)
                for q in range(SLOTS):
                    ps.wait_filled(sp, i, released_by(GROUP_UNITS - SLOTS + q))
                    load(i + 1, q)
            load_rest(GROUPS - 1)

        @block.tensor
        def _(pe):
            def open_tile(key):
                n = order.number(key)
                if n >= BANKS:
                    pe.wait_ge(drained[n % BANKS], n // BANKS)
                return psum[:, n % BANKS, :]

            def unit(name):
                n = unit_number[name]
                pe.wait_ge(landed[n % SLOTS], landed_by[name])
                return unit_views(name, n % SLOTS)

            def used(name):
                unit_use[name] = order.count

            def transposes(key, sources):
                t = open_tile(key)
                for j, src in enumerate(sources):
                    rows, width = src.shape
                    last = nc.tensor.transpose(t[0:width, j * P:j * P + rows], src, ident[0:rows, 0:rows])
                last.then_inc(filled, 1)

            def product(dst, lhs, rhs, count, first=True, final=True):
                for k in range(count):
                    last = nc.tensor.matmul(dst, lhs(k), rhs(k), start=first and k == 0, stop=final and k == count - 1)
                return last

            def tokens_by_weights(key, xT, t, w, width=WIDE):
                dst = open_tile(key)
                product(dst[:, 0:width], lambda k: xT[:, k, t * P:(t + 1) * P], lambda k: w[:, k, 0:width],
                        w.shape[1]).then_inc(filled, 1)

            pe.wait_ge(s["ident_ready"], 1)
            pe.wait_ge(s["rows_in"], 16 * 9)
            t = open_tile("cols")
            nc.tensor.transpose(t[:, 0:ROWS_A], rows_a[0:ROWS_A, 0, :], ident[0:ROWS_A, 0:ROWS_A])
            nc.tensor.transpose(t[:, P:2 * P], rows_a[:, 1, :], ident).then_inc(filled, 1)

            for t in range(NT):
                pe.wait_ge(s["xn_ready"], t + 1)
                for half in range(2):
                    transposes(("hT", t, half), [xn[:, t, (4 * half + j) * P:(4 * half + j + 1) * P] for j in range(4)])
            for t in range(NT):
                for half in range(2):
                    wait_drained(pe, ("hT", t, half))
            for i in (0, 1, 2, 3):
                w, = unit(f"in{i}")
                for t in range(NT):
                    tokens_by_weights(("in", i, t), hT, t, w)
                used(f"in{i}")
                if i == 1:
                    for t in range(NT):
                        pe.wait_ge(s["mn_ready"], t + 1)
                        for half in range(2):
                            transposes(("mT", t, half), [mem[:, t, (4 * half + j) * P:(4 * half + j + 1) * P] for j in range(4)])

            def channels_by_tokens(key, w, first):
                dst = open_tile(key)
                for c in range(2):
                    last = product(dst[:, c * SEQ:(c + 1) * SEQ],
                                   lambda k: w[:, k, first + c * P:first + (c + 1) * P], lambda k: hT[:, k, :], KD)
                last.then_inc(filled, 1)

            w, = unit("in4")
            dst = open_tile("v_rest")
            for t in range(NT):
                last = product(dst[:, t * SEQ:(t + 1) * SEQ], lambda k: hT[:, k, t * P:(t + 1) * P],
                               lambda k: w[:, k, 0:256], KD)
            last.then_inc(filled, 1)
            channels_by_tokens(("cv", 0), w, 256)
            used("in4")
            w, = unit("in9")
            for t in range(NT):
                tokens_by_weights(("in", 9, t), hT, t, w)
            used("in9")
            for t in range(NT):
                for half in range(2):
                    wait_drained(pe, ("mT", t, half))
            for i in range(2):
                w, = unit(f"mk{i}")
                for t in range(NT):
                    tokens_by_weights(("mk", i, t), mT, t, w)
                used(f"mk{i}")

            def conv_piece(i):
                name = f"in{5 + (i - 1) // 2}"
                if (i - 1) % 2 == 0:
                    conv_piece.w, = unit(name)
                channels_by_tokens(("cv", i), conv_piece.w, ((i - 1) % 2) * 256)
                if (i - 1) % 2 == 1:
                    used(name)

            def gate_piece(i):
                name = f"in{10 + i // 2}"
                if i % 2 == 0:
                    gate_piece.w, = unit(name)
                tokens_by_weights(("gate", i // 2, i % 2), hT, i % 2, gate_piece.w)
                if i % 2 == 1:
                    used(name)

            for i in range(1, 9):
                conv_piece(i)
            for i in range(2):
                gate_piece(i)

            for t in range(NT):
                pe.wait_ge(s["qk_ready"], t + 1)
                for j in range(3):
                    transposes(("qkT", t, j), [qk[:, t, 8 * j + 2 * i:8 * j + 2 * i + 2, :].rearrange("p h d -> p (h d)")
                                               for i in range(4)])
            for t in range(NT):
                pe.wait_ge(s["qk_ready"], NT + t + 1)
                for j in range(2):
                    transposes(("qk_memT", t, j), [qk_mem[:, t, 4 * j + i, :] for i in range(4)])

            def scores(j):
                kind, t, pair = j // 4, j // 2 % 2, j % 2
                if j == 0:
                    for tt in range(NT):
                        for jj in range(3):
                            wait_drained(pe, ("qkT", tt, jj))
                if j == 12:
                    for tt in range(NT):
                        for jj in range(2):
                            wait_drained(pe, ("qk_memT", tt, jj))
                dst = open_tile(("scores", j))
                for i in range(2):
                    if kind < 3:
                        head = 4 * kind + pair + 2 * i
                        part = slice(DH * (head % 2), DH * (head % 2) + DH)
                        q, k = qkT[part, head // 2, t * P:(t + 1) * P], qkT[part, 6 + head // 2, :]
                    else:
                        q, k = qk_memT[:, pair + 2 * i, t * P:(t + 1) * P], qk_memT[:, 4 + pair + 2 * i, :]
                    last = nc.tensor.matmul(dst[:, i * SEQ:(i + 1) * SEQ], q, k, start=True, stop=True)
                last.then_inc(filled, 1)

            def turn_probs(j):
                pe.wait_ge(s["probs_ready"], 2 * (j + 1))
                transposes(("PT", j), [S[:, j % 3, i, k * P:(k + 1) * P] for i in range(2) for k in range(NT)])

            def values(j):
                kind, pair = j // 4, j % 2
                wait_drained(pe, ("PT", j))
                if j == 0:
                    wait_drained(pe, ("in", 3, 0))
                    wait_drained(pe, ("in", 3, 1))
                    wait_drained(pe, "v_rest")
                if j == 12:
                    wait_drained(pe, ("mk", 1, 0))
                    wait_drained(pe, ("mk", 1, 1))
                dst = open_tile(("values", j))
                width = DH if kind < 3 else MEM_DH
                for i in range(2):
                    head = (4 * kind if kind < 3 else 0) + pair + 2 * i
                    v = v_dil if kind < 3 else v_mem
                    last = product(dst[:, i * width:(i + 1) * width], lambda k: PT[:, j % 3, 2 * i + k, :],
                                   lambda k: v[:, k, head * width:(head + 1) * width], NT)
                last.then_inc(filled, 1)

            for j in range(18):
                if j < 16:
                    scores(j)
                    if j in PIECES:
                        gate_piece(PIECES[j])
                if 1 <= j <= 16:
                    turn_probs(j - 1)
                if j >= 2:
                    values(j - 2)

            def project(branch, names, lhs, count):
                views = [unit(n)[0] for n in names]
                weights = [(v, k) for v in views for k in range(v.shape[1])]
                for t in range(NT):
                    for half in range(2):
                        dst = open_tile(("proj", branch, t, half))
                        product(dst, lambda k: lhs[:, k, t * P:(t + 1) * P],
                                lambda k: weights[k][0][:, weights[k][1], half * WIDE:(half + 1) * WIDE],
                                count).then_inc(filled, 1)
                for n in names:
                    used(n)

            pe.wait_ge(s["z_ready"], CONV_TILES)
            project(1, ["pc0", "pc1"], cb, 6)
            pe.wait_ge(s["o_ready"], NT)
            transposes("o_dilT", [o_dil[:, t, 0, k * P:(k + 1) * P] for t in range(NT) for k in range(2)])
            for t in range(NT):
                wait_drained(pe, ("values", 15))
                transposes(("o_memT", t), [o_mem[:, t, k * P:(k + 1) * P] for k in range(4)])

            wait_drained(pe, "o_dilT")
            project(0, ["pa"], oT, 2)
            for t in range(NT):
                wait_drained(pe, ("o_memT", t))
            project(2, ["pm"], oT[:, 2:6, :], 4)

            for t in range(NT):
                pe.wait_ge(s["merged_ready"], 2 * (t + 1))
                for half in range(2):
                    transposes(("mergedT", t, half),
                               [merged[:, t, (4 * half + j) * P:(4 * half + j + 1) * P] for j in range(4)])
            for t in range(NT):
                for half in range(2):
                    wait_drained(pe, ("mergedT", t, half))
            for i in range(2):
                w, = unit(f"wo{i}")
                for t in range(NT):
                    tokens_by_weights(("wo", i, t), mergedT, t, w)
                used(f"wo{i}")

            def modulation(i, context):
                w, = unit(f"ad{i}")
                for c in ((c_wide, c_ctx_wide) if context else (c_wide,)):
                    dst = open_tile(("ad", i, 0 if c is c_wide else 1))
                    product(dst, lambda k: c[:, k, :], lambda k: w[:, k, :], KD).then_inc(filled, 1)
                used(f"ad{i}")

            pe.wait_ge(s["c_wide_ready"], 2)
            modulation(0, True)

            for t in range(NT):
                pe.wait_ge(s["h2_ready"], t + 1)
                for half in range(2):
                    transposes(("h2T", t, half), [h2[:, t, (4 * half + j) * P:(4 * half + j + 1) * P] for j in range(4)])
            for t in range(NT):
                for half in range(2):
                    wait_drained(pe, ("h2T", t, half))
            pe.wait_ge(s["small_in"], 16 * N_SMALL)
            dst = open_tile("router")
            for t in range(NT):
                last = product(dst[:, t * 36:(t + 1) * 36], lambda k: h2T[:, k, t * P:(t + 1) * P],
                               lambda k: router_w[:, k, :], KD)
            last.then_inc(filled, 1)
            modulation(1, True)
            pe.wait_ge(s["hot_ready"], 1)
            dst = open_tile("rank")
            nc.tensor.matmul(dst[:, 0:4], above, r_hot[:, 0, :], start=True, stop=True)
            nc.tensor.matmul(dst[:, 4:8], ones, r_hot[:, 0, :], start=True, stop=False)
            nc.tensor.matmul(dst[:, 4:8], above, r_hot[:, 1, :], start=False, stop=True)
            nc.tensor.matmul(dst[:, 8:12], ones, r_hot[:, 0, :], start=True, stop=False)
            nc.tensor.matmul(dst[:, 8:12], ones, r_hot[:, 1, :], start=False, stop=True).then_inc(filled, 1)
            modulation(2, True)
            modulation(3, True)
            pe.wait_ge(s["place_ready"], NT * GROUPS)
            for t in range(NT):
                transposes(("placeT", t), [place[:, t, g, :] for g in range(GROUPS)])
            dst = open_tile("w_slot")
            for g in range(GROUPS):
                last = product(dst[:, 8 * g:8 * g + 8], lambda t: place[:, t, g, :], lambda t: r_we[:, t, :], NT)
            last.then_inc(filled, 1)
            for t in range(NT):
                wait_drained(pe, ("placeT", t))
            FIRST_PASS.start(order.count)
            experts_pe(pe, FIRST_PASS)
            where_overflow(pe, lambda: second_pass_pe(pe))
            order.count += GROUPS * MOE_TILES
            second_block_pe(pe, open_tile, unit, used, transposes, product, tokens_by_weights, modulation)

        @block.scalar
        def _(act_eng):
            eng = act_eng
            roots = [0]

            def root(ap):
                roots[0] += 1
                eng.wait_ge(s["root_asked"], roots[0])
                nc.scalar.activation(ap, ap, ACT.Sqrt).then_inc(s["root_done"], 1)

            def copy_out(key, dst, cols=WIDE, func=ACT.Copy):
                t = wait_filled(eng, key)
                src = t[:, 0:cols]
                if len(dst.shape) == 3:
                    src = src.rearrange("p (a b) -> p a b", a=dst.shape[1])
                nc.scalar.activation(dst, src, func).then_inc(drain_of(key), 1)

            eng.dma_start(x[:, :, :], a["x"][0].rearrange("(t p) d -> p t d", p=P)).then_inc(s["x_in"], 16)
            root(stats[:, 0:2])
            for dst, src in small_loads:
                eng.dma_start(dst, src).then_inc(s["small_in"], 16)
            root(stats[:, 2:4])
            for i in range(3):
                for t in range(NT):
                    copy_out(("in", i, t), qk[:, t, 8 * i:8 * i + 8, :])
            eng.wait_ge(s["angles_ready"], 1)
            nc.scalar.activation(rope[:, 7, :, :, :], rope[:, 6, :, :, :], ACT.Sin).then_inc(s["tables_ready"], 1)
            for t in range(NT):
                copy_out(("in", 3, t), v_dil[:, t, 0:WIDE])
            copy_out("v_rest", v_dil[:, :, WIDE:768])
            eng.wait_ge(s["zeros_ready"], 1)
            copy_out(("cv", 0), u_conv[:, 0:2, 1:SEQ + 1])
            for t in range(NT):
                copy_out(("in", 9, t), qk_mem[:, t, 0:4, :])
            for t in range(NT):
                copy_out(("mk", 0, t), qk_mem[:, t, 4:8, :])
            for t in range(NT):
                copy_out(("mk", 1, t), v_mem[:, t, :])

            def conv_piece(i):
                if i < 3:
                    copy_out(("cv", i), u_conv[:, 2 * i:2 * i + 2, 1:SEQ + 1])
                elif i < 6:
                    copy_out(("cv", i), cb[:, 2 * i - 6:2 * i - 4, :])

            def gate_piece(i):
                copy_out(("gate", i // 2, i % 2), gates[:, i % 2, (i // 2) * WIDE:(i // 2 + 1) * WIDE], func=ACT.Sigmoid)

            for i in range(2 * NT):
                if i < 6:
                    conv_piece(i + 1)
                root(head_root[:, i % 2, 0:24] if i < NT else head_root[:, i % 2, 0:8])
            conv_piece(5)
            for i in range(2):
                gate_piece(i)
            for t in range(NT):
                for j in range(3):
                    copy_out(("qkT", t, j), qkT[:, 4 * j:4 * j + 4, t * P:(t + 1) * P])
            for t in range(NT):
                for j in range(2):
                    copy_out(("qk_memT", t, j), qk_memT[:, 4 * j:4 * j + 4, t * P:(t + 1) * P])

            def probabilities(j):
                kind, t, pair = j // 4, j // 2 % 2, j % 2
                eng.wait_ge(s["logits_ready"], j + 1)
                for i in range(2):
                    h = pair + 2 * i
                    nc.scalar.activation(S[:, j % 3, i, :], S[:, j % 3, i, :], ACT.Exp,
                                         bias=neg_max[:, t, kind, h:h + 1],
                                         accum_out=den[:, t, kind, h:h + 1]).then_inc(s["probs_ready"], 1)

            for j in range(18):
                if j < 16:
                    if j in PIECES:
                        gate_piece(PIECES[j])
                    probabilities(j)
                if 1 <= j <= 16:
                    copy_out(("PT", j - 1), PT[:, (j - 1) % 3, :, :])
            for t in range(NT):
                eng.wait_ge(s["peaks_ready"], t + 1)
                nc.scalar.activation(combine[:, t, :, :], combine[:, t, :, :], ACT.Exp).then_inc(s["peaks_exp"], 1)
            t = wait_filled(eng, "o_dilT")
            for tt in range(NT):
                last = nc.scalar.copy(oT[:, 0:2, tt * P:(tt + 1) * P],
                                      t[:, tt * 256:(tt + 1) * 256].rearrange("p (k c) -> p k c", k=2))
            last.then_inc(drain_of("o_dilT"), 1)
            for t in range(NT):
                copy_out(("o_memT", t), oT[:, 2:6, t * P:(t + 1) * P])
            for t in range(NT):
                for half in range(2):
                    copy_out(("mergedT", t, half), mergedT[:, 4 * half:4 * half + 4, t * P:(t + 1) * P])
            wait_drained(eng, "cols")
            nc.scalar.activation(r_col[:, 0:8, 0], cols[:, P + 120:P + 128], ACT.Silu).then_inc(s["c_silu"], 1)
            nc.scalar.activation(r_col[:, 0:8, 1], cols[:, 114:122], ACT.Silu).then_inc(s["c_silu"], 1)
            root(stats[:, 4:6])
            for t in range(NT):
                for half in range(2):
                    copy_out(("h2T", t, half), h2T[:, 4 * half:4 * half + 4, t * P:(t + 1) * P])
            eng.wait_ge(s["gate_logits"], 1)
            nc.scalar.activation(r_tmp[:, 0, :, 0:4], r_tmp[:, 0, :, 0:4], ACT.Exp).then_inc(s["gate_exp"], 1)
            eng.wait_ge(s["gate_logits"], 2)
            nc.scalar.activation(r_col[:, 6, :], r_col[:, 6, :], ACT.Exp).then_inc(s["gate_exp"], 1)
            for t in range(NT):
                copy_out(("placeT", t), placeT[:, :, t * P:(t + 1) * P])
            experts_act(eng, FIRST_PASS)
            where_overflow(eng, lambda: second_pass_act(eng))
            second_block_act(eng, root, copy_out)

        @block.vector
        def _(eng):
            steps, roots = [0], [0]
            v = nc.vector

            def step(ins):
                steps[0] += 1
                ins.then_inc(s["dve_step"], 1)

            def link(ins):
                step(ins)
                eng.wait_ge(s["dve_step"], steps[0])

            def root_ask(ss, n, eps=EPS):
                roots[0] += 1
                v.tensor_scalar(ss, ss, 1.0 / n, eps, ALU.mult, ALU.add).then_inc(s["root_asked"], 1)

            def root_take(ss, signal=None):
                eng.wait_ge(s["root_done"], roots[0])
                ins = v.reciprocal(ss, ss)
                if signal:
                    ins.then_inc(s[signal], 1)
                else:
                    link(ins)

            def root_mean(ss, n, eps=EPS):
                root_ask(ss, n, eps)
                root_take(ss)

            def square_sums(src, junk, ss):
                link(v.tensor_tensor_reduce(junk, src, src, 1.0, 0.0, ALU.mult, ALU.add, ss))

            def spread(ap, *shape):
                return ap.unsqueeze(len(ap.shape)).to_broadcast([P, *shape])

            eng.wait_ge(s["x_in"], 16)
            for t in range(NT):
                square_sums(x[:, t, :], xn[:, t, :], stats[:, t:t + 1])
            root_mean(stats[:, 0:2], D)
            for t in range(NT):
                v.tensor_scalar(xn[:, t, :], x[:, t, :], stats[:, t:t + 1], None, ALU.mult).then_inc(s["xn_ready"], 1)
            t = wait_filled(eng, "cols")
            step(v.tensor_copy(cols[:, 0:ROWS_A], t[:, 0:ROWS_A]))
            v.tensor_copy(cols[:, P:2 * P], t[:, P:2 * P]).then_inc(drain_of("cols"), 1)
            wait_drained(eng, "cols")

            def columns_out(key, dst, gain):
                t = wait_filled(eng, key)
                v.tensor_tensor(dst, t.rearrange("p (k c) -> p k c", k=4), spread(gain, 4, P), ALU.mult)\
                 .then_inc(drain_of(key), 1)

            for t in range(NT):
                for half in range(2):
                    columns_out(("hT", t, half), hT[:, 4 * half:4 * half + 4, t * P:(t + 1) * P],
                                cols[:, 4 * half:4 * half + 4])
            eng.wait_ge(s["mem_in"], 16)
            for t in range(NT):
                square_sums(mem[:, t, :], merged[:, t, :], stats[:, 2 + t:3 + t])
            root_mean(stats[:, 2:4], D)
            for t in range(NT):
                v.tensor_scalar(mem[:, t, :], mem[:, t, :], stats[:, 2 + t:3 + t], None, ALU.mult).then_inc(s["mn_ready"], 1)
            for t in range(NT):
                for half in range(2):
                    columns_out(("mT", t, half), mT[:, 4 * half:4 * half + 4, t * P:(t + 1) * P],
                                cols[:, 8 + 4 * half:12 + 4 * half])

            eng.wait_ge(s["small_in"], 16 * N_SMALL)
            eng.wait_ge(s["consts_ready"], 1)
            angle, turns, reduced = rope[:, 0, :, :, :], rope[:, 1, :, :, :], rope[:, 2, :, :, :]
            link(v.tensor_copy(rope[:, 3, 0, :, 0], pos_i[:, :]))
            for i in range(2):
                step(v.tensor_tensor(angle[:, i, :, :], spread(rope[:, 3, 0, :, 0], NT, ROT),
                                     inv_freq[:, :].unsqueeze(1).to_broadcast([P, NT, ROT]), ALU.mult))
            eng.wait_ge(s["dve_step"], steps[0])
            step(v.tensor_scalar(turns[:, 0, :, :], angle[:, 0, :, :], 1.0 / (2 * np.pi), 0.25, ALU.mult, ALU.add))
            link(v.tensor_scalar(turns[:, 1, :, :], angle[:, 1, :, :], 1.0 / (2 * np.pi), None, ALU.mult))
            link(v.tensor_scalar(turns, turns, ROUND, None, ALU.add))
            link(v.tensor_scalar(turns, turns, ROUND, None, ALU.subtract))
            link(v.scalar_tensor_tensor(reduced, turns, -TURN[0], angle, ALU.mult, ALU.add))
            link(v.scalar_tensor_tensor(reduced, turns, -TURN[1], reduced, ALU.mult, ALU.add))
            link(v.scalar_tensor_tensor(reduced, turns, -TURN[2], reduced, ALU.mult, ALU.add))
            link(v.tensor_scalar(reduced[:, 0, :, :], reduced[:, 0, :, :], np.pi / 2, None, ALU.add))
            v.tensor_scalar(rope[:, 6, :, :, :], reduced, 3.1415925, -3.1415925, ALU.min, ALU.max).then_inc(s["angles_ready"], 1)
            cos, sin = rope[:, 7, 0, :, :], rope[:, 7, 1, :, :]
            for i, dil in ((2, 4), (3, 16)):
                link(v.tensor_scalar(mask_i, distance, dil - 1, None, ALU.bitwise_and))
                link(v.tensor_scalar(mask[:, i, :], mask_i, 0.0, FAR, ALU.not_equal, ALU.mult))

            eng.wait_ge(s["tables_ready"], 1)
            for t in range(NT):
                for i in range(3):
                    wait_drained(eng, ("in", i, t))
                if t:
                    eng.wait_ge(s["qk_ready"], t)
                heads, ss = qk[:, t, :, :], head_root[:, t, 0:24]
                link(v.tensor_tensor(squares, heads, heads, ALU.mult))
                link(v.tensor_reduce(ss, squares, AX.X, ALU.add))
                root_mean(ss, DH)
                link(v.tensor_tensor(heads, heads, spread(ss, 24, DH), ALU.mult))
                for i in range(2):
                    step(v.tensor_tensor(heads[:, 12 * i:12 * i + 12, :], heads[:, 12 * i:12 * i + 12, :],
                                         head_gain[:, i, :].unsqueeze(1).to_broadcast([P, 12, DH]), ALU.mult))
                eng.wait_ge(s["dve_step"], steps[0])
                x1, x2 = heads[:, :, 0:ROT], heads[:, :, ROT:2 * ROT]
                tmp = squares[:, :, 0:4 * ROT].rearrange("p h (f r) -> p f h r", f=4)
                c = cos[:, t, :].unsqueeze(1).to_broadcast([P, 24, ROT])
                sn = sin[:, t, :].unsqueeze(1).to_broadcast([P, 24, ROT])
                for f, (one, two) in enumerate(((x1, c), (x2, sn), (x2, c), (x1, sn))):
                    step(v.tensor_tensor(tmp[:, f, :, :], one, two, ALU.mult))
                eng.wait_ge(s["dve_step"], steps[0])
                step(v.tensor_tensor(x1, tmp[:, 0, :, :], tmp[:, 1, :, :], ALU.subtract))
                eng.wait_ge(s["dve_step"], steps[0])
                v.tensor_tensor(x2, tmp[:, 2, :, :], tmp[:, 3, :, :], ALU.add).then_inc(s["qk_ready"], 1)
            for t in range(NT):
                wait_drained(eng, ("in", 9, t))
                wait_drained(eng, ("mk", 0, t))
                eng.wait_ge(s["qk_ready"], NT + t)
                heads, ss = qk_mem[:, t, :, :], head_root[:, t, 0:8]
                sq = squares.rearrange("p h d -> p (h d)")[:, 0:1024].rearrange("p (h d) -> p h d", h=8)
                link(v.tensor_tensor(sq, heads, heads, ALU.mult))
                link(v.tensor_reduce(ss, sq, AX.X, ALU.add))
                root_mean(ss, MEM_DH)
                link(v.tensor_tensor(heads, heads, spread(ss, 8, MEM_DH), ALU.mult))
                step(v.tensor_tensor(heads[:, 0:4, :], heads[:, 0:4, :],
                                     mem_gain[:, 0, :].unsqueeze(1).to_broadcast([P, 4, MEM_DH]), ALU.mult))
                eng.wait_ge(s["dve_step"], steps[0])
                v.tensor_tensor(heads[:, 4:8, :], heads[:, 4:8, :],
                                mem_gain[:, 1, :].unsqueeze(1).to_broadcast([P, 4, MEM_DH]), ALU.mult).then_inc(s["qk_ready"], 1)

            def logits(j):
                kind, t, pair = j // 4, j // 2 % 2, j % 2
                buf, key = S[:, j % 3, :, :], ("scores", j)
                if j >= 3:
                    wait_filled(eng, ("PT", j - 3))
                src = wait_filled(eng, key).rearrange("p (h k) -> p h k", h=2)
                if kind < 3:
                    rows = mask[:, t if kind == 0 else kind + 1, :]
                    v.scalar_tensor_tensor(buf, src, DH ** -0.5, rows.unsqueeze(1).to_broadcast([P, 2, SEQ]),
                                           ALU.mult, ALU.add).then_inc(drain_of(key), 1)
                else:
                    v.tensor_scalar(buf, src, MEM_DH ** -0.5, None, ALU.mult).then_inc(drain_of(key), 1)
                wait_drained(eng, key)
                v.tensor_reduce(neg_max[:, t, kind, pair:pair + 3:2], buf, AX.X, ALU.max, negate=True)\
                 .then_inc(s["logits_ready"], 1)

            def outputs(j):
                kind, t, pair = j // 4, j // 2 % 2, j % 2
                key = ("values", j)
                if kind < 3:
                    src = wait_filled(eng, key)[:, 0:2 * DH].rearrange("p (h d) -> p h d", h=2)
                    dst = o_dil[:, t, kind, :].rearrange("p (h d) -> p h d", h=4)[:, pair:pair + 3:2, :]
                    v.tensor_copy(dst, src).then_inc(drain_of(key), 1)
                else:
                    eng.wait_ge(s["probs_ready"], 2 * (j + 1))
                    rden = combine[:, 2 + t, 0, 2 * pair:2 * pair + 2]
                    link(v.reciprocal(rden, den[:, t, 3, pair:pair + 3:2]))
                    src = wait_filled(eng, key)[:, 0:256].rearrange("p (h d) -> p h d", h=2)
                    v.tensor_tensor(o_mem[:, t, :].rearrange("p (h d) -> p h d", h=4)[:, pair:pair + 3:2, :], src,
                                    spread(rden, 2, MEM_DH), ALU.mult).then_inc(drain_of(key), 1)

            def convolve(i):
                key = ("cv", i)
                src = wait_filled(eng, key)
                c0 = 2 * (i - 6)
                for k in range(3):
                    wait_drained(eng, ("cv", k))
                    wait_drained(eng, ("cv", 3 + k))
                u = u_conv[:, c0:c0 + 2, 1:SEQ + 1]
                v.tensor_tensor(u, src.rearrange("p (c t) -> p c t", c=2), u, ALU.mult).then_inc(drain_of(key), 1)
                wait_drained(eng, key)
                for c in range(2):
                    ch, dst = c0 + c, tap[:, c, :]
                    w = [cols[:, 24 + 6 * k + ch:25 + 6 * k + ch] for k in range(3)]
                    link(v.tensor_scalar(dst, u_conv[:, ch, 0:SEQ], w[0], None, ALU.mult))
                    link(v.scalar_tensor_tensor(dst, u_conv[:, ch, 1:SEQ + 1], w[1], dst, ALU.mult, ALU.add))
                    link(v.scalar_tensor_tensor(dst, u_conv[:, ch, 2:SEQ + 2], w[2], dst, ALU.mult, ALU.add))
                    v.tensor_tensor(cb[:, ch, :], cb[:, ch, :], dst, ALU.mult).then_inc(s["z_ready"], 1)

            eng.wait_ge(s["zeros_ready"], 1)
            for i in (6, 7, 8):
                convolve(i)
            for j in range(18):
                if j < 16:
                    logits(j)
                if j >= 2:
                    outputs(j - 2)

            for t in range(NT):
                m, e = neg_max[:, t, 0:3, :], combine[:, t, :, :]
                low = combine[:, 2 + t, 1, :]
                link(v.tensor_reduce(low, m.rearrange("p g h -> p h g"), AX.X, ALU.min))
                eng.wait_ge(s["dve_step"], steps[0])
                v.tensor_tensor(e, low.unsqueeze(1).to_broadcast([P, 3, 4]), m, ALU.subtract).then_inc(s["peaks_ready"], 1)
                eng.wait_ge(s["peaks_exp"], t + 1)
                total = combine[:, 2 + t, 2, :]
                weighed = mix[:, 0:12].rearrange("p (g h) -> p g h", g=3)
                link(v.tensor_tensor(weighed, e, den[:, t, 0:3, :], ALU.mult))
                link(v.tensor_reduce(total, weighed.rearrange("p g h -> p h g"), AX.X, ALU.add))
                link(v.reciprocal(total, total))
                link(v.tensor_tensor(e, e, total.unsqueeze(1).to_broadcast([P, 3, 4]), ALU.mult))
                o = o_dil[:, t, :, :].rearrange("p g (h d) -> p g h d", h=4)
                for g in range(3):
                    step(v.tensor_tensor(o[:, g, :, :], o[:, g, :, :], spread(e[:, g, :], 4, DH), ALU.mult))
                eng.wait_ge(s["dve_step"], steps[0])
                link(v.tensor_tensor(o_dil[:, t, 0, :], o_dil[:, t, 0, :], o_dil[:, t, 1, :], ALU.add))
                v.tensor_tensor(o_dil[:, t, 0, :], o_dil[:, t, 0, :], o_dil[:, t, 2, :], ALU.add).then_inc(s["o_ready"], 1)
                eng.wait_ge(s["o_ready"], t + 1)

            for branch in (1, 0, 2):
                for t in range(NT):
                    for half in range(2):
                        key = ("proj", branch, t, half)
                        c = branch * D + half * WIDE
                        wait_drained(eng, ("gate", c // WIDE, t))
                        src, gate = wait_filled(eng, key), gates[:, t, c:c + WIDE]
                        dst = merged[:, t, half * WIDE:(half + 1) * WIDE]
                        if branch == 1:
                            v.tensor_tensor(dst, src, gate, ALU.mult).then_inc(drain_of(key), 1)
                        else:
                            v.tensor_tensor(gate, src, gate, ALU.mult).then_inc(drain_of(key), 1)
                            wait_drained(eng, key)
                            wait_drained(eng, ("proj", 1, t, half))
                            if branch == 2:
                                eng.wait_ge(s["dve_step"], steps[0])
                                v.tensor_tensor(dst, dst, gate, ALU.add).then_inc(s["merged_ready"], 1)
                            else:
                                step(v.tensor_tensor(dst, dst, gate, ALU.add))
            for i in range(2):
                for t in range(NT):
                    key = ("wo", i, t)
                    part = x[:, t, i * WIDE:(i + 1) * WIDE]
                    v.tensor_tensor(part, wait_filled(eng, key), part, ALU.add).then_inc(drain_of(key), 1)

            eng.wait_ge(s["c_silu"], 2)
            for i, c in enumerate((c_wide, c_ctx_wide)):
                v.tensor_copy(c, spread(r_col[:, 0:8, i], 8, P)).then_inc(s["c_wide_ready"], 1)

            def modulation(i, which, dst, plus_one):
                key = ("ad", i, which)
                src = wait_filled(eng, key)
                v.scalar_tensor_tensor(dst, src, 1.0 if plus_one else 0.0, dst, ALU.add, ALU.add).then_inc(drain_of(key), 1)

            for i in range(2):
                for t in range(NT):
                    wait_drained(eng, ("wo", i, t))
            for t in range(NT):
                square_sums(x[:, t, :], h2[:, t, :], stats[:, 4 + t:5 + t])
            root_mean(stats[:, 4:6], D)
            eng.wait_ge(s["wide_in"], 16)
            for t in range(NT):
                v.scalar_tensor_tensor(h2[:, t, :], x[:, t, :], stats[:, 4 + t:5 + t], ffn_gain, ALU.mult, ALU.mult)\
                 .then_inc(s["h2_ready"], 1)
            eng.wait_ge(s["mod_in"], 32)

            def mixer_rows(i):
                for which, dst in enumerate((mod_a, mod_c)):
                    modulation(i, which, dst[:, i // 2, (i % 2) * WIDE:(i % 2 + 1) * WIDE], i >= 2)

            mixer_rows(0)
            src = wait_filled(eng, "router")
            v.tensor_tensor(r_log, src[:, 0:72].rearrange("p (t c) -> p t c", t=NT),
                            router_b[:, :].unsqueeze(1).to_broadcast([P, NT, 36]), ALU.add).then_inc(drain_of("router"), 1)
            wait_drained(eng, "router")
            groups, peak = r_log[:, :, 0:4], r_col[:, 0, :]
            link(v.tensor_reduce(peak, groups, AX.X, ALU.max))
            v.tensor_tensor(r_tmp[:, 0, :, 0:4], groups, spread(peak, NT, 4), ALU.subtract).then_inc(s["gate_logits"], 1)

            def first_of(values, top, out, n, signal=None):
                prio = r_prio[:, 8 - n:8].unsqueeze(1).to_broadcast([P, NT, n])
                link(v.tensor_tensor(out, values, spread(top, NT, n), ALU.is_equal))
                link(v.tensor_tensor(out, out, prio, ALU.mult))
                link(v.tensor_reduce(r_col[:, 1, :], out, AX.X, ALU.max))
                ins = v.tensor_tensor(out, out, spread(r_col[:, 1, :], NT, n), ALU.is_equal)
                if signal:
                    ins.then_inc(s[signal], 1)
                else:
                    link(ins)

            first_of(groups, peak, r_hot, 4, "hot_ready")
            eng.wait_ge(s["hot_ready"], 1)
            mixer_rows(1)
            eng.wait_ge(s["gate_exp"], 1)
            link(v.tensor_reduce(r_col[:, 2, :], r_tmp[:, 0, :, 0:4], AX.X, ALU.add))
            link(v.reciprocal(r_col[:, 2, :], r_col[:, 2, :]))
            for t in range(NT):
                step(v.tensor_tensor(r_big[:, t, :, :], r_log[:, t, 4:36].rearrange("p (g e) -> p g e", g=GROUPS),
                                     spread(r_hot[:, t, :], GROUPS, 8), ALU.mult))
            eng.wait_ge(s["dve_step"], steps[0])
            sel, hot1, hot2 = r_tmp[:, 2, :, :], r_tmp[:, 3, :, :], r_tmp[:, 4, :, :]
            link(v.tensor_reduce(sel, r_big.rearrange("p t g e -> p t e g"), AX.X, ALU.add))
            link(v.tensor_reduce(r_col[:, 3, :], sel, AX.X, ALU.max))
            first_of(sel, r_col[:, 3, :], hot1, 8)
            link(v.scalar_tensor_tensor(sel, hot1, FAR, sel, ALU.mult, ALU.add))
            link(v.tensor_reduce(r_col[:, 4, :], sel, AX.X, ALU.max))
            first_of(sel, r_col[:, 4, :], hot2, 8)
            v.tensor_tensor(r_col[:, 6, :], r_col[:, 4, :], r_col[:, 3, :], ALU.subtract).then_inc(s["gate_logits"], 1)
            eng.wait_ge(s["gate_exp"], 2)
            link(v.tensor_scalar(r_col[:, 7, :], r_col[:, 6, :], 1.0, None, ALU.add))
            link(v.reciprocal(r_col[:, 7, :], r_col[:, 7, :]))
            link(v.tensor_tensor(r_col[:, 7, :], r_col[:, 7, :], r_col[:, 2, :], ALU.mult))
            link(v.tensor_tensor(r_col[:, 6, :], r_col[:, 6, :], r_col[:, 7, :], ALU.mult))
            step(v.tensor_tensor(hot1, hot1, spread(r_col[:, 7, :], NT, 8), ALU.mult))
            link(v.tensor_tensor(hot2, hot2, spread(r_col[:, 6, :], NT, 8), ALU.mult))
            link(v.tensor_tensor(r_we, hot1, hot2, ALU.add))
            src = wait_filled(eng, "rank")
            v.tensor_copy(r_rank, src[:, 0:12]).then_inc(drain_of("rank"), 1)
            wait_drained(eng, "rank")
            link(v.tensor_reduce(r_col[:, 8, 0:1], r_rank[:, 8:12], AX.X, ALU.max))
            v.tensor_scalar(overflow[:, :], r_col[:, 8, 0:1], float(P), None, ALU.is_gt).then_inc(s["flag_ready"], 1)
            for t in range(NT):
                for g in range(GROUPS):
                    v.tensor_scalar(place[:, t, g, :], slot_row, r_rank[:, 4 * t + g:4 * t + g + 1],
                                    r_hot[:, t, g:g + 1], ALU.is_equal, ALU.mult).then_inc(s["place_ready"], 1)
            mixer_rows(2)
            mixer_rows(3)
            src = wait_filled(eng, "w_slot")
            v.tensor_copy(w_slot.rearrange("p g e -> p (g e)"), src[:, 0:32]).then_inc(drain_of("w_slot"), 1)
            wait_drained(eng, "w_slot")
            for t in range(NT):
                wait_drained(eng, ("placeT", t))
            experts_dve(eng, FIRST_PASS)
            where_overflow(eng, lambda: second_pass_dve(eng))
            for m in LAST_TILES:
                FIRST_PASS.wait_drained(eng, GROUPS - 1, m)
            second_block_dve(eng, step, link, root_mean, root_ask, root_take, square_sums, spread)

        @block.gpsimd
        def _(eng):
            g, steps = nc.gpsimd, [0]

            def link(ins):
                steps[0] += 1
                ins.then_inc(s["pool_step"], 1)
                eng.wait_ge(s["pool_step"], steps[0])

            def keep_where(dst, pattern, base, channel, op, fill):
                link(g.affine_select(out=dst, in_=dst, pattern=pattern, compare_op=op, fill=fill, base=base,
                                     channel_multiplier=channel))

            link(g.memset(ident, 0.0))
            g.affine_select(out=ident, in_=ident, pattern=[[-1, P]], compare_op=ALU.not_equal, fill=1.0, base=0,
                            channel_multiplier=1).then_inc(s["ident_ready"], 1)
            link(g.memset(const[:, 1:10, :], 1.0))
            keep_where(upto, [[1, P]], 0, -1, ALU.is_ge, 0.0)
            keep_where(since, [[-1, P]], 0, 1, ALU.is_ge, 0.0)
            keep_where(below, [[-1, P]], 0, 1, ALU.is_gt, 0.0)
            keep_where(above, [[1, P]], 0, -1, ALU.is_gt, 0.0)
            for m, n in ((blk16, 16), (lev32, 32), (lev64, 64)):
                wide = m.rearrange("p (b c) -> p b c", c=n)
                keep_where(wide, [[-n, P // n], [0, n]], 0, 1, ALU.is_ge, 0.0)
                keep_where(wide, [[n, P // n], [0, n]], n - 1, -1, ALU.is_ge, 0.0)
            link(g.tensor_tensor(lev128, lev128, lev64, ALU.subtract))
            link(g.tensor_tensor(lev64, lev64, lev32, ALU.subtract))
            link(g.tensor_tensor(lev32, lev32, blk16, ALU.subtract))
            link(g.iota(slot_row, [[1, P]], base=0, channel_multiplier=0, allow_small_or_imprecise_dtypes=True))
            link(g.iota(r_prio[:, :], [[-1, 8]], base=8, channel_multiplier=0, allow_small_or_imprecise_dtypes=True))
            link(g.iota(distance, [[-1, SEQ]], base=SEQ, channel_multiplier=1))
            for i in range(ROT):
                link(g.memset(inv_freq[:, i:i + 1], float(np.float32(THETA) ** np.float32(-i / ROT))))
            link(g.memset(mask[:, 0:2, :], 0.0))
            for t in range(NT):
                keep_where(mask[:, t, :], [[-1, SEQ]], t * P + BAND, 1, ALU.is_ge, FAR)
                keep_where(mask[:, t, :], [[1, SEQ]], BAND - t * P, -1, ALU.is_ge, FAR)
            g.memset(u_conv[:, :, 0:1], 0.0).then_inc(s["consts_ready"], 1)
            g.memset(u_conv[:, :, SEQ + 1:SEQ + 2], 0.0).then_inc(s["zeros_ready"], 1)
            eng.wait_ge(s["o_ready"], NT)
            eng.wait_ge(s["z_ready"], CONV_TILES)
            eng.dma_start(ffn_gain, a["g_ffn"][0].partition_broadcast(P)).then_inc(s["wide_in"], 16)
            wait_filled(eng, ("wo", 1, 1))
            bias = a["b_ada_2"][0]
            eng.dma_start(mod_a.rearrange("p i d -> p (i d)"), bias[0:2 * D].partition_broadcast(P)).then_inc(s["mod_in"], 16)
            eng.dma_start(mod_c.rearrange("p i d -> p (i d)"), bias[0:2 * D].partition_broadcast(P)).then_inc(s["mod_in"], 16)
            eng.dma_start(ctx_in, a["ctx_2"][0].rearrange("(t p) d -> p t d", p=P)).then_inc(s["ctx_in"], 16)
            second_block_pool(eng, g, link)

        @block.sync
        def _(sp):
            def load(name):
                n = unit_number[name]
                for dst, (src, tiles) in zip(unit_views(name, n % SLOTS), unit_source(name)):
                    sp.dma_start(dst, src.rearrange("(k p) n -> p k n", p=P)).then_inc(landed[n % SLOTS], 16)

            for table, which in ((COLS_A, 0), (COLS_B, 1)):
                for name, (first, count) in table.items():
                    src = a[name]
                    flat = {1: "(a p) -> a p", 2: "x (a p) -> (x a) p", 3: "x y (a p) -> (x y a) p"}[len(src.shape)]
                    sp.dma_start(rows_a[first:first + count, which, :], src.rearrange(flat, p=P)).then_inc(s["rows_in"], 16)
            sp.wait_ge(s["x_in"], 16)
            for n, name in enumerate(before_experts):
                if n == 2:
                    sp.dma_start(mem, a["mem"][0].rearrange("(t p) d -> p t d", p=P)).then_inc(s["mem_in"], 16)
                if n >= SLOTS:
                    sp.wait_ge(filled, unit_use[before_experts[n - SLOTS]])
                load(name)
            first_loads(sp, FIRST_PASS, lambda q: sp.wait_ge(filled, unit_use[before_experts[FIRST_UNIT - SLOTS + q]]))
            experts_sp(sp, FIRST_PASS)
            where_overflow(sp, lambda: second_pass_sp(sp))
            second_block_sp(sp, load)


INPUTS = ("x mem positions g_mix g_mem w_in g_qn_attn g_kn_attn w_conv w_mem_kv g_qn_mem g_kn_mem w_proj_attn w_proj_conv "
          "w_proj_mem w_out g_ffn w_router_group b_router_group w_router_expert b_router_expert w_gate w_up w_down c_2 ctx_2 "
          "c_ctx_2 w_ada_2 b_ada_2 w_in_2 conv_w_ssd_2 conv_b_ssd_2 dt_bias_ssd_2 a_log_ssd_2 d_skip_ssd_2 norm_w_ssd_2 "
          "conv_w_gdn_2 dt_bias_gdn_2 a_log_gdn_2 norm_w_gdn_2 w_out_2 ln1_g_2 ln1_b_2 w_ffn_gate_2 w_ffn_up_2 w_ffn_down_2 "
          "ln2_g_2 ln2_b_2").split()


def kernel(**inputs):
    import numpy as _np
    import concourse.bacc as _bacc
    from concourse import mybir as _mybir
    from concourse.bass_utils import run_bass_kernel_spmd as _run

    nc = _bacc.Bacc("TRN2", target_bir_lowering=False, num_devices=1)
    arrays, args = {}, {}
    for name in INPUTS:
        value = _np.ascontiguousarray(inputs[name])
        arrays[f"in_{name}"] = value
        args[name] = nc.dram_tensor(f"in_{name}", value.shape, _mybir.dt.from_np(value.dtype), kind="ExternalInput").ap()
    out = nc.dram_tensor("out_0", (1, SEQ, D), F32, kind="ExternalOutput").ap()
    two_block_kernel(nc, args, out)
    r = _run(nc, [arrays], core_ids=[0])
    return r.results[0]["out_0"]
```
